# Optimizing a Trainium2 kernel written in Bass

```python
import math
import jax, jax.numpy as jnp
from jax import lax
import numpy as np

D_MODEL = 1024
BATCH = 1
SEQ = 256
DEPTH = 2
DEC_BATCH = 8
DEC_SEQ = 1
PAST_LEN = 2048
PAGE_SIZE = 128

D_CONV = D_MODEL // 2
DW_WIDTH = 31
N_HEADS = 4
HEAD_K = 128
HEAD_V = 128
QK_CONV = 4
CHUNK = 64
D_DELTA_K = N_HEADS * HEAD_K
D_DELTA_V = N_HEADS * HEAD_V
CONV_DIM = 2 * D_DELTA_K + D_DELTA_V
D_FF = ((8 * D_MODEL // 3 + 127) // 128) * 128
N_EXPERTS = 8
TOP_K = 2
D_FF_EXPERT = D_FF
N_DENSE = (DEPTH + 1) // 2
N_MOE = DEPTH // 2
EPS = 1e-6

OFF_GLU = 0
OFF_QKV = OFF_GLU + 2 * D_CONV
OFF_Z = OFF_QKV + CONV_DIM
OFF_A = OFF_Z + D_DELTA_V
OFF_B = OFF_A + N_HEADS
OFF_GATE_A = OFF_B + N_HEADS
OFF_GATE_B = OFF_GATE_A + D_MODEL
N_IN = OFF_GATE_B + D_MODEL

kernel_name = 'conformer_gated_deltanet_hybrid_step'

def _rmsnorm(x, g):
    xf = x.astype(jnp.float32)
    y = xf * lax.rsqrt(jnp.mean(xf * xf, axis=-1, keepdims=True) + EPS)
    return (y * g.astype(jnp.float32)).astype(x.dtype)

def _l2norm(t):
    return t * lax.rsqrt(jnp.sum(t * t, axis=-1, keepdims=True) + EPS)

def _causal_depthwise_conv(x, buf, w):
    xp = jnp.concatenate([buf.astype(x.dtype), x], axis=1)
    y = lax.conv_general_dilated(
        xp, w[:, None, :].astype(x.dtype), window_strides=(1,), padding='VALID',
        dimension_numbers=('NWC', 'WIO', 'NWC'), feature_group_count=x.shape[-1])
    new_buf = xp[:, xp.shape[1] - (w.shape[0] - 1):]
    return y, new_buf

def _gated_delta_rule(q, k, v, beta, g, S0):
    Bn, T, H, _ = q.shape
    C = min(CHUNK, T)
    pad = (-T) % C
    n = (T + pad) // C

    def blocks(t):
        t = jnp.pad(t, [(0, 0), (0, pad)] + [(0, 0)] * (t.ndim - 2))
        t = t.reshape((Bn, n, C) + t.shape[2:])
        return jnp.moveaxis(t, 3, 1)

    q, k, v, beta, g = blocks(q), blocks(k), blocks(v), blocks(beta), blocks(g)
    gc = jnp.cumsum(g, axis=-1)
    idx = jnp.arange(C)
    tril = idx[:, None] >= idx[None, :]
    strict = idx[:, None] > idx[None, :]
    diff = gc[..., :, None] - gc[..., None, :]
    L = jnp.where(tril, jnp.exp(jnp.where(tril, diff, 0.0)), 0.0)
    kb = k * beta[..., None]
    M = jnp.where(strict, jnp.einsum('bhnid,bhnjd->bhnij', kb, k) * L, 0.0)
    eye = jnp.eye(C, dtype=jnp.float32)
    Tm = lax.linalg.triangular_solve(eye + M, jnp.broadcast_to(eye, M.shape),
                                     left_side=True, lower=True, unit_diagonal=True)
    u = jnp.einsum('bhnij,bhnjv->bhniv', Tm, v * beta[..., None])
    w = jnp.einsum('bhnij,bhnjk->bhnik', Tm, kb * jnp.exp(gc)[..., None])
    a_intra = jnp.einsum('bhnik,bhnjk->bhnij', q, k) * L
    qg = q * jnp.exp(gc)[..., None]
    g_last = gc[..., -1]
    kd = k * jnp.exp(g_last[..., None] - gc)[..., None]
    dl = jnp.exp(g_last)
    xs = (jnp.moveaxis(u, 2, 0), jnp.moveaxis(w, 2, 0), jnp.moveaxis(a_intra, 2, 0),
          jnp.moveaxis(qg, 2, 0), jnp.moveaxis(kd, 2, 0), jnp.moveaxis(dl, 2, 0))

    def step(S, inp):
        u_c, w_c, a_c, qg_c, kd_c, dl_c = inp
        v_new = u_c - jnp.einsum('bhik,bhkv->bhiv', w_c, S)
        o = jnp.einsum('bhik,bhkv->bhiv', qg_c, S) + jnp.einsum('bhij,bhjv->bhiv', a_c, v_new)
        S = S * dl_c[..., None, None] + jnp.einsum('bhik,bhiv->bhkv', kd_c, v_new)
        return S, o

    S, o = lax.scan(step, S0, xs)
    o = jnp.transpose(o, (1, 0, 3, 2, 4)).reshape(Bn, n * C, H, o.shape[-1])[:, :T]
    return o, S

def _conformer_conv(glu, buf, dw_w, dw_b, ln_g, ln_b, w_out):
    u = glu[..., :D_CONV] * jax.nn.sigmoid(glu[..., D_CONV:])
    c, new_buf = _causal_depthwise_conv(u, buf, dw_w)
    c = (c + dw_b).astype(jnp.float32)
    mu = jnp.mean(c, axis=-1, keepdims=True)
    var = jnp.mean(jnp.square(c - mu), axis=-1, keepdims=True)
    c = (c - mu) * lax.rsqrt(var + EPS) * ln_g.astype(jnp.float32) + ln_b.astype(jnp.float32)
    c = jax.nn.silu(c).astype(glu.dtype)
    return c @ w_out, new_buf

def _gated_deltanet(qkv, z, a, b, conv_buf, S0, conv_w, a_log, dt_bias, o_norm_g, w_out):
    Bn, T, _ = qkv.shape
    f32 = jnp.float32
    c, new_buf = _causal_depthwise_conv(qkv, conv_buf, conv_w)
    c = jax.nn.silu(c.astype(f32))
    q = c[..., :D_DELTA_K].reshape(Bn, T, N_HEADS, HEAD_K)
    k = c[..., D_DELTA_K:2 * D_DELTA_K].reshape(Bn, T, N_HEADS, HEAD_K)
    v = c[..., 2 * D_DELTA_K:].reshape(Bn, T, N_HEADS, HEAD_V)
    q = _l2norm(q) * (HEAD_K ** -0.5)
    k = _l2norm(k)
    beta = jax.nn.sigmoid(b.astype(f32))
    g = -jnp.exp(a_log.astype(f32)) * jax.nn.softplus(a.astype(f32) + dt_bias.astype(f32))
    o, S = _gated_delta_rule(q, k, v, beta, g, S0.astype(f32))
    o = o * lax.rsqrt(jnp.mean(o * o, axis=-1, keepdims=True) + EPS) * o_norm_g.astype(f32)
    o = o * jax.nn.silu(z.astype(f32).reshape(Bn, T, N_HEADS, HEAD_V))
    y = o.reshape(Bn, T, D_DELTA_V).astype(qkv.dtype) @ w_out
    return y, new_buf, S.astype(S0.dtype)

def _swiglu(h, wg, wu, wd):
    return (jax.nn.silu(h @ wg) * (h @ wu)) @ wd

def _moe(h, router, wg, wu, wd):
    logits = jnp.einsum('btd,de->bte', h.astype(jnp.float32), router.astype(jnp.float32))
    top_v, top_i = lax.top_k(logits, TOP_K)
    probs = jax.nn.softmax(top_v, axis=-1)
    gates = jnp.sum(jax.nn.one_hot(top_i, N_EXPERTS, dtype=jnp.float32) * probs[..., None], axis=-2)
    y = jnp.zeros_like(h)
    for e in range(N_EXPERTS):
        y = y + gates[..., e:e + 1].astype(h.dtype) * _swiglu(h, wg[e], wu[e], wd[e])
    return y

def _trunk(x, S0, qkv0, dw0, P):
    news_S, news_q, news_d = [], [], []
    for l in range(DEPTH):
        h = _rmsnorm(x, P['norm1_g'][l])
        p = h @ P['w_in'][l]
        yA, dbuf = _conformer_conv(p[..., OFF_GLU:OFF_QKV], dw0[l], P['dw_w'][l], P['dw_b'][l],
                                   P['ln_g'][l], P['ln_b'][l], P['w_conv_out'][l])
        yB, qbuf, S = _gated_deltanet(p[..., OFF_QKV:OFF_Z], p[..., OFF_Z:OFF_A], p[..., OFF_A:OFF_B],
                                      p[..., OFF_B:OFF_GATE_A], qkv0[l], S0[l], P['qkv_conv_w'][l],
                                      P['a_log'][l], P['dt_bias'][l], P['o_norm_g'][l], P['w_delta_out'][l])
        merged = (jax.nn.sigmoid(p[..., OFF_GATE_A:OFF_GATE_B]) * yA
                  + jax.nn.sigmoid(p[..., OFF_GATE_B:N_IN]) * yB)
        x = x + merged @ P['w_o'][l]
        h2 = _rmsnorm(x, P['norm2_g'][l])
        i = l // 2
        if l % 2 == 0:
            x = x + _swiglu(h2, P['ffn_w_gate'][i], P['ffn_w_up'][i], P['ffn_w_down'][i])
        else:
            x = x + _moe(h2, P['router_w'][i], P['exp_w_gate'][i], P['exp_w_up'][i], P['exp_w_down'][i])
        news_S.append(S)
        news_q.append(qbuf)
        news_d.append(dbuf)
    y = _rmsnorm(x, P['final_norm_g'])
    return y, jnp.stack(news_S), jnp.stack(news_q), jnp.stack(news_d)

def setup_inputs(seed: int = 0) -> dict:
    key = jax.random.key(seed)
    ks = iter(jax.random.split(key, 40))

    def nrm(shape, scale):
        return scale * jax.random.normal(next(ks), shape, jnp.float32)

    x_prompt = nrm((BATCH, SEQ, D_MODEL), 1.0)
    x_sample = nrm((DEC_BATCH, DEC_SEQ, D_MODEL), 1.0)
    state_delta = nrm((DEPTH, DEC_BATCH, N_HEADS, HEAD_K, HEAD_V), 0.1)
    state_qkv_conv = nrm((DEPTH, DEC_BATCH, QK_CONV - 1, CONV_DIM), 1.0)
    state_dwconv = nrm((DEPTH, DEC_BATCH, DW_WIDTH - 1, D_CONV), 0.5)
    norm1_g = 1.0 + nrm((DEPTH, D_MODEL), 0.02)
    w_in = nrm((DEPTH, D_MODEL, N_IN), D_MODEL ** -0.5)
    qkv_conv_w = nrm((DEPTH, QK_CONV, CONV_DIM), QK_CONV ** -0.5)
    a_log = jnp.log(jax.random.uniform(next(ks), (DEPTH, N_HEADS), jnp.float32, 1.0, 16.0))
    dt = jnp.exp(jax.random.uniform(next(ks), (DEPTH, N_HEADS), jnp.float32,
                                    math.log(1e-3), math.log(1e-1)))
    dt_bias = dt + jnp.log(-jnp.expm1(-dt))
    o_norm_g = 1.0 + nrm((DEPTH, HEAD_V), 0.02)
    w_delta_out = nrm((DEPTH, D_DELTA_V, D_MODEL), D_DELTA_V ** -0.5)
    dw_w = nrm((DEPTH, DW_WIDTH, D_CONV), DW_WIDTH ** -0.5)
    dw_b = nrm((DEPTH, D_CONV), 0.02)
    ln_g = 1.0 + nrm((DEPTH, D_CONV), 0.02)
    ln_b = nrm((DEPTH, D_CONV), 0.02)
    w_conv_out = nrm((DEPTH, D_CONV, D_MODEL), D_CONV ** -0.5)
    w_o = nrm((DEPTH, D_MODEL, D_MODEL), D_MODEL ** -0.5)
    norm2_g = 1.0 + nrm((DEPTH, D_MODEL), 0.02)
    ffn_w_gate = nrm((N_DENSE, D_MODEL, D_FF), D_MODEL ** -0.5)
    ffn_w_up = nrm((N_DENSE, D_MODEL, D_FF), D_MODEL ** -0.5)
    ffn_w_down = nrm((N_DENSE, D_FF, D_MODEL), D_FF ** -0.5)
    router_w = nrm((N_MOE, D_MODEL, N_EXPERTS), D_MODEL ** -0.5)
    exp_w_gate = nrm((N_MOE, N_EXPERTS, D_MODEL, D_FF_EXPERT), D_MODEL ** -0.5)
    exp_w_up = nrm((N_MOE, N_EXPERTS, D_MODEL, D_FF_EXPERT), D_MODEL ** -0.5)
    exp_w_down = nrm((N_MOE, N_EXPERTS, D_FF_EXPERT, D_MODEL), D_FF_EXPERT ** -0.5)
    final_norm_g = 1.0 + nrm((D_MODEL,), 0.02)
    return {'x_prompt': x_prompt, 'x_sample': x_sample, 'state_delta': state_delta,
            'state_qkv_conv': state_qkv_conv, 'state_dwconv': state_dwconv,
            'norm1_g': norm1_g, 'w_in': w_in, 'qkv_conv_w': qkv_conv_w, 'a_log': a_log,
            'dt_bias': dt_bias, 'o_norm_g': o_norm_g, 'w_delta_out': w_delta_out,
            'dw_w': dw_w, 'dw_b': dw_b, 'ln_g': ln_g, 'ln_b': ln_b, 'w_conv_out': w_conv_out,
            'w_o': w_o, 'norm2_g': norm2_g, 'ffn_w_gate': ffn_w_gate, 'ffn_w_up': ffn_w_up,
            'ffn_w_down': ffn_w_down, 'router_w': router_w, 'exp_w_gate': exp_w_gate,
            'exp_w_up': exp_w_up, 'exp_w_down': exp_w_down, 'final_norm_g': final_norm_g}

def reference(x_prompt, x_sample, state_delta, state_qkv_conv, state_dwconv,
              norm1_g, w_in, qkv_conv_w, a_log, dt_bias, o_norm_g, w_delta_out,
              dw_w, dw_b, ln_g, ln_b, w_conv_out, w_o, norm2_g,
              ffn_w_gate, ffn_w_up, ffn_w_down, router_w, exp_w_gate, exp_w_up, exp_w_down,
              final_norm_g):
    P = dict(norm1_g=norm1_g, w_in=w_in, qkv_conv_w=qkv_conv_w, a_log=a_log, dt_bias=dt_bias,
             o_norm_g=o_norm_g, w_delta_out=w_delta_out, dw_w=dw_w, dw_b=dw_b, ln_g=ln_g,
             ln_b=ln_b, w_conv_out=w_conv_out, w_o=w_o, norm2_g=norm2_g,
             ffn_w_gate=ffn_w_gate, ffn_w_up=ffn_w_up, ffn_w_down=ffn_w_down,
             router_w=router_w, exp_w_gate=exp_w_gate, exp_w_up=exp_w_up,
             exp_w_down=exp_w_down, final_norm_g=final_norm_g)
    nb = x_prompt.shape[0]
    S0_p = jnp.zeros((DEPTH, nb, N_HEADS, HEAD_K, HEAD_V), state_delta.dtype)
    q0_p = jnp.zeros((DEPTH, nb, QK_CONV - 1, CONV_DIM), state_qkv_conv.dtype)
    d0_p = jnp.zeros((DEPTH, nb, DW_WIDTH - 1, D_CONV), state_dwconv.dtype)
    y_prompt, S_p, q_p, d_p = _trunk(x_prompt, S0_p, q0_p, d0_p, P)
    y_sample, S_s, q_s, d_s = _trunk(x_sample, state_delta, state_qkv_conv, state_dwconv, P)
    return (y_prompt, y_sample, S_p, q_p, d_p, S_s, q_s, d_s)


_drawn_inputs = setup_inputs


def setup_inputs(seed=0):
    import zlib

    import numpy as np

    out = dict(_drawn_inputs(seed))
    spreads = {}
    factors = {}
    for name, (base, spread) in spreads.items():
        noise = np.random.default_rng([zlib.crc32(name.encode()), seed]).standard_normal(out[name].shape)
        drawn = base * np.exp(spread * noise) if base else spread * noise
        out[name] = __import__('jax').numpy.asarray(drawn.astype(out[name].dtype))
    for name, factor in factors.items():
        out[name] = (out[name] * factor).astype(out[name].dtype)
    return out
```

```python
from contextlib import ExitStack

import numpy as np

import concourse.bass as bass
from concourse import mybir

ALU = mybir.AluOpType
ACT = mybir.ActivationFunctionType
F32 = mybir.dt.float32
AX_X = mybir.AxisListType.X

P = 128
D = 1024
KD = D // P
TP = 256
NB = 8
T = TP + NB
NC = TP // P
H = 4
U = NC * H
DEPTH = 2
DW = 31
QW = 4
CT = 4
QT = 12
FT = 22
NE = 8
EPS = 1e-6
N_PROJ = 40
N_MIX = 8
N_WO = 8
N_FFN = 66
N_LAYER = N_PROJ + N_MIX + N_WO
RING = 22
LEVELS = 7
SAMPLE_ROW = P - NB


def first_position(section):
    return {"mix0": 0, "ffn": 3 * RING, "mix1": 6 * RING, "experts": 9 * RING}[section]


def build(nc, a, o):
    ctx = ExitStack()
    with ctx:
        def sb(name, shape, dt=F32):
            return ctx.enter_context(nc.sbuf_tensor(name, [P] + list(shape), dt))

        def sem(name):
            return ctx.enter_context(nc.semaphore(name))

        ring = sb("ring", [RING, KD, P])
        xT = sb("xT", [KD, T])
        hT = sb("hT", [KD, T])
        early = sb("early", [NB * H * P])
        n_pad = CT * (DW - 1 + TP)
        u_pad = early[:, 0:n_pad].rearrange("p (c n) -> p c n", c=CT)
        u_win = early[:, n_pad:n_pad + CT * NB * DW].rearrange("p (c b n) -> p c b n", c=CT, b=NB)
        s0 = early[:, :].rearrange("p (u n) -> p u n", n=P)
        c = sb("c", [CT, T])
        qkv = sb("qkv", [QT, T])
        zs = sb("zs", [H, T])
        gs = sb("gs", [2 * KD, T])
        work = sb("work", [9, U * P])
        consts = sb("consts", [3 + LEVELS, P])
        small = sb("small", [576])
        prm = sb("prm", [a["params"].shape[1]])

        ident, ones, triu = (consts[:, i, :] for i in range(3))
        psum = ctx.enter_context(nc.psum_tensor("psum", [P, 8, 512], F32))

        def pair(b):
            return psum[:, b:b + 2, :].rearrange("p b (u i) -> p (b u) i", i=P)

        def units(w):
            return work[:, w, :].rearrange("p (u i) -> p u i", i=P)

        pads = work[:, 3:7, :].rearrange("p a b -> p (a b)")
        q_pad = pads[:, 0:QT * (QW - 1 + TP)].rearrange("p (t n) -> p t n", t=QT)
        q_win = pads[:, QT * (QW - 1 + TP):QT * (QW - 1 + TP + NB * QW)].rearrange(
            "p (t b n) -> p t b n", t=QT, b=NB)
        sq_qk = work[:, 3:6, :].rearrange("p a b -> p (a b)")[:, 0:2 * H * T].rearrange("p (k t) -> p k t", t=T)
        act_all = work[:, 0:6, :].rearrange("p a b -> p (a b)")[:, 0:FT * T].rearrange("p (f t) -> p f t", t=T)
        silu_g = work[:, 6, 0:3 * T].rearrange("p (r t) -> p r t", t=T)
        gate_row = gs[:, 0:NE, :]
        sq = gs[:, 0:KD, :]

        def glu_gate(j):
            return work[:, 7, (j % 2) * T:(j % 2 + 1) * T]

        def norm4(w):
            return work[:, w:w + 2, :].rearrange("p a b -> p (a b)")[:, 0:H * T].rearrange("p (h t) -> p h t", t=T)

        vmask = work[:, 0:4, :].rearrange("p a (u d) -> p (a u) d", d=P)

        at = {}
        pos = 0
        for name, n in PARAMS:
            at[name] = pos
            pos += n

        def par(name, i, n=1):
            return prm[:, at[name] + i:at[name] + i + n]

        def par_block(name, l, k):
            return prm[:, at[name] + l * k:at[name] + (l + 1) * k]

        smalls = {}
        spos = [0]

        def sm(name, n):
            smalls[name] = (spos[0], n)
            spos[0] += n
            return small[:, spos[0] - n:spos[0]]

        t_a = sm("t_a", 12)
        t_abs = sm("t_abs", 12)
        t_exp = sm("t_exp", 12)
        t_ln = sm("t_ln", 12)
        g_tok = sm("g_tok", 12)
        b_exp = sm("b_exp", 12)
        beta = sm("beta", 12)
        nea = sm("nea", 4)
        ab_tok = sm("ab_tok", 24)
        tables = sm("tables", 96)
        gcc = tables[:, 0:8]
        gl = tables[:, 8:16]
        betas = tables[:, 64:96]
        gd = sm("gd", 8)
        egc = sm("egc", 8)
        egl = sm("egl", 8)
        kdsc = sm("kdsc", 8)
        nbeg = sm("nbeg", 8)
        samp_rhs = sm("samp_rhs", 64)
        egs = sm("egs", 32)
        vn_s = sm("vn_s", 32)
        k_s = sm("k_s", 32)
        qk_s = sm("qk_s", 32)
        o_t = sm("o_t", 32)
        s_prod = sm("s_prod", 32)
        rl = sm("rl", 24)
        assert spos[0] <= 576
        rstd = sb("rstd", [T])
        rows32 = sb("rows32", [2, P])
        rt = sb("rt", [8, 24])

        slot_loaded = [sem(f"slot_loaded{i}") for i in range(RING)]
        units_used = sem("units_used")
        x_loaded = sem("x_loaded")
        consts_loaded = sem("consts_loaded")
        states_loaded = sem("states_loaded")
        dw_loaded = sem("dw_loaded")
        zeros_set = sem("zeros_set")
        squares_done = sem("squares_done")
        sums_done = sem("sums_done")
        h_done = sem("h_done")
        glu_sig = sem("glu_sig")
        glu_done = sem("glu_done")
        conv_out = sem("conv_out")
        act_evac = sem("act_evac")
        ab_done = sem("ab_done")
        soft_in = sem("soft_in")
        soft_exp = sem("soft_exp")
        g_done = sem("g_done")
        g_rows = sem("g_rows")
        l_args = sem("l_args")
        exp_small = sem("exp_small")
        exp_big = sem("exp_big")
        pool_l = sem("pool_l")
        qconv_done = sem("qconv_done")
        qkv_silu = sem("qkv_silu")
        qk_squares = sem("qk_squares")
        qk_sums = sem("qk_sums")
        rms_done = sem("rms_done")
        qk_rms = sem("qk_rms")
        o_rms = sem("o_rms")
        ln_rms = sem("ln_rms")
        qk_normed = sem("qk_normed")
        gram_done = sem("gram_done")
        gram_taken = sem("gram_taken")
        level_masked = sem("level_masked")
        first_tr = sem("first_tr")
        tu_done = sem("tu_done")
        b_mm = sem("b_mm")
        b_taken = sem("b_taken")
        pq_mm = sem("pq_mm")
        kv_tr = sem("kv_tr")
        kv_taken = sem("kv_taken")
        w_mm = sem("w_mm")
        w_taken = sem("w_taken")
        vn_mm = sem("vn_mm")
        vn_taken = sem("vn_taken")
        os_mm = sem("os_mm")
        os_taken = sem("os_taken")
        samp_mm = sem("samp_mm")
        samp_vn = sem("samp_vn")
        samp_tr = sem("samp_tr")
        samp_rows = sem("samp_rows")
        samp_vm = sem("samp_vm")
        s0_scaled = sem("s0_scaled")
        outer_mm = sem("outer_mm")
        outer_taken = sem("outer_taken")
        o_squares = sem("o_squares")
        o_sums = sem("o_sums")
        o_done = sem("o_done")
        ln_sum = sem("ln_sum")
        ln_cen = sem("ln_cen")
        ln_sq = sem("ln_sq")
        ln_var = sem("ln_var")
        ln_norm = sem("ln_norm")
        c_done = sem("c_done")
        merged_done = sem("merged_done")
        x_done = sem("x_done")
        silu_done = sem("silu_done")
        act_done = sem("act_done")
        down_done = sem("down_done")
        down_taken = sem("down_taken")
        router_mm = sem("router_mm")
        gates_exp_in = sem("gates_exp_in")
        gates_exp = sem("gates_exp")
        gate_rhs = sem("gate_rhs")
        gate_mm = sem("gate_mm")
        gate_taken = sem("gate_taken")
        gate_step = sem("gate_step")
        s0_loaded = sem("s0_loaded")
        y_done = sem("y_done")
        state_out = sem("state_out")
        final_out = sem("final_out")
        dve_step = sem("dve_step")
        act_step = sem("act_step")
        pool_step = sem("pool_step")

        ordinal = {}
        n = 0
        for section, count in (("mix0", N_LAYER), ("ffn", N_FFN), ("mix1", N_LAYER)):
            for i in range(count):
                ordinal[first_position(section) + i] = n
                n += 1
        base_ord = {"mix0": 0, "ffn": N_LAYER, "mix1": N_LAYER + N_FFN, "experts": 2 * N_LAYER + N_FFN}

        def uses_before(position):
            return sum(1 for p in ordinal if p < position and p % RING == position % RING)

        block = ctx.enter_context(nc.Block())

        @block.sync
        def _(sp):
            def load_static(section, i, src):
                p = first_position(section) + i
                before = [q for q in ordinal if q < p and q % RING == p % RING]
                if before:
                    sp.wait_ge(units_used, ordinal[max(before)] + 1)
                sp.dma_start(ring[:, p % RING, :, :].rearrange("p k n -> p (k n)"), src).then_inc(slot_loaded[p % RING], 16)

            def load_rest(section, revolutions, src, base):
                with sp.Fori(1, revolutions) as r:
                    for s in range(RING):
                        sp.wait_ge(units_used, r * RING + (base + s + 1 - RING))
                        sp.dma_start(ring[:, s, :, :].rearrange("p k n -> p (k n)"),
                                     src[bass.ds(r * RING + s, 1), :, :].rearrange("a p n -> p (a n)")
                                     ).then_inc(slot_loaded[s], 16)

            for i in range(N_LAYER):
                load_static("mix0", i, a["w_mixer"][0, i])
            for i in range(RING):
                load_static("ffn", i, a["w_ffn"][i])
            load_rest("ffn", N_FFN // RING, a["w_ffn"], base_ord["ffn"])
            for i in range(N_LAYER):
                load_static("mix1", i, a["w_mixer"][1, i])
            for i in range(RING):
                load_static("experts", i, a["w_exp"][i])
            load_rest("experts", NE * N_FFN // RING, a["w_exp"], base_ord["experts"])

        @block.gpsimd
        def _(pool):
            pool_n = [0]

            def settle(ins):
                pool_n[0] += 1
                ins.then_inc(pool_step, 1)
                pool.wait_ge(pool_step, pool_n[0])

            pool.dma_start(xT[:, :, :].rearrange("p k t -> p (k t)"), a["xT"]).then_inc(x_loaded, 16)
            pool.dma_start(prm[:, :], a["params"]).then_inc(consts_loaded, 16)
            pool.dma_start(consts[:, :, :].rearrange("p k t -> p (k t)"), a["consts"]).then_inc(consts_loaded, 16)
            for l in range(DEPTH):
                if l:
                    pool.wait_ge(merged_done, KD * l)
                    pool.wait_ge(state_out, 16 * 6 * l)
                    pool.wait_ge(down_taken, KD * l)
                nc.gpsimd.memset(u_pad[:, :, 0:DW - 1], 0.0).then_inc(zeros_set, 1)
                nc.gpsimd.memset(q_pad[:, :, 0:QW - 1], 0.0).then_inc(zeros_set, 1)
                pool.dma_start(early[:, n_pad:n_pad + CT * NB * DW], a["dw_win"][l]).then_inc(dw_loaded, 16)
                pool.dma_start(q_win.rearrange("p t b n -> p (t b n)"), a["qkv_win"][l]).then_inc(states_loaded, 16)
                pool.wait_ge(exp_big, 3 * l + 2)
                nc.gpsimd.tensor_tensor(units(1), units(1), triu.rearrange("p (a i) -> p a i", a=1).broadcast_to([P, U, P]), ALU.mult)
                pool.wait_ge(exp_big, 3 * l + 3)
                pool.wait_ge(g_done, l + 1)
                nc.gpsimd.tensor_tensor(units(2), units(2), beta[:, 0:U].rearrange("p (u a) -> p u a", a=1).broadcast_to([P, U, P]),
                                        ALU.mult).then_inc(pool_l, 1)
                pool.wait_ge(glu_done, CT * (l + 1))
                pool.dma_start(o["dwp"][l], u_pad[:, :, TP:TP + DW - 1]).then_inc(state_out, 16)
                pool.dma_start(o["dws"][l], early[:, n_pad:n_pad + CT * NB * DW]).then_inc(state_out, 16)
                pool.wait_ge(act_evac, 32 * l + QT)
                pool.dma_start(o["qkp"][l], q_pad[:, :, TP:TP + QW - 1]).then_inc(state_out, 16)
                pool.dma_start(o["qks"][l], q_win.rearrange("p t b n -> p (t b n)")).then_inc(state_out, 16)
                pool.wait_ge(conv_out, CT * (l + 1))
                pool.wait_ge(state_out, 16 * (6 * l + 4))
                pool.dma_start(early[:, :], a["s0"][l]).then_inc(s0_loaded, 16)
                pool.wait_ge(gram_taken, 2 * l + 2)
                for v in range(LEVELS):
                    if v == 2:
                        pool.wait_ge(tu_done, LEVELS * l + 1)
                    elif v > 2:
                        pool.wait_ge(b_mm, (LEVELS - 1) * l + v - 2)
                    nc.gpsimd.tensor_tensor(units(5 + v % 2), units(7),
                                            consts[:, 3 + v, :].rearrange("p (a i) -> p a i", a=1).broadcast_to([P, U, P]),
                                            ALU.mult).then_inc(level_masked, 1)
                pool.wait_ge(samp_mm, l + 1)
                pool.wait_ge(exp_small, 2 * l + 2)
                nc.gpsimd.tensor_tensor(s0[:, :, :], s0[:, :, :], egs.rearrange("p (u a) -> p u a", a=1).broadcast_to([P, NB * H, P]),
                                        ALU.mult).then_inc(s0_scaled, 1)
                pool.wait_ge(os_taken, 2 * l + 2)
                pool.dma_start(o["sp"][l], units(3)[:, 0:H, :].rearrange("p h d -> p (h d)")).then_inc(state_out, 16)
                pool.wait_ge(outer_taken, 8 * (l + 1))
                pool.dma_start(o["ss"][l], early[:, :]).then_inc(state_out, 16)
            pool.wait_ge(y_done, KD)
            pool.dma_start(o["yT"], hT[:, :, :].rearrange("p k t -> p (k t)")).then_inc(final_out, 16)
            pool.wait_ge(state_out, 16 * 6 * DEPTH)
            pool.wait_ge(final_out, 16)

        @block.scalar
        def _(act):
            act_n = [0]

            def settle(ins):
                act_n[0] += 1
                ins.then_inc(act_step, 1)
                act.wait_ge(act_step, act_n[0])

            A = nc.scalar.activation

            def model_squares(l2):
                for k in range(KD):
                    if k == 0:
                        act.wait_ge(x_loaded, 16)
                    if l2 % 2:
                        act.wait_ge(x_done, KD * (l2 // 2) + k + 1)
                    elif l2:
                        act.wait_ge(down_taken, (0 if l2 == 2 else KD * NE) + k + 1)
                    A(sq[:, k, :], xT[:, k, :], ACT.Square).then_inc(squares_done, 1)

            def model_rms(l2):
                act.wait_ge(sums_done, l2 + 1)
                A(rstd[:, :], psum[:, 7, 0:T], ACT.Sqrt, scale=1.0 / D, bias=par("eps", 0)).then_inc(rms_done, 1)

            act.wait_ge(consts_loaded, 32)
            for l in range(DEPTH):
                model_squares(2 * l)
                model_rms(2 * l)
                for j in range(CT):
                    act.wait_ge(units_used, base_ord[f"mix{l}"] + 2 * j + 2)
                    if j >= 2:
                        act.wait_ge(glu_done, CT * l + j - 1)
                    A(glu_gate(j), psum[:, (2 * j + 1) % 4, 0:T], ACT.Sigmoid).then_inc(glu_sig, 1)
                act.wait_ge(soft_in, l + 1)
                A(t_exp, t_abs, ACT.Exp, scale=-1.0).then_inc(soft_exp, 1)
                act.wait_ge(soft_exp, 4 * l + 1)
                A(b_exp.rearrange("p (t n) -> p t n", t=3), ab_tok.rearrange("p (t n) -> p t n", t=3)[:, :, H:2 * H], ACT.Exp, scale=-1.0).then_inc(soft_exp, 1)
                A(nea, par_block("a_log", l, H), ACT.Exp).then_inc(soft_exp, 1)
                A(t_ln, t_exp, ACT.Ln, bias=1.0).then_inc(soft_exp, 1)

                def evac_qkv(t):
                    act.wait_ge(units_used, base_ord[f"mix{l}"] + 8 + t + 1)
                    if t == 0:
                        act.wait_ge(states_loaded, 16 * (l + 1))
                        act.wait_ge(zeros_set, 2 * l + 2)
                    b = (8 + t) % 4
                    A(q_pad[:, t, QW - 1:QW - 1 + TP], psum[:, b, 0:TP], ACT.Copy)
                    A(q_win[:, t, :, QW - 1], psum[:, b, TP:T], ACT.Copy).then_inc(act_evac, 1)

                evac_qkv(0)
                evac_qkv(1)
                act.wait_ge(l_args, l + 1)
                A(units(0), pair(6), ACT.Exp).then_inc(exp_big, 1)
                A(egc, gcc, ACT.Exp)
                A(egl, gl, ACT.Exp)
                A(egs, tables[:, 32:64], ACT.Exp).then_inc(exp_small, 1)
                A(kdsc, gd, ACT.Exp).then_inc(exp_small, 1)
                A(units(1), units(1), ACT.Exp).then_inc(exp_big, 1)
                A(units(2), units(2), ACT.Exp, scale=-1.0).then_inc(exp_big, 1)
                for t in range(2, QT):
                    evac_qkv(t)
                for t in range(H):
                    act.wait_ge(units_used, base_ord[f"mix{l}"] + 20 + t + 1)
                    A(zs[:, t, :], psum[:, (20 + t) % 4, 0:T], ACT.Silu).then_inc(act_evac, 1)
                for t in range(QT):
                    act.wait_ge(qconv_done, QT * l + t + 1)
                    A(qkv[:, t, :], qkv[:, t, :], ACT.Silu).then_inc(qkv_silu, 1)
                act.wait_ge(qkv_silu, QT * (l + 1))
                act.wait_ge(state_out, 16 * (6 * l + 4))
                for t in range(2 * H):
                    A(sq_qk[:, t, :], qkv[:, t, :], ACT.Square).then_inc(qk_squares, 1)

                for i in range(2):
                    act.wait_ge(qk_sums, 2 * H * l + (i + 1) * H)
                    if i:
                        act.wait_ge(qk_normed, 2 * l + 1)
                    A(norm4(7), psum[:, 4:8, 0:T], ACT.Sqrt, bias=par("eps", 0)).then_inc(qk_rms, 1)

                def gate(t):
                    act.wait_ge(units_used, base_ord[f"mix{l}"] + 24 + t + 1)
                    A(gs[:, t, :], psum[:, (24 + t) % 4, 0:T], ACT.Sigmoid).then_inc(act_evac, 1)

                gate(0)
                gate(1)
                gate(2)
                gate(3)
                for v in range(1, LEVELS):
                    act.wait_ge(b_mm, (LEVELS - 1) * l + v)
                    A(units(8), pair(4), ACT.Copy).then_inc(b_taken, 1)
                    gate(2 * v + 2)
                    gate(2 * v + 3)
                act.wait_ge(w_mm, l + 1)
                A(units(8), pair(4), ACT.Copy).then_inc(w_taken, 1)
                for h in range(H):
                    if h == 0:
                        act.wait_ge(os_taken, 2 * l + 2)
                        act.wait_ge(samp_vn, 2 * l + 2)
                    A(work[:, 4 + h, 0:T], qkv[:, 8 + h, :], ACT.Square).then_inc(o_squares, 1)
                act.wait_ge(o_sums, H * (l + 1))
                A(norm4(0), psum[:, 4:8, 0:T], ACT.Sqrt, scale=1.0 / P, bias=par("eps", 0)).then_inc(o_rms, 1)
                act.wait_ge(ln_cen, CT * (l + 1))
                for j in range(CT):
                    A(work[:, 4 + j, 512:512 + T], c[:, j, :], ACT.Square).then_inc(ln_sq, 1)
                act.wait_ge(ln_var, l + 1)
                A(rstd[:, :], psum[:, 1, 0:T], ACT.Sqrt, scale=1.0 / (CT * P), bias=par("eps", 0)).then_inc(ln_rms, 1)
                for j in range(CT):
                    act.wait_ge(ln_norm, CT * l + j + 1)
                    A(c[:, j, :], c[:, j, :], ACT.Silu, scale=par("ln_g", l * CT + j), bias=par("ln_b", l * CT + j)).then_inc(c_done, 1)
                act.wait_ge(merged_done, KD * (l + 1))
                model_squares(2 * l + 1)
                model_rms(2 * l + 1)
                if l == 0:
                    with act.Fori(0, 2) as half:
                        for j in range(FT // 2):
                            f = half * (FT // 2) + j
                            act.wait_ge(units_used, f * 2 + (base_ord["ffn"] + 1))
                            if j == 0:
                                act.wait_ge(act_done, f)
                            elif j >= 3:
                                act.wait_ge(act_done, f - 2)
                            A(silu_g[:, j % 3, :], psum[:, 2 * (j % 3), 0:T], ACT.Silu).then_inc(silu_done, 1)
                else:
                    act.wait_ge(gates_exp_in, 1)
                    A(rt[:, 3, 0:3], rt[:, 2, 0:3], ACT.Exp).then_inc(gates_exp, 1)
                    with act.Fori(0, NE) as e:
                        with act.Fori(0, 2) as half:
                            for j in range(FT // 2):
                                act.wait_ge(units_used, e * N_FFN + half * FT + (base_ord["experts"] + 2 * j + 1))
                                f = e * FT + half * (FT // 2) + j
                                if j == 0:
                                    act.wait_ge(act_done, f + FT)
                                elif j >= 3:
                                    act.wait_ge(act_done, f + (FT - 2))
                                A(silu_g[:, j % 3, :], psum[:, 2 * (j % 3), 0:T], ACT.Silu).then_inc(silu_done, 1)
            model_squares(2 * DEPTH)
            model_rms(2 * DEPTH)

        @block.vector
        def _(dve):
            V = nc.vector
            dve_n = [0]

            def settle(ins):
                dve_n[0] += 1
                ins.then_inc(dve_step, 1)
                dve.wait_ge(dve_step, dve_n[0])

            def model_norm(l2, g_name, g_at, out, done):
                dve.wait_ge(rms_done, l2 + 1)
                settle(V.reciprocal(rstd[:, :], rstd[:, :]))
                for k in range(KD):
                    V.scalar_tensor_tensor(out[:, k, :], xT[:, k, :], par(g_name, g_at + k), rstd[:, :], ALU.mult, ALU.mult).then_inc(done, 1)

            dve.wait_ge(consts_loaded, 32)
            dve.wait_ge(x_loaded, 16)
            for l in range(DEPTH):
                model_norm(2 * l, "norm1", l * KD, hT, h_done)
                for j in range(CT):
                    dve.wait_ge(glu_sig, CT * l + j + 1)
                    if j == 0:
                        dve.wait_ge(dw_loaded, 16 * (l + 1))
                        dve.wait_ge(zeros_set, 2 * l + 1)
                    sg = glu_gate(j)
                    V.tensor_tensor(u_pad[:, j, DW - 1:], psum[:, (2 * j) % 4, 0:TP], sg[:, 0:TP], ALU.mult)
                    V.tensor_tensor(u_win[:, j, :, DW - 1], psum[:, (2 * j) % 4, TP:T], sg[:, TP:T], ALU.mult).then_inc(glu_done, 1)
                dve.wait_ge(ab_done, l + 1)
                settle(V.tensor_copy(ab_tok, psum[:, 4, 0:24]))
                ab = ab_tok.rearrange("p (t n) -> p t n", t=3)
                settle(V.tensor_tensor(t_a.rearrange("p (t n) -> p t n", t=3), ab[:, :, 0:H],
                                       par_block("dt_bias", l, H).rearrange("p (a n) -> p a n", a=1).broadcast_to([P, 3, H]), ALU.add))
                V.scalar_tensor_tensor(t_abs, t_a, -1.0, t_a, ALU.mult, ALU.max).then_inc(soft_in, 1)
                dve.wait_ge(soft_exp, 4 * (l + 1))
                settle(V.scalar_tensor_tensor(g_tok, t_a, 0.0, t_ln, ALU.max, ALU.add))
                settle(V.scalar_tensor_tensor(g_tok.rearrange("p (t n) -> p t n", t=3), g_tok.rearrange("p (t n) -> p t n", t=3), -1.0,
                                              nea.rearrange("p (a n) -> p a n", a=1).broadcast_to([P, 3, H]), ALU.mult, ALU.mult))
                settle(V.tensor_scalar(b_exp, b_exp, 1.0, None, ALU.add))
                settle(V.reciprocal(beta, b_exp))
                smask = par("samp_mask", 0, NB)
                for i, col in enumerate((g_tok, beta)):
                    V.tensor_tensor(samp_rhs[:, i * 32:(i + 1) * 32].rearrange("p (b h) -> p b h", h=H),
                                    smask.rearrange("p (b a) -> p b a", a=1).broadcast_to([P, NB, H]),
                                    col[:, 8:12].rearrange("p (a h) -> p a h", a=1).broadcast_to([P, NB, H]), ALU.mult)
                V.tensor_tensor(units(0), triu.rearrange("p (a i) -> p a i", a=1).broadcast_to([P, U, P]),
                                g_tok[:, 0:U].rearrange("p (u a) -> p u a", a=1).broadcast_to([P, U, P]), ALU.mult).then_inc(g_done, 1)
                dve.wait_ge(g_rows, l + 1)
                V.tensor_copy(tables[:, 32:96], psum[:, 4, 64:128])
                settle(V.tensor_copy(tables[:, 0:16], psum[:, 4, 32:48]))
                V.tensor_tensor(gd, gl, gcc, ALU.subtract)
                settle(V.tensor_tensor(units(1), pair(6), gcc.rearrange("p (u a) -> p u a", a=1).broadcast_to([P, U, P]), ALU.subtract))
                settle(V.tensor_scalar(work[:, 2, :], work[:, 1, :], 0.0, None, ALU.max))
                V.tensor_scalar(work[:, 1, :], work[:, 1, :], 0.0, None, ALU.min).then_inc(l_args, 1)
                dve.wait_ge(exp_small, 2 * l + 2)
                settle(V.scalar_tensor_tensor(nbeg, beta[:, 0:U], -1.0, egc, ALU.mult, ALU.mult))
                dve.wait_ge(glu_done, CT * (l + 1))
                for tap in range(DW):
                    for j in range(CT):
                        w = par("dw_w", (l * CT + j) * DW + tap)
                        if tap == 0:
                            ins = V.tensor_scalar(c[:, j, 0:TP], u_pad[:, j, 0:TP], w, par("dw_b", l * CT + j), ALU.mult, ALU.add)
                        else:
                            ins = V.scalar_tensor_tensor(c[:, j, 0:TP], u_pad[:, j, tap:tap + TP], w, c[:, j, 0:TP], ALU.mult, ALU.add)
                    settle(ins)
                prod = work[:, 8, 0:CT * NB * DW].rearrange("p (c b n) -> p c b n", c=CT, b=NB)
                for j in range(CT):
                    ins = V.tensor_tensor(prod[:, j], u_win[:, j], par("dw_w", (l * CT + j) * DW, DW).rearrange("p (a n) -> p a n", a=1).broadcast_to([P, NB, DW]), ALU.mult)
                settle(ins)
                for j in range(CT):
                    ins = V.tensor_reduce(c[:, j, TP:T], prod[:, j], AX_X, ALU.add)
                settle(ins)
                for j in range(CT):
                    V.tensor_scalar(c[:, j, TP:T], c[:, j, TP:T], par("dw_b", l * CT + j), None, ALU.add).then_inc(conv_out, 1)
                for t0 in range(0, QT, 4):
                    for tap in range(QW):
                        for t in range(t0, t0 + 4):
                            if tap == 0:
                                dve.wait_ge(act_evac, 32 * l + t + 1)
                            w = par("qk_w", (l * QT + t) * QW + tap)
                            if tap == 0:
                                ins = V.tensor_scalar(qkv[:, t, 0:TP], q_pad[:, t, 0:TP], w, None, ALU.mult)
                            else:
                                ins = V.scalar_tensor_tensor(qkv[:, t, 0:TP], q_pad[:, t, tap:tap + TP], w, qkv[:, t, 0:TP], ALU.mult, ALU.add)
                        settle(ins)
                    for t in range(t0, t0 + 4):
                        qprod = work[:, 8, 32 * t:32 * (t + 1)].rearrange("p (b n) -> p b n", b=NB)
                        ins = V.tensor_tensor(qprod, q_win[:, t], par("qk_w", (l * QT + t) * QW, QW).rearrange("p (a n) -> p a n", a=1).broadcast_to([P, NB, QW]), ALU.mult)
                    settle(ins)
                    for t in range(t0, t0 + 4):
                        qprod = work[:, 8, 32 * t:32 * (t + 1)].rearrange("p (b n) -> p b n", b=NB)
                        V.tensor_reduce(qkv[:, t, TP:T], qprod, AX_X, ALU.add).then_inc(qconv_done, 1)
                for i in range(2):
                    dve.wait_ge(qk_rms, 2 * l + i + 1)
                    settle(V.reciprocal(norm4(7), norm4(7)))
                    group = qkv[:, i * H:(i + 1) * H, :]
                    V.scalar_tensor_tensor(group, group, float(P) ** -0.5 if i == 0 else 1.0, norm4(7), ALU.mult, ALU.mult).then_inc(qk_normed, 1)
                dve.wait_ge(qk_normed, 2 * l + 2)
                dve.wait_ge(pool_l, l + 1)
                dve.wait_ge(gram_done, 2 * l + 1)
                V.tensor_tensor(units(7), pair(4), units(2), ALU.mult).then_inc(gram_taken, 1)
                dve.wait_ge(gram_done, 2 * l + 2)
                V.tensor_tensor(units(1), pair(6), units(1), ALU.mult).then_inc(gram_taken, 1)
                q4 = qkv[:, 0:H, 0:TP].rearrange("p h (c i) -> p c h i", c=NC)
                w04 = work[:, 0, :].rearrange("p (c h i) -> p c h i", c=NC, h=H)
                for cc in range(NC):
                    settle(V.tensor_tensor(w04[:, cc], w04[:, cc], q4[:, cc], ALU.mult))
                ib = ident.rearrange("p (a i) -> p a i", a=1).broadcast_to([P, U, P])
                dve.wait_ge(level_masked, LEVELS * l + 1)
                V.tensor_tensor(units(3), ib, units(5), ALU.subtract)
                dve.wait_ge(first_tr, l + 1)
                V.tensor_tensor(units(4), ib, pair(4), ALU.subtract).then_inc(tu_done, 1)
                for v in range(1, LEVELS):
                    n_pq = (2 * (LEVELS - 1) - 1) * l + 2 * (v - 1)
                    dve.wait_ge(pq_mm, n_pq + 1)
                    u_ins = V.tensor_tensor(units(4), units(4), pair(6), ALU.subtract)
                    if v < LEVELS - 1:
                        dve.wait_ge(pq_mm, n_pq + 2)
                        u_ins = V.tensor_tensor(units(3), units(3), pair(4), ALU.subtract)
                    u_ins.then_inc(tu_done, 1)
                bc = lambda col: col.rearrange("p (u a) -> p u a", a=1).broadcast_to([P, U, P])
                dve.wait_ge(kv_tr, l + 1)
                V.tensor_tensor(units(5), pair(4), bc(nbeg), ALU.mult)
                V.tensor_tensor(units(7), pair(4), bc(kdsc), ALU.mult)
                V.tensor_tensor(units(6), pair(6), bc(beta[:, 0:U]), ALU.mult).then_inc(kv_taken, 1)
                q_s = qkv[:, 0:H, TP:T].rearrange("p h b -> p b h")
                kk = qkv[:, H:2 * H, TP:T].rearrange("p h b -> p b h")
                vv = qkv[:, 2 * H:3 * H, TP:T].rearrange("p h b -> p b h")

                def bh(t):
                    return t.rearrange("p (b h) -> p b h", h=H)

                V.tensor_copy(bh(k_s), kk)
                V.tensor_tensor(bh(s_prod), q_s, kk, ALU.mult).then_inc(samp_vn, 1)
                for cc in range(NC):
                    dve.wait_ge(vn_mm, NC * l + cc + 1)
                    V.tensor_copy(work[:, 2, cc * 512:cc * 512 + 512], psum[:, 6, :]).then_inc(vn_taken, 1)
                    dve.wait_ge(os_mm, 2 * NC * l + 2 * cc + 1)
                    V.tensor_copy(qkv[:, 8:12, cc * P:(cc + 1) * P], psum[:, 4, :].rearrange("p (h i) -> p h i", h=H))
                    dve.wait_ge(os_mm, 2 * NC * l + 2 * cc + 2)
                    if cc == 0:
                        V.tensor_copy(work[:, 3, 0:512], psum[:, 5, :]).then_inc(os_taken, 1)
                    else:
                        for h in range(H):
                            ins = V.scalar_tensor_tensor(units(3)[:, h, :], units(3)[:, h, :], egl[:, cc * H + h:cc * H + h + 1],
                                                         psum[:, 5, h * P:(h + 1) * P], ALU.mult, ALU.add)
                        ins.then_inc(os_taken, 1)
                dve.wait_ge(samp_mm, l + 1)
                sk = psum[:, 7, 0:64].rearrange("p (u n) -> p u n", n=2)
                settle(V.tensor_tensor(vn_s, sk[:, :, 1], egs, ALU.mult))
                settle(V.tensor_tensor(bh(vn_s), vv, bh(vn_s), ALU.subtract))
                settle(V.tensor_tensor(vn_s, vn_s, betas, ALU.mult))
                V.tensor_tensor(o_t, sk[:, :, 0], egs, ALU.mult)
                settle(V.tensor_tensor(qk_s, psum[:, 7, 64:96], vn_s, ALU.mult))
                V.tensor_tensor(vv, bh(o_t), bh(qk_s), ALU.add).then_inc(samp_vn, 1)
                dve.wait_ge(samp_tr, l + 1)
                settle(V.tensor_copy(rows32[0:32, 0, :], psum[0:32, 7, 128:256]))
                V.tensor_copy(rows32[0:32, 1, :], psum[0:32, 7, 256:384]).then_inc(samp_rows, 1)
                dve.wait_ge(state_out, 16 * (6 * l + 5))
                V.tensor_tensor(vmask[0:32], rows32[0:32, 0, :].rearrange("p (a d) -> p a d", a=1).broadcast_to([32, 32, P]),
                                ident[0:32, 0:32].rearrange("p (u a) -> p u a", a=1).broadcast_to([32, 32, P]), ALU.mult).then_inc(samp_vm, 1)
                dve.wait_ge(s0_scaled, l + 1)
                for g in range(8):
                    dve.wait_ge(outer_mm, 8 * l + g + 1)
                    blk = s0[:, 4 * g:4 * g + 4, :].rearrange("p u d -> p (u d)")
                    V.tensor_tensor(blk, blk, psum[:, 4 + g % 2, :], ALU.add).then_inc(outer_taken, 1)
                dve.wait_ge(o_rms, l + 1)
                settle(V.reciprocal(norm4(0), norm4(0)))
                o_all = qkv[:, 2 * H:3 * H, :]
                settle(V.scalar_tensor_tensor(o_all, o_all, par("o_g", l), norm4(0), ALU.mult, ALU.mult))
                V.tensor_tensor(o_all, o_all, zs[:, :, :], ALU.mult).then_inc(o_done, 1)
                dve.wait_ge(ln_sum, l + 1)
                for j in range(CT):
                    V.scalar_tensor_tensor(c[:, j, :], psum[:, 0, 0:T], -1.0 / (CT * P), c[:, j, :], ALU.mult, ALU.add).then_inc(ln_cen, 1)
                dve.wait_ge(ln_rms, l + 1)
                settle(V.reciprocal(rstd[:, :], rstd[:, :]))
                for j in range(CT):
                    V.tensor_tensor(c[:, j, :], c[:, j, :], rstd[:, :], ALU.mult).then_inc(ln_norm, 1)
                for t in range(KD):
                    dve.wait_ge(units_used, base_ord[f"mix{l}"] + N_PROJ + t + 1)
                    settle(V.tensor_tensor(gs[:, t, :], gs[:, t, :], psum[:, 2 * (t % 2), 0:T], ALU.mult))
                    settle(V.tensor_tensor(gs[:, KD + t, :], gs[:, KD + t, :], psum[:, 2 * (t % 2) + 1, 0:T], ALU.mult))
                    V.tensor_tensor(hT[:, t, :], gs[:, t, :], gs[:, KD + t, :], ALU.add).then_inc(merged_done, 1)
                for t in range(KD):
                    dve.wait_ge(units_used, base_ord[f"mix{l}"] + N_PROJ + N_MIX + t + 1)
                    V.tensor_tensor(xT[:, t, :], xT[:, t, :], psum[:, t % 4, 0:T], ALU.add).then_inc(x_done, 1)
                dve.wait_ge(x_done, KD * (l + 1))
                model_norm(2 * l + 1, "norm2", l * KD, hT, h_done)
                if l == 0:
                    with dve.Fori(0, 2) as half:
                        for j in range(FT // 2):
                            f = half * (FT // 2) + j
                            dve.wait_ge(silu_done, f + 1)
                            dve.wait_ge(units_used, f * 2 + (base_ord["ffn"] + 2))
                            V.tensor_tensor(act_all[:, bass.ds(f, 1), :].rearrange("p a t -> p (a t)"), silu_g[:, j % 3, :],
                                            psum[:, 2 * (j % 3) + 1, 0:T], ALU.mult).then_inc(act_done, 1)
                    for t in range(KD):
                        if t % 4 == 3:
                            dve.wait_ge(units_used, base_ord["ffn"] + 2 * FT + (t + 1) * FT // KD)
                        else:
                            dve.wait_ge(down_done, t + 1 - t // 4)
                        if t >= 1:
                            dve.wait_ge(down_taken, t)
                        V.tensor_tensor(xT[:, t, :], xT[:, t, :], psum[:, 6 + t % 2, 0:T], ALU.add).then_inc(down_taken, 1)
                    dve.wait_ge(down_taken, KD)
                else:
                    dve.wait_ge(router_mm, 1)
                    lg = psum[:, 4, 0:24]
                    r3 = lambda t: t.rearrange("p (t e) -> p t e", e=NE)
                    c3 = lambda t: t.rearrange("p (t a) -> p t a", a=1).broadcast_to([P, 3, NE])
                    iota = par("iota", 0, 24)
                    logit, oh1, oh2, tmp = rl, rt[:, 5, :], rt[:, 6, :], rt[:, 7, :]
                    settle(V.tensor_copy(logit, lg))
                    settle(V.tensor_reduce(rt[:, 0, 0:3], r3(logit), AX_X, ALU.max))

                    def first_of(value, onehot):
                        settle(V.tensor_tensor(r3(tmp), r3(logit), c3(value), ALU.is_lt))
                        settle(V.scalar_tensor_tensor(tmp, tmp, 64.0, iota, ALU.mult, ALU.add))
                        settle(V.tensor_reduce(rt[:, 4, 0:3], r3(tmp), AX_X, ALU.min))
                        settle(V.tensor_tensor(r3(onehot), r3(iota), c3(rt[:, 4, 0:3]), ALU.is_equal))

                    first_of(rt[:, 0, 0:3], oh1)
                    settle(V.scalar_tensor_tensor(logit, oh1, -3.0e38, logit, ALU.mult, ALU.add))
                    settle(V.tensor_reduce(rt[:, 1, 0:3], r3(logit), AX_X, ALU.max))
                    first_of(rt[:, 1, 0:3], oh2)
                    V.tensor_tensor(rt[:, 2, 0:3], rt[:, 1, 0:3], rt[:, 0, 0:3], ALU.subtract).then_inc(gates_exp_in, 1)
                    dve.wait_ge(gates_exp, 1)
                    settle(V.tensor_scalar(rt[:, 0, 0:3], rt[:, 3, 0:3], 1.0, None, ALU.add))
                    settle(V.reciprocal(rt[:, 1, 0:3], rt[:, 0, 0:3]))
                    settle(V.tensor_tensor(rt[:, 2, 0:3], rt[:, 3, 0:3], rt[:, 1, 0:3], ALU.mult))
                    settle(V.tensor_tensor(r3(oh1), r3(oh1), c3(rt[:, 1, 0:3]), ALU.mult))
                    settle(V.tensor_tensor(r3(oh2), r3(oh2), c3(rt[:, 2, 0:3]), ALU.mult))
                    settle(V.tensor_tensor(oh1, oh1, oh2, ALU.add))
                    for m in range(3):
                        if m:
                            dve.wait_ge(gate_mm, m)
                        V.tensor_tensor(units(0), ib, bc(oh1[:, m * NE:(m + 1) * NE]), ALU.mult).then_inc(gate_rhs, 1)
                        dve.wait_ge(gate_mm, m + 1)
                        if m < 2:
                            V.tensor_copy(gate_row[:, :, m * P:(m + 1) * P], pair(4)).then_inc(gate_taken, 1)
                        else:
                            V.tensor_copy(gate_row[:, :, TP:T], pair(4)[:, :, SAMPLE_ROW:P]).then_inc(gate_taken, 1)
                    dve.wait_ge(gate_taken, 3)
                    with dve.Fori(0, NE) as e:
                        with dve.Fori(0, 2) as half:
                            for j in range(FT // 2):
                                f = half * (FT // 2) + j
                                dve.wait_ge(silu_done, e * FT + f + (FT + 1))
                                dve.wait_ge(units_used, e * N_FFN + half * FT + (base_ord["experts"] + 2 * j + 2))
                                V.tensor_tensor(act_all[:, bass.ds(f, 1), :].rearrange("p a t -> p (a t)"), silu_g[:, j % 3, :],
                                                psum[:, 2 * (j % 3) + 1, 0:T], ALU.mult).then_inc(act_done, 1)
                        for t in range(KD):
                            if t % 4 == 3:
                                dve.wait_ge(units_used, e * N_FFN + (base_ord["experts"] + 2 * FT + (t + 1) * FT // KD))
                            else:
                                dve.wait_ge(down_done, e * 6 + (6 + t + 1 - t // 4))
                            dve.wait_ge(down_taken, e * KD + (KD + t))
                            V.tensor_tensor(work[:, 7, 0:T], psum[:, 6 + t % 2, 0:T],
                                                      gate_row[:, bass.ds(e, 1), :].rearrange("p a t -> p (a t)"), ALU.mult).then_inc(gate_step, 1)
                            dve.wait_ge(gate_step, e * KD + (t + 1))
                            V.tensor_tensor(xT[:, t, :], xT[:, t, :], work[:, 7, 0:T], ALU.add).then_inc(down_taken, 1)
                    dve.wait_ge(down_taken, KD * (NE + 1))
            model_norm(2 * DEPTH, "final", 0, hT, y_done)

        @block.tensor
        def _(pe):
            M = nc.tensor.matmul

            def arrived(section, i):
                p = first_position(section) + i
                pe.wait_ge(slot_loaded[p % RING], 16 * (uses_before(p) + 1))
                return ring[:, p % RING, :, :]

            def model_sums(l2):
                for k in range(KD):
                    pe.wait_ge(squares_done, KD * l2 + k + 1)
                    last = M(psum[:, 7, 0:T], ones, sq[:, k, :], start=(k == 0), stop=(k == KD - 1))
                last.then_inc(sums_done, 1)

            pe.wait_ge(consts_loaded, 32)
            for l in range(DEPTH):
                section = f"mix{l}"
                if l:
                    pe.wait_ge(down_taken, KD)
                model_sums(2 * l)

                def project(t):
                    w = arrived(section, t)
                    if t == 0:
                        pe.wait_ge(h_done, 2 * KD * l + KD)
                    elif 4 <= t < 12:
                        pe.wait_ge(glu_done, CT * l + (t - 4) // 2 + 1)
                    elif t >= 12:
                        pe.wait_ge(act_evac, 32 * l + t - 4 - 8 + 1)
                    for k in range(KD):
                        last = M(psum[:, t % 4, 0:T], w[:, k, :], hT[:, k, :], start=(k == 0), stop=(k == KD - 1))
                    last.then_inc(units_used, 1)

                for t in range(8):
                    project(t)
                for m, t0 in enumerate((0, P, T - P)):
                    for k in range(KD):
                        last = M(psum[:, 4, m * 8:m * 8 + 8], hT[:, k, t0:t0 + P], par_block("w_ab", l, KD * 8)[:, k * 8:(k + 1) * 8],
                                 start=(k == 0), stop=(k == KD - 1))
                last.then_inc(ab_done, 1)
                project(8)
                project(9)
                pe.wait_ge(g_done, l + 1)
                for b in range(2):
                    M(psum[:, 6 + b, :], ones, work[:, 0, b * 512:b * 512 + 512], start=True, stop=True)
                M(psum[:, 4, 32:40], triu, g_tok[:, 0:U], start=True, stop=True)
                M(psum[:, 4, 40:48], ones, g_tok[:, 0:U], start=True, stop=True)
                M(psum[:, 4, 64:128], ones, samp_rhs, start=True, stop=True).then_inc(g_rows, 1)
                for t in range(10, 24):
                    project(t)
                for t in range(2 * H):
                    if t == 0:
                        pe.wait_ge(exp_small, 2 * l + 2)
                        pe.wait_ge(l_args, l + 1)
                        pe.wait_ge(exp_big, 3 * l + 1)
                    if t == H:
                        project(24)
                        pe.wait_ge(qk_rms, 2 * l + 1)
                    pe.wait_ge(qk_squares, 2 * H * l + t + 1)
                    M(psum[:, 4 + t % 4, 0:T], ones, sq_qk[:, t, :], start=True, stop=True).then_inc(qk_sums, 1)
                project(25)
                pe.wait_ge(qk_normed, 2 * (l + 1))

                def kq(first, h, cc):
                    return qkv[:, first + h, cc * P:(cc + 1) * P]

                for cc in range(NC):
                    for h in range(H):
                        last = M(psum[:, 4 + cc, h * P:(h + 1) * P], kq(H, h, cc), kq(H, h, cc), start=True, stop=True)
                last.then_inc(gram_done, 1)
                for cc in range(NC):
                    for h in range(H):
                        last = M(psum[:, 6 + cc, h * P:(h + 1) * P], kq(H, h, cc), kq(0, h, cc), start=True, stop=True)
                last.then_inc(gram_done, 1)
                project(26)
                project(27)
                pe.wait_ge(level_masked, LEVELS * l + 1)
                pe.wait_ge(gram_taken, 2 * l + 1)
                for u in range(U):
                    last = nc.tensor.transpose(pair(4)[:, u, :], units(5)[:, u, :], ident)
                last.then_inc(first_tr, 1)
                for v in range(1, LEVELS):
                    pe.wait_ge(tu_done, LEVELS * l + v)
                    pe.wait_ge(level_masked, LEVELS * l + v + 1)
                    for u in range(U):
                        last = M(pair(4)[:, u, :], units(5 + v % 2)[:, u, :], units(4)[:, u, :], start=True, stop=True)
                    last.then_inc(b_mm, 1)
                    project(26 + 2 * v)
                    pe.wait_ge(b_taken, (LEVELS - 1) * l + v)
                    if v == 1:
                        pe.wait_ge(gram_taken, 2 * l + 2)
                    for u in range(U):
                        last = M(pair(6)[:, u, :], units(3)[:, u, :], units(8)[:, u, :], start=True, stop=True)
                    last.then_inc(pq_mm, 1)
                    if v < LEVELS - 1:
                        for u in range(U):
                            last = M(pair(4)[:, u, :], units(8)[:, u, :], units(3)[:, u, :], start=True, stop=True)
                        last.then_inc(pq_mm, 1)
                    project(27 + 2 * v)
                pe.wait_ge(tu_done, LEVELS * (l + 1))
                for cc in range(NC):
                    for h in range(H):
                        nc.tensor.transpose(psum[:, 4 + cc, h * P:(h + 1) * P], kq(H, h, cc), ident)
                        last = nc.tensor.transpose(psum[:, 6 + cc, h * P:(h + 1) * P], kq(2 * H, h, cc), ident)
                last.then_inc(kv_tr, 1)
                pe.wait_ge(kv_taken, l + 1)
                for u in range(U):
                    last = M(pair(4)[:, u, :], units(5)[:, u, :], units(4)[:, u, :], start=True, stop=True)
                last.then_inc(w_mm, 1)
                pe.wait_ge(samp_vn, 2 * l + 1)
                pe.wait_ge(s0_loaded, 16 * (l + 1))
                for b in range(NB):
                    for h in range(H):
                        u = b * H + h
                        M(psum[:, 7, 2 * u:2 * u + 2], s0[:, u, :], qkv[:, h:2 * H:H, TP + b], start=True, stop=True)
                M(psum[:, 7, 64:96], ones, s_prod, start=True, stop=True).then_inc(samp_mm, 1)
                for cc in range(NC):
                    if cc:
                        pe.wait_ge(os_taken, 2 * l + cc)
                    else:
                        pe.wait_ge(w_taken, l + 1)
                    for h in range(H):
                        u = cc * H + h
                        last = M(psum[:, 6, h * P:(h + 1) * P], units(4)[:, u, :], units(6)[:, u, :], start=True, stop=(cc == 0))
                        if cc:
                            last = M(psum[:, 6, h * P:(h + 1) * P], units(8)[:, u, :], units(3)[:, h, :], start=False, stop=True)
                    last.then_inc(vn_mm, 1)
                    pe.wait_ge(vn_taken, NC * l + cc + 1)
                    for h in range(H):
                        u = cc * H + h
                        last = M(psum[:, 4, h * P:(h + 1) * P], units(2)[:, u, :], units(1)[:, u, :], start=True, stop=(cc == 0))
                        if cc:
                            last = M(psum[:, 4, h * P:(h + 1) * P], units(3)[:, h, :], units(0)[:, u, :], start=False, stop=True)
                    last.then_inc(os_mm, 1)
                    for h in range(H):
                        u = cc * H + h
                        last = M(psum[:, 5, h * P:(h + 1) * P], units(7)[:, u, :], units(2)[:, u, :], start=True, stop=True)
                    last.then_inc(os_mm, 1)
                pe.wait_ge(samp_vn, 2 * l + 2)
                nc.tensor.transpose(psum[0:32, 7, 128:256], vn_s, ident)
                nc.tensor.transpose(psum[0:32, 7, 256:384], k_s, ident).then_inc(samp_tr, 1)
                pe.wait_ge(samp_rows, l + 1)
                pe.wait_ge(samp_vm, l + 1)
                pe.wait_ge(os_taken, 2 * l + 2)
                for g in range(8):
                    if g >= 2:
                        pe.wait_ge(outer_taken, 8 * l + g - 1)
                    M(psum[:, 4 + g % 2, :], rows32[0:32, 1, :], vmask[0:32, 4 * g:4 * g + 4, :].rearrange("p u d -> p (u d)"),
                      start=True, stop=True).then_inc(outer_mm, 1)
                pe.wait_ge(outer_taken, 8 * (l + 1))
                for h in range(H):
                    pe.wait_ge(o_squares, H * l + h + 1)
                    M(psum[:, 4 + h, 0:T], ones, work[:, 4 + h, 0:T], start=True, stop=True).then_inc(o_sums, 1)
                pe.wait_ge(conv_out, CT * (l + 1))
                pe.wait_ge(act_evac, 32 * (l + 1))
                for j in range(CT):
                    last = M(psum[:, 0, 0:T], ones, c[:, j, :], start=(j == 0), stop=(j == CT - 1))
                last.then_inc(ln_sum, 1)
                for j in range(CT):
                    pe.wait_ge(ln_sq, CT * l + j + 1)
                    last = M(psum[:, 1, 0:T], ones, work[:, 4 + j, 512:512 + T], start=(j == 0), stop=(j == CT - 1))
                last.then_inc(ln_var, 1)
                pe.wait_ge(o_done, l + 1)
                pe.wait_ge(c_done, CT * (l + 1))
                for t in range(KD):
                    w = arrived(section, N_PROJ + t)
                    if t >= 2:
                        pe.wait_ge(merged_done, KD * l + t - 1)
                    for j in range(CT):
                        M(psum[:, 2 * (t % 2), 0:T], w[:, j, :], c[:, j, :], start=(j == 0), stop=(j == CT - 1))
                    for h in range(H):
                        last = M(psum[:, 2 * (t % 2) + 1, 0:T], w[:, CT + h, :], qkv[:, 8 + h, :], start=(h == 0), stop=(h == H - 1))
                    last.then_inc(units_used, 1)
                pe.wait_ge(merged_done, KD * (l + 1))
                for t in range(KD):
                    w = arrived(section, N_PROJ + N_MIX + t)
                    if t >= 4:
                        pe.wait_ge(x_done, KD * l + t - 3)
                    for k in range(KD):
                        last = M(psum[:, t % 4, 0:T], w[:, k, :], hT[:, k, :], start=(k == 0), stop=(k == KD - 1))
                    last.then_inc(units_used, 1)
                model_sums(2 * l + 1)

                def hidden(loaded, n_act, j):
                    if j in (0, 1):
                        pe.wait_ge(act_done, n_act - 1)
                    else:
                        pe.wait_ge(act_done, n_act - 2)
                    for i in range(2):
                        pe.wait_ge(slot_loaded[2 * j + i], loaded(2 * j + i))
                        for k in range(KD):
                            last = M(psum[:, 2 * (j % 3) + i, 0:T], ring[:, 2 * j + i, k, :], hT[:, k, :], start=(k == 0), stop=(k == KD - 1))
                        last.then_inc(units_used, 1)

                def down(loaded, n_act, n_taken):
                    for i in range(KD * FT):
                        t, f = divmod(i, FT)
                        s = i // KD
                        if i % KD == 0:
                            pe.wait_ge(slot_loaded[s], loaded(s))
                        if i == 0:
                            pe.wait_ge(act_done, n_act + FT)
                        if f == 0:
                            pe.wait_ge(down_taken, n_taken + t - 1)
                        last = M(psum[:, 6 + t % 2, 0:T], ring[:, s, i % KD, :], act_all[:, f, :], start=(f == 0), stop=(f == FT - 1))
                        if i % KD == KD - 1:
                            last.then_inc(units_used, 1)
                        elif f == FT - 1:
                            last.then_inc(down_done, 1)

                if l == 0:
                    n0 = [uses_before(first_position("ffn") + s) for s in range(RING)]
                    pe.wait_ge(h_done, 2 * KD)
                    for half in range(2):
                        for j in range(FT // 2):
                            n_act = half * (FT // 2) + j
                            if n_act >= 3:
                                pe.wait_ge(act_done, n_act - (1 if j < 2 else 2))
                            for i in range(2):
                                pe.wait_ge(slot_loaded[2 * j + i], 16 * (n0[2 * j + i] + half + 1))
                                for k in range(KD):
                                    last = M(psum[:, 2 * (j % 3) + i, 0:T], ring[:, 2 * j + i, k, :], hT[:, k, :], start=(k == 0), stop=(k == KD - 1))
                                last.then_inc(units_used, 1)
                    for i in range(KD * FT):
                        t, f = divmod(i, FT)
                        s = i // KD
                        if i % KD == 0:
                            pe.wait_ge(slot_loaded[s], 16 * (n0[s] + 3))
                        if i == 0:
                            pe.wait_ge(act_done, FT)
                        if f == 0 and t >= 2:
                            pe.wait_ge(down_taken, t - 1)
                        last = M(psum[:, 6 + t % 2, 0:T], ring[:, s, i % KD, :], act_all[:, f, :], start=(f == 0), stop=(f == FT - 1))
                        if i % KD == KD - 1:
                            last.then_inc(units_used, 1)
                        elif f == FT - 1:
                            last.then_inc(down_done, 1)
                else:
                    n0 = [uses_before(first_position("experts") + s) for s in range(RING)]
                    pe.wait_ge(h_done, 4 * KD)
                    for m, t0 in enumerate((0, P, T - P)):
                        for k in range(KD):
                            last = M(psum[:, 4, m * 8:m * 8 + 8], hT[:, k, t0:t0 + P], par("router", k * 8, 8),
                                     start=(k == 0), stop=(k == KD - 1))
                    last.then_inc(router_mm, 1)
                    for m in range(3):
                        pe.wait_ge(gate_rhs, m + 1)
                        if m:
                            pe.wait_ge(gate_taken, m)
                        M(psum[:, 4, :], ones, work[:, 0, 0:512], start=True, stop=True)
                        M(psum[:, 5, :], ones, work[:, 0, 512:1024], start=True, stop=True).then_inc(gate_mm, 1)
                    pe.wait_ge(gate_taken, 3)
                    with pe.Fori(0, NE) as e:
                        with pe.Fori(0, 2) as half:
                            for j in range(FT // 2):
                                hidden(lambda s: e * 48 + half * 16 + 16 * (n0[s] + 1), e * FT + half * (FT // 2) + (FT + j), j)
                        down(lambda s: e * 48 + 16 * (n0[s] + 3), e * FT + FT, e * KD + KD)
            pe.wait_ge(down_taken, KD * (NE + 1))
            model_sums(2 * DEPTH)


PARAMS = [("norm1", DEPTH * KD), ("norm2", DEPTH * KD), ("final", KD), ("o_g", DEPTH), ("dw_b", DEPTH * CT),
          ("ln_g", DEPTH * CT), ("ln_b", DEPTH * CT), ("dw_w", DEPTH * CT * DW), ("qk_w", DEPTH * QT * QW),
          ("a_log", DEPTH * H), ("dt_bias", DEPTH * H), ("w_ab", DEPTH * KD * 8), ("router", KD * NE),
          ("samp_mask", NB), ("iota", 24), ("eps", 1)]


def kernel(x_prompt, x_sample, state_delta, state_qkv_conv, state_dwconv, norm1_g, w_in, qkv_conv_w,
           a_log, dt_bias, o_norm_g, w_delta_out, dw_w, dw_b, ln_g, ln_b, w_conv_out, w_o, norm2_g,
           ffn_w_gate, ffn_w_up, ffn_w_down, router_w, exp_w_gate, exp_w_up, exp_w_down, final_norm_g):
    import concourse.bacc as bacc
    from concourse.bass_utils import run_bass_kernel_spmd

    n = lambda x: np.ascontiguousarray(np.asarray(x))
    L, F = DEPTH, np.float32

    def feat(x):
        x = n(x)
        lead = tuple(range(x.ndim - 1))
        y = x.reshape(x.shape[:-1] + (x.shape[-1] // P, P))
        return y.transpose((y.ndim - 1, y.ndim - 2) + lead)

    def by_layer(x):
        return n(x).reshape(L, -1, P).transpose(2, 0, 1).reshape(P, -1)

    def out_tiles(w):
        w = n(w)
        return w.reshape(w.shape[0] // P, P, w.shape[1] // P, P).transpose(2, 1, 0, 3).reshape(w.shape[1] // P, P, -1)

    def ffn_units(wg, wu, wd):
        gu = np.stack([out_tiles(wg), out_tiles(wu)], 1).reshape(2 * FT, P, KD * P)
        blocks = n(wd).reshape(FT, P, KD, P).transpose(2, 0, 1, 3).reshape(FT, KD, P, P)
        return np.concatenate([gu, blocks.transpose(0, 2, 1, 3).reshape(FT, P, KD * P)])

    w_in = n(w_in)
    w_mixer = np.empty((L, N_LAYER, P, KD * P), F)
    for l in range(L):
        t = out_tiles(w_in[l, :, 0:3072])
        w_mixer[l, 0:8:2], w_mixer[l, 1:8:2], w_mixer[l, 8:24] = t[0:4], t[4:8], t[8:24]
        w_mixer[l, 24:40] = out_tiles(w_in[l, :, 3080:])
        w_mixer[l, 40:48] = np.concatenate([out_tiles(w_conv_out[l]), out_tiles(w_delta_out[l])], 2)
        w_mixer[l, 48:56] = out_tiles(w_o[l])
    w_exp = np.concatenate([ffn_units(exp_w_gate[0][e], exp_w_up[0][e], exp_w_down[0][e]) for e in range(NE)])

    everywhere = lambda x: np.broadcast_to(n(x).reshape(1, -1), (P, n(x).size))
    packed = {
        "norm1": by_layer(norm1_g), "norm2": by_layer(norm2_g), "final": n(final_norm_g).reshape(KD, P).T,
        "o_g": n(o_norm_g).T, "dw_b": by_layer(dw_b), "ln_g": by_layer(ln_g), "ln_b": by_layer(ln_b),
        "dw_w": n(dw_w).reshape(L, DW, CT, P).transpose(3, 0, 2, 1).reshape(P, -1),
        "qk_w": n(qkv_conv_w).reshape(L, QW, QT, P).transpose(3, 0, 2, 1).reshape(P, -1),
        "a_log": everywhere(a_log), "dt_bias": everywhere(dt_bias),
        "w_ab": w_in[:, :, 3072:3080].reshape(L, KD, P, 8).transpose(2, 0, 1, 3).reshape(P, -1),
        "router": n(router_w)[0].reshape(KD, P, NE).transpose(1, 0, 2).reshape(P, -1),
        "samp_mask": (np.arange(P)[:, None] == SAMPLE_ROW + np.arange(NB)[None]).astype(F),
        "eps": np.full((P, 1), EPS, F),
        "iota": np.broadcast_to(np.tile(np.arange(NE), 3).astype(F)[None], (P, 3 * NE)),
    }
    i, j = np.arange(P)[:, None], np.arange(P)[None]
    masks = [i == j, i >= 0 * j, j >= i]
    for v in range(LEVELS):
        b = 1 << v
        masks.append((i // (2 * b) == j // (2 * b)) & (i // b % 2 == 1) & (j // b % 2 == 0))
    x_all = np.concatenate([n(x_prompt)[0], n(x_sample)[:, 0]], 0)

    def window(state, taps):
        s = n(state)
        w = np.zeros((L, P, s.shape[-1] // P, NB, taps), F)
        w[..., :-1] = s.reshape(L, NB, taps - 1, -1, P).transpose(0, 4, 3, 1, 2)
        return w.reshape(L, P, -1)

    arrays = {
        "xT": feat(x_all).reshape(P, -1), "params": np.concatenate([packed[k] for k, _ in PARAMS], 1),
        "consts": np.stack(masks, 1).astype(F).reshape(P, -1), "w_mixer": w_mixer,
        "w_ffn": ffn_units(ffn_w_gate[0], ffn_w_up[0], ffn_w_down[0]), "w_exp": w_exp,
        "s0": n(state_delta).transpose(0, 3, 1, 2, 4).reshape(L, P, -1),
        "dw_win": window(state_dwconv, DW), "qkv_win": window(state_qkv_conv, QW),
    }
    outs = {"yT": (P, KD * T), "sp": (L, P, H * P), "ss": (L, P, NB * H * P), "dwp": (L, P, CT, DW - 1),
            "dws": (L, P, CT * NB * DW), "qkp": (L, P, QT, QW - 1), "qks": (L, P, QT * NB * QW)}

    nc = bacc.Bacc("TRN2", target_bir_lowering=False, num_devices=1)
    ins = {}
    for name, value in arrays.items():
        arrays[name] = np.ascontiguousarray(value)
        assert arrays[name].dtype == F, name
        ins[name] = nc.dram_tensor("in_" + name, value.shape, F32, kind="ExternalInput").ap()
    o = {name: nc.dram_tensor("out_" + name, shape, F32, kind="ExternalOutput").ap() for name, shape in outs.items()}
    build(nc, ins, o)
    r = run_bass_kernel_spmd(nc, [{"in_" + k: v for k, v in arrays.items()}], core_ids=[0]).results[0]
    g = {name: np.asarray(r["out_" + name]) for name in outs}

    y = g["yT"].reshape(P, KD, T).transpose(2, 1, 0).reshape(T, D)

    def rows(x, lead):
        x = x.reshape((L, P) + lead)
        return n(np.moveaxis(x, (2, 1), (-2, -1)).reshape((L,) + lead[1:] + (-1,)))

    return (
        n(y[None, :TP]), n(y[TP:, None]),
        n(g["sp"].reshape(L, P, H, P).transpose(0, 2, 1, 3)[:, None]),
        rows(g["qkp"], (QT, QW - 1))[:, None], rows(g["dwp"], (CT, DW - 1))[:, None],
        n(g["ss"].reshape(L, P, NB, H, P).transpose(0, 2, 3, 1, 4)),
        n(rows(g["qks"], (QT, NB, QW))[:, :, 1:]), n(rows(g["dws"], (CT, NB, DW))[:, :, 1:]),
    )
```

```python
from contextlib import ExitStack

import numpy as np

import concourse.bass as bass
from concourse import mybir

ALU = mybir.AluOpType
ACT = mybir.ActivationFunctionType
F32 = mybir.dt.float32
AX_X = mybir.AxisListType.X

P = 128
D = 1024
KD = D // P
TP = 256
NB = 8
T = TP + NB
NC = TP // P
H = 4
U = NC * H
DEPTH = 2
DW = 31
QW = 4
CT = 4
QT = 12
FT = 22
NE = 8
EPS = 1e-6
N_PROJ = 40
N_MIX = 8
N_WO = 8
N_FFN = 66
N_LAYER = N_PROJ + N_MIX + N_WO
RING = 22
LEVELS = 7
CAP = 96
MAX_JOBS = (2 * T + NE * (CAP - 1)) // CAP + 1
SAMPLE_ROW = P - NB


def first_position(section):
    return {"mix0": 0, "ffn": 3 * RING, "mix1": 6 * RING, "experts": 9 * RING}[section]


def build(nc, a, o):
    ctx = ExitStack()
    with ctx:
        def sb(name, shape, dt=F32):
            return ctx.enter_context(nc.sbuf_tensor(name, [P] + list(shape), dt))

        def sem(name):
            return ctx.enter_context(nc.semaphore(name))

        ring = sb("ring", [RING, KD, P])
        xT = sb("xT", [KD, T])
        hT = sb("hT", [KD, T])
        early = sb("early", [NB * H * P])
        n_pad = CT * (DW - 1 + TP)
        u_pad = early[:, 0:n_pad].rearrange("p (c n) -> p c n", c=CT)
        u_win = early[:, n_pad:n_pad + CT * NB * DW].rearrange("p (c b n) -> p c b n", c=CT, b=NB)
        s0 = early[:, :].rearrange("p (u n) -> p u n", n=P)
        c = sb("c", [CT, T])
        qkv = sb("qkv", [QT, T])
        zs = sb("zs", [H, T])
        gs = sb("gs", [2 * KD, T])
        work = sb("work", [9, U * P])
        consts = sb("consts", [4, P])
        level_masks = sb("level_masks", [LEVELS, P], mybir.dt.bfloat16)
        small = sb("small", [576])
        prm = sb("prm", [a["params"].shape[1]])

        ident, ones, triu, triu_strict = (consts[:, i, :] for i in range(4))
        psum = ctx.enter_context(nc.psum_tensor("psum", [P, 8, 512], F32))

        def pair(b):
            return psum[:, b:b + 2, :].rearrange("p b (u i) -> p (b u) i", i=P)

        def units(w):
            return work[:, w, :].rearrange("p (u i) -> p u i", i=P)

        pads = work[:, 3:7, :].rearrange("p a b -> p (a b)")
        q_pad = pads[:, 0:QT * (QW - 1 + TP)].rearrange("p (t n) -> p t n", t=QT)
        q_win = pads[:, QT * (QW - 1 + TP):QT * (QW - 1 + TP + NB * QW)].rearrange(
            "p (t b n) -> p t b n", t=QT, b=NB)
        sq_qk = work[:, 3:6, :].rearrange("p a b -> p (a b)")[:, 0:2 * H * T].rearrange("p (k t) -> p k t", t=T)
        act_all = work[:, 0:6, :].rearrange("p a b -> p (a b)")[:, 0:FT * T].rearrange("p (f t) -> p f t", t=T)
        silu_g = work[:, 6, 0:3 * T].rearrange("p (r t) -> p r t", t=T)
        h_tok = gs[:, :, :].rearrange("p k t -> p (k t)")[:, 0:3 * D].rearrange("p (m d) -> p m d", m=3)
        act_job = work[:, 0:3, :].rearrange("p a b -> p (a b)")[:, 0:FT * CAP].rearrange("p (f s) -> p f s", s=CAP)
        h_job = work[:, 3, 0:KD * CAP].rearrange("p (k s) -> p k s", s=CAP)
        y_job = work[:, 4, 0:KD * CAP].rearrange("p (k s) -> p k s", s=CAP)
        y_tok = work[0:CAP, 5, :]
        silu_job = work[:, 6, 0:3 * CAP].rearrange("p (r s) -> p r s", s=CAP)
        put = work[0:CAP, 7, 0:T]
        put_2 = work[0:CAP, 7, T:2 * T]
        take = work[:, 8, 0:3 * CAP].rearrange("p (m s) -> p m s", m=3)
        rows4 = c[:, :, :]
        sq = gs[:, 0:KD, :]

        def glu_gate(j):
            return work[:, 7, (j % 2) * T:(j % 2 + 1) * T]

        def norm4(w):
            return work[:, w:w + 2, :].rearrange("p a b -> p (a b)")[:, 0:H * T].rearrange("p (h t) -> p h t", t=T)

        vmask = work[:, 0:4, :].rearrange("p a (u d) -> p (a u) d", d=P)

        at = {}
        pos = 0
        for name, n in PARAMS:
            at[name] = pos
            pos += n

        def par(name, i, n=1):
            return prm[:, at[name] + i:at[name] + i + n]

        def par_block(name, l, k):
            return prm[:, at[name] + l * k:at[name] + (l + 1) * k]

        smalls = {}
        spos = [0]

        def sm(name, n):
            smalls[name] = (spos[0], n)
            spos[0] += n
            return small[:, spos[0] - n:spos[0]]

        t_a = sm("t_a", 12)
        t_abs = sm("t_abs", 12)
        t_exp = sm("t_exp", 12)
        t_ln = sm("t_ln", 12)
        g_tok = sm("g_tok", 12)
        b_exp = sm("b_exp", 12)
        beta = sm("beta", 12)
        nea = sm("nea", 4)
        ab_tok = sm("ab_tok", 24)
        tables = sm("tables", 96)
        gcc = tables[:, 0:8]
        gl = tables[:, 8:16]
        betas = tables[:, 64:96]
        gd = sm("gd", 8)
        egc = sm("egc", 8)
        egl = sm("egl", 8)
        kdsc = sm("kdsc", 8)
        nbeg = sm("nbeg", 8)
        samp_rhs = sm("samp_rhs", 64)
        egs = sm("egs", 32)
        vn_s = sm("vn_s", 32)
        k_s = sm("k_s", 32)
        qk_s = sm("qk_s", 32)
        o_t = sm("o_t", 32)
        s_prod = sm("s_prod", 32)
        rl = sm("rl", 24)
        assert spos[0] <= 576
        rstd = sb("rstd", [T])
        rows32 = sb("rows32", [2, P])
        rt = sb("rt", [12, 24])
        scan = sb("scan", [4, 2 * NE])
        slot_no = sb("slot_no", [1])
        jobs = ctx.enter_context(nc.sbuf_tensor("jobs", [P, MAX_JOBS + 1], mybir.dt.int32))

        slot_loaded = [sem(f"slot_loaded{i}") for i in range(RING)]
        units_used = sem("units_used")
        x_loaded = sem("x_loaded")
        consts_loaded = sem("consts_loaded")
        states_loaded = sem("states_loaded")
        dw_loaded = sem("dw_loaded")
        zeros_set = sem("zeros_set")
        squares_done = sem("squares_done")
        sums_done = sem("sums_done")
        h_done = sem("h_done")
        glu_sig = sem("glu_sig")
        glu_done = sem("glu_done")
        conv_out = sem("conv_out")
        act_evac = sem("act_evac")
        ab_done = sem("ab_done")
        soft_in = sem("soft_in")
        soft_exp = sem("soft_exp")
        g_done = sem("g_done")
        g_rows = sem("g_rows")
        l_args = sem("l_args")
        exp_small = sem("exp_small")
        exp_big = sem("exp_big")
        pool_l = sem("pool_l")
        qconv_done = sem("qconv_done")
        qkv_silu = sem("qkv_silu")
        qk_squares = sem("qk_squares")
        qk_sums = sem("qk_sums")
        rms_done = sem("rms_done")
        qk_rms = sem("qk_rms")
        o_rms = sem("o_rms")
        ln_rms = sem("ln_rms")
        qk_normed = sem("qk_normed")
        gram_done = sem("gram_done")
        gram_taken = sem("gram_taken")
        level_masked = sem("level_masked")
        first_tr = sem("first_tr")
        tu_done = sem("tu_done")
        b_mm = sem("b_mm")
        b_taken = sem("b_taken")
        pq_mm = sem("pq_mm")
        kv_tr = sem("kv_tr")
        kv_taken = sem("kv_taken")
        w_mm = sem("w_mm")
        w_taken = sem("w_taken")
        vn_mm = sem("vn_mm")
        vn_taken = sem("vn_taken")
        os_mm = sem("os_mm")
        os_taken = sem("os_taken")
        samp_mm = sem("samp_mm")
        samp_vn = sem("samp_vn")
        samp_tr = sem("samp_tr")
        samp_rows = sem("samp_rows")
        samp_vm = sem("samp_vm")
        s0_scaled = sem("s0_scaled")
        outer_mm = sem("outer_mm")
        outer_taken = sem("outer_taken")
        o_squares = sem("o_squares")
        o_sums = sem("o_sums")
        o_done = sem("o_done")
        ln_sum = sem("ln_sum")
        ln_cen = sem("ln_cen")
        ln_sq = sem("ln_sq")
        ln_var = sem("ln_var")
        ln_norm = sem("ln_norm")
        c_done = sem("c_done")
        merged_done = sem("merged_done")
        x_done = sem("x_done")
        silu_done = sem("silu_done")
        act_done = sem("act_done")
        down_done = sem("down_done")
        down_taken = sem("down_taken")
        router_mm = sem("router_mm")
        gates_exp_in = sem("gates_exp_in")
        gates_exp = sem("gates_exp")
        h_tr = sem("h_tr")
        h_tok_done = sem("h_tok_done")
        chosen = sem("chosen")
        ranks_mm = sem("ranks_mm")
        jobs_done = sem("jobs_done")
        take_done = sem("take_done")
        rows_rhs = sem("rows_rhs")
        rows_mm = sem("rows_mm")
        rows_done = sem("rows_done")
        gather_mm = sem("gather_mm")
        h_job_done = sem("h_job_done")
        y_taken = sem("y_taken")
        y_tr = sem("y_tr")
        y_tok_done = sem("y_tok_done")
        put_done = sem("put_done")
        scatter_mm = sem("scatter_mm")
        put_step = sem("put_step")
        s0_loaded = sem("s0_loaded")
        y_done = sem("y_done")
        state_out = sem("state_out")
        final_out = sem("final_out")
        dve_step = sem("dve_step")
        act_step = sem("act_step")
        pool_step = sem("pool_step")

        ordinal = {}
        n = 0
        for section, count in (("mix0", N_LAYER), ("ffn", N_FFN), ("mix1", N_LAYER)):
            for i in range(count):
                ordinal[first_position(section) + i] = n
                n += 1
        base_ord = {"mix0": 0, "ffn": N_LAYER, "mix1": N_LAYER + N_FFN, "experts": 2 * N_LAYER + N_FFN}

        def uses_before(position):
            return sum(1 for p in ordinal if p < position and p % RING == position % RING)

        block = ctx.enter_context(nc.Block())

        @block.sync
        def _(sp):
            def load_static(section, i, src):
                p = first_position(section) + i
                before = [q for q in ordinal if q < p and q % RING == p % RING]
                if before:
                    sp.wait_ge(units_used, ordinal[max(before)] + 1)
                sp.dma_start(ring[:, p % RING, :, :].rearrange("p k n -> p (k n)"), src).then_inc(slot_loaded[p % RING], 16)

            def load_rest(section, revolutions, src, base):
                with sp.Fori(1, revolutions) as r:
                    for s in range(RING):
                        sp.wait_ge(units_used, r * RING + (base + s + 1 - RING))
                        sp.dma_start(ring[:, s, :, :].rearrange("p k n -> p (k n)"),
                                     src[bass.ds(r * RING + s, 1), :, :].rearrange("a p n -> p (a n)")
                                     ).then_inc(slot_loaded[s], 16)

            for i in range(N_LAYER):
                load_static("mix0", i, a["w_mixer"][0, i])
            for i in range(RING):
                load_static("ffn", i, a["w_ffn"][i])
            load_rest("ffn", N_FFN // RING, a["w_ffn"], base_ord["ffn"])
            for i in range(N_LAYER):
                load_static("mix1", i, a["w_mixer"][1, i])
            for i in range(RING):
                load_static("experts", i, a["w_exp"][i])

            def load_expert(expert, job, first_revolution):
                with sp.Fori(first_revolution, N_FFN // RING) as r:
                    for s in range(RING):
                        sp.wait_ge(units_used, job * N_FFN + r * RING + (base_ord["experts"] + s + 1 - RING))
                        sp.dma_start(ring[:, s, :, :].rearrange("p k n -> p (k n)"),
                                     a["w_exp"][bass.ds(expert * N_FFN + r * RING + s, 1), :, :].rearrange("a p n -> p (a n)")
                                     ).then_inc(slot_loaded[s], 16)

            load_expert(0, 0, 1)
            sp.wait_ge(jobs_done, 1)
            n_jobs = sp.value_load(jobs[0:1, MAX_JOBS:MAX_JOBS + 1], min_val=2, max_val=MAX_JOBS)
            with sp.Fori(1, n_jobs) as job:
                expert = sp.value_load(jobs[0:1, bass.ds(job, 1)], min_val=0, max_val=NE - 1)
                load_expert(expert, job, 0)

        @block.gpsimd
        def _(pool):
            pool_n = [0]

            def settle(ins):
                pool_n[0] += 1
                ins.then_inc(pool_step, 1)
                pool.wait_ge(pool_step, pool_n[0])

            pool.dma_start(xT[:, :, :].rearrange("p k t -> p (k t)"), a["xT"]).then_inc(x_loaded, 16)
            pool.dma_start(prm[:, :], a["params"]).then_inc(consts_loaded, 16)
            pool.dma_start(consts[:, :, :].rearrange("p k t -> p (k t)"), a["consts"]).then_inc(consts_loaded, 16)
            pool.dma_start(level_masks[:, :, :].rearrange("p k t -> p (k t)"), a["level_masks"]).then_inc(consts_loaded, 16)
            for l in range(DEPTH):
                if l:
                    pool.wait_ge(merged_done, KD * l)
                    pool.wait_ge(state_out, 16 * 6 * l)
                    pool.wait_ge(down_taken, KD * l)
                nc.gpsimd.memset(u_pad[:, :, 0:DW - 1], 0.0).then_inc(zeros_set, 1)
                nc.gpsimd.memset(q_pad[:, :, 0:QW - 1], 0.0).then_inc(zeros_set, 1)
                pool.dma_start(early[:, n_pad:n_pad + CT * NB * DW], a["dw_win"][l]).then_inc(dw_loaded, 16)
                pool.dma_start(q_win.rearrange("p t b n -> p (t b n)"), a["qkv_win"][l]).then_inc(states_loaded, 16)
                pool.wait_ge(exp_big, 3 * l + 2)
                nc.gpsimd.tensor_tensor(units(1), units(1), triu.rearrange("p (a i) -> p a i", a=1).broadcast_to([P, U, P]), ALU.mult)
                pool.wait_ge(exp_big, 3 * l + 3)
                pool.wait_ge(g_done, l + 1)
                nc.gpsimd.tensor_tensor(units(2), units(2), beta[:, 0:U].rearrange("p (u a) -> p u a", a=1).broadcast_to([P, U, P]),
                                        ALU.mult).then_inc(pool_l, 1)
                pool.wait_ge(glu_done, CT * (l + 1))
                pool.dma_start(o["dwp"][l], u_pad[:, :, TP:TP + DW - 1]).then_inc(state_out, 16)
                pool.dma_start(o["dws"][l], early[:, n_pad:n_pad + CT * NB * DW]).then_inc(state_out, 16)
                pool.wait_ge(act_evac, 32 * l + QT)
                pool.dma_start(o["qkp"][l], q_pad[:, :, TP:TP + QW - 1]).then_inc(state_out, 16)
                pool.dma_start(o["qks"][l], q_win.rearrange("p t b n -> p (t b n)")).then_inc(state_out, 16)
                pool.wait_ge(conv_out, CT * (l + 1))
                pool.wait_ge(state_out, 16 * (6 * l + 4))
                pool.dma_start(early[:, :], a["s0"][l]).then_inc(s0_loaded, 16)
                pool.wait_ge(consts_loaded, 48)
                pool.wait_ge(gram_taken, 2 * l + 2)
                for v in range(LEVELS):
                    if v == 2:
                        pool.wait_ge(tu_done, LEVELS * l + 1)
                    elif v > 2:
                        pool.wait_ge(b_mm, (LEVELS - 1) * l + v - 2)
                    nc.gpsimd.tensor_tensor(units(5 + v % 2), units(7),
                                            level_masks[:, v, :].rearrange("p (a i) -> p a i", a=1).broadcast_to([P, U, P]),
                                            ALU.mult).then_inc(level_masked, 1)
                pool.wait_ge(samp_mm, l + 1)
                pool.wait_ge(exp_small, 2 * l + 2)
                nc.gpsimd.tensor_tensor(s0[:, :, :], s0[:, :, :], egs.rearrange("p (u a) -> p u a", a=1).broadcast_to([P, NB * H, P]),
                                        ALU.mult).then_inc(s0_scaled, 1)
                pool.wait_ge(os_taken, 2 * l + 2)
                pool.dma_start(o["sp"][l], units(3)[:, 0:H, :].rearrange("p h d -> p (h d)")).then_inc(state_out, 16)
                pool.wait_ge(outer_taken, 8 * (l + 1))
                pool.dma_start(o["ss"][l], early[:, :]).then_inc(state_out, 16)
            pool.wait_ge(y_done, KD)
            pool.dma_start(o["yT"], hT[:, :, :].rearrange("p k t -> p (k t)")).then_inc(final_out, 16)
            pool.wait_ge(state_out, 16 * 6 * DEPTH)
            pool.wait_ge(final_out, 16)

        @block.scalar
        def _(act):
            act_n = [0]

            def settle(ins):
                act_n[0] += 1
                ins.then_inc(act_step, 1)
                act.wait_ge(act_step, act_n[0])

            A = nc.scalar.activation

            def model_squares(l2):
                for k in range(KD):
                    if k == 0:
                        act.wait_ge(x_loaded, 16)
                    if l2 % 2:
                        act.wait_ge(x_done, KD * (l2 // 2) + k + 1)
                    elif l2 == 2:
                        act.wait_ge(down_taken, k + 1)
                    A(sq[:, k, :], xT[:, k, :], ACT.Square).then_inc(squares_done, 1)

            def model_rms(l2):
                act.wait_ge(sums_done, l2 + 1)
                A(rstd[:, :], psum[:, 7, 0:T], ACT.Sqrt, scale=1.0 / D, bias=par("eps", 0)).then_inc(rms_done, 1)

            act.wait_ge(consts_loaded, 48)
            for l in range(DEPTH):
                model_squares(2 * l)
                model_rms(2 * l)
                for j in range(CT):
                    act.wait_ge(units_used, base_ord[f"mix{l}"] + 2 * j + 2)
                    if j >= 2:
                        act.wait_ge(glu_done, CT * l + j - 1)
                    A(glu_gate(j), psum[:, (2 * j + 1) % 4, 0:T], ACT.Sigmoid).then_inc(glu_sig, 1)
                act.wait_ge(soft_in, l + 1)
                A(t_exp, t_abs, ACT.Exp, scale=-1.0).then_inc(soft_exp, 1)
                act.wait_ge(soft_exp, 4 * l + 1)
                A(b_exp.rearrange("p (t n) -> p t n", t=3), ab_tok.rearrange("p (t n) -> p t n", t=3)[:, :, H:2 * H], ACT.Exp, scale=-1.0).then_inc(soft_exp, 1)
                A(nea, par_block("a_log", l, H), ACT.Exp).then_inc(soft_exp, 1)
                A(t_ln, t_exp, ACT.Ln, bias=1.0).then_inc(soft_exp, 1)

                def evac_qkv(t):
                    act.wait_ge(units_used, base_ord[f"mix{l}"] + 8 + t + 1)
                    if t == 0:
                        act.wait_ge(states_loaded, 16 * (l + 1))
                        act.wait_ge(zeros_set, 2 * l + 2)
                    b = (8 + t) % 4
                    A(q_pad[:, t, QW - 1:QW - 1 + TP], psum[:, b, 0:TP], ACT.Copy)
                    A(q_win[:, t, :, QW - 1], psum[:, b, TP:T], ACT.Copy).then_inc(act_evac, 1)

                evac_qkv(0)
                evac_qkv(1)
                act.wait_ge(l_args, l + 1)
                A(units(0), pair(6), ACT.Exp).then_inc(exp_big, 1)
                A(egc, gcc, ACT.Exp)
                A(egl, gl, ACT.Exp)
                A(egs, tables[:, 32:64], ACT.Exp).then_inc(exp_small, 1)
                A(kdsc, gd, ACT.Exp).then_inc(exp_small, 1)
                A(units(1), units(1), ACT.Exp).then_inc(exp_big, 1)
                A(units(2), units(2), ACT.Exp, scale=-1.0).then_inc(exp_big, 1)
                for t in range(2, QT):
                    evac_qkv(t)
                for t in range(H):
                    act.wait_ge(units_used, base_ord[f"mix{l}"] + 20 + t + 1)
                    A(zs[:, t, :], psum[:, (20 + t) % 4, 0:T], ACT.Silu).then_inc(act_evac, 1)
                for t in range(QT):
                    act.wait_ge(qconv_done, QT * l + t + 1)
                    A(qkv[:, t, :], qkv[:, t, :], ACT.Silu).then_inc(qkv_silu, 1)
                act.wait_ge(qkv_silu, QT * (l + 1))
                act.wait_ge(state_out, 16 * (6 * l + 4))
                for t in range(2 * H):
                    A(sq_qk[:, t, :], qkv[:, t, :], ACT.Square).then_inc(qk_squares, 1)

                for i in range(2):
                    act.wait_ge(qk_sums, 2 * H * l + (i + 1) * H)
                    if i:
                        act.wait_ge(qk_normed, 2 * l + 1)
                    A(norm4(7), psum[:, 4:8, 0:T], ACT.Sqrt, bias=par("eps", 0)).then_inc(qk_rms, 1)

                def gate(t):
                    act.wait_ge(units_used, base_ord[f"mix{l}"] + 24 + t + 1)
                    A(gs[:, t, :], psum[:, (24 + t) % 4, 0:T], ACT.Sigmoid).then_inc(act_evac, 1)

                gate(0)
                gate(1)
                gate(2)
                gate(3)
                for v in range(1, LEVELS):
                    act.wait_ge(b_mm, (LEVELS - 1) * l + v)
                    A(units(8), pair(4), ACT.Copy).then_inc(b_taken, 1)
                    gate(2 * v + 2)
                    gate(2 * v + 3)
                act.wait_ge(w_mm, l + 1)
                A(units(8), pair(4), ACT.Copy).then_inc(w_taken, 1)
                for h in range(H):
                    if h == 0:
                        act.wait_ge(os_taken, 2 * l + 2)
                        act.wait_ge(samp_vn, 2 * l + 2)
                    A(work[:, 4 + h, 0:T], qkv[:, 8 + h, :], ACT.Square).then_inc(o_squares, 1)
                act.wait_ge(o_sums, H * (l + 1))
                A(norm4(0), psum[:, 4:8, 0:T], ACT.Sqrt, scale=1.0 / P, bias=par("eps", 0)).then_inc(o_rms, 1)
                act.wait_ge(ln_cen, CT * (l + 1))
                for j in range(CT):
                    A(work[:, 4 + j, 512:512 + T], c[:, j, :], ACT.Square).then_inc(ln_sq, 1)
                act.wait_ge(ln_var, l + 1)
                A(rstd[:, :], psum[:, 1, 0:T], ACT.Sqrt, scale=1.0 / (CT * P), bias=par("eps", 0)).then_inc(ln_rms, 1)
                for j in range(CT):
                    act.wait_ge(ln_norm, CT * l + j + 1)
                    A(c[:, j, :], c[:, j, :], ACT.Silu, scale=par("ln_g", l * CT + j), bias=par("ln_b", l * CT + j)).then_inc(c_done, 1)
                act.wait_ge(merged_done, KD * (l + 1))
                model_squares(2 * l + 1)
                model_rms(2 * l + 1)
                if l == 0:
                    with act.Fori(0, 2) as half:
                        for j in range(FT // 2):
                            f = half * (FT // 2) + j
                            act.wait_ge(units_used, f * 2 + (base_ord["ffn"] + 1))
                            if j == 0:
                                act.wait_ge(act_done, f)
                            elif j >= 3:
                                act.wait_ge(act_done, f - 2)
                            A(silu_g[:, j % 3, :], psum[:, 2 * (j % 3), 0:T], ACT.Silu).then_inc(silu_done, 1)
                else:
                    for m in range(3):
                        act.wait_ge(h_tr, m + 1)
                        A(h_tok[:, m, :], psum[:, (0, 2, 6)[m]:(0, 2, 6)[m] + 2, :].rearrange("p b n -> p (b n)"), ACT.Copy).then_inc(h_tok_done, 1)
                    act.wait_ge(gates_exp_in, 1)
                    A(rt[:, 3, 0:3], rt[:, 2, 0:3], ACT.Exp).then_inc(gates_exp, 1)

                    def gathered(job):
                        act.wait_ge(gather_mm, job + 1)
                        A(work[:, 3, 0:KD * CAP].rearrange("p (b n) -> p b n", b=2), psum[:, 0:2, 0:4 * CAP], ACT.Copy).then_inc(h_job_done, 1)

                    gathered(0)
                    act.wait_ge(jobs_done, 1)
                    n_jobs = act.value_load(jobs[0:1, MAX_JOBS:MAX_JOBS + 1], min_val=2, max_val=MAX_JOBS)
                    with act.Fori(0, n_jobs) as job:
                        with act.Fori(0, 2) as half:
                            for j in range(FT // 2):
                                act.wait_ge(units_used, job * N_FFN + half * FT + (base_ord["experts"] + 2 * j + 1))
                                f = job * FT + half * (FT // 2) + j
                                if j == 0:
                                    act.wait_ge(act_done, f + FT)
                                elif j >= 3:
                                    act.wait_ge(act_done, f + (FT - 2))
                                A(silu_job[:, j % 3, :], psum[:, 2 * (j % 3), 0:CAP], ACT.Silu).then_inc(silu_done, 1)
                        for t in range(KD):
                            if t % 4 == 3:
                                act.wait_ge(units_used, job * N_FFN + (base_ord["experts"] + 2 * FT + (t + 1) * FT // KD))
                            else:
                                act.wait_ge(down_done, job * 6 + (6 + t + 1 - t // 4))
                            A(y_job[:, t, :], psum[:, 6 + t % 2, 0:CAP], ACT.Copy).then_inc(y_taken, 1)
                        gathered(job + 1)
                        act.wait_ge(y_tr, job + 1)
                        A(y_tok, psum[0:CAP, 2:4, :].rearrange("p b n -> p (b n)"), ACT.Copy).then_inc(y_tok_done, 1)
                    act.wait_ge(down_taken, n_jobs * KD + KD)
            model_squares(2 * DEPTH)
            model_rms(2 * DEPTH)

        @block.vector
        def _(dve):
            V = nc.vector
            dve_n = [0]

            def settle(ins):
                dve_n[0] += 1
                ins.then_inc(dve_step, 1)
                dve.wait_ge(dve_step, dve_n[0])

            def model_norm(l2, g_name, g_at, out, done):
                dve.wait_ge(rms_done, l2 + 1)
                settle(V.reciprocal(rstd[:, :], rstd[:, :]))
                for k in range(KD):
                    V.scalar_tensor_tensor(out[:, k, :], xT[:, k, :], par(g_name, g_at + k), rstd[:, :], ALU.mult, ALU.mult).then_inc(done, 1)

            dve.wait_ge(consts_loaded, 48)
            dve.wait_ge(x_loaded, 16)
            for l in range(DEPTH):
                model_norm(2 * l, "norm1", l * KD, hT, h_done)
                for j in range(CT):
                    dve.wait_ge(glu_sig, CT * l + j + 1)
                    if j == 0:
                        dve.wait_ge(dw_loaded, 16 * (l + 1))
                        dve.wait_ge(zeros_set, 2 * l + 1)
                    sg = glu_gate(j)
                    V.tensor_tensor(u_pad[:, j, DW - 1:], psum[:, (2 * j) % 4, 0:TP], sg[:, 0:TP], ALU.mult)
                    V.tensor_tensor(u_win[:, j, :, DW - 1], psum[:, (2 * j) % 4, TP:T], sg[:, TP:T], ALU.mult).then_inc(glu_done, 1)
                dve.wait_ge(ab_done, l + 1)
                settle(V.tensor_copy(ab_tok, psum[:, 4, 0:24]))
                ab = ab_tok.rearrange("p (t n) -> p t n", t=3)
                settle(V.tensor_tensor(t_a.rearrange("p (t n) -> p t n", t=3), ab[:, :, 0:H],
                                       par_block("dt_bias", l, H).rearrange("p (a n) -> p a n", a=1).broadcast_to([P, 3, H]), ALU.add))
                V.scalar_tensor_tensor(t_abs, t_a, -1.0, t_a, ALU.mult, ALU.max).then_inc(soft_in, 1)
                dve.wait_ge(soft_exp, 4 * (l + 1))
                settle(V.scalar_tensor_tensor(g_tok, t_a, 0.0, t_ln, ALU.max, ALU.add))
                settle(V.scalar_tensor_tensor(g_tok.rearrange("p (t n) -> p t n", t=3), g_tok.rearrange("p (t n) -> p t n", t=3), -1.0,
                                              nea.rearrange("p (a n) -> p a n", a=1).broadcast_to([P, 3, H]), ALU.mult, ALU.mult))
                settle(V.tensor_scalar(b_exp, b_exp, 1.0, None, ALU.add))
                settle(V.reciprocal(beta, b_exp))
                smask = par("samp_mask", 0, NB)
                for i, col in enumerate((g_tok, beta)):
                    V.tensor_tensor(samp_rhs[:, i * 32:(i + 1) * 32].rearrange("p (b h) -> p b h", h=H),
                                    smask.rearrange("p (b a) -> p b a", a=1).broadcast_to([P, NB, H]),
                                    col[:, 8:12].rearrange("p (a h) -> p a h", a=1).broadcast_to([P, NB, H]), ALU.mult)
                V.tensor_tensor(units(0), triu.rearrange("p (a i) -> p a i", a=1).broadcast_to([P, U, P]),
                                g_tok[:, 0:U].rearrange("p (u a) -> p u a", a=1).broadcast_to([P, U, P]), ALU.mult).then_inc(g_done, 1)
                dve.wait_ge(g_rows, l + 1)
                V.tensor_copy(tables[:, 32:96], psum[:, 4, 64:128])
                settle(V.tensor_copy(tables[:, 0:16], psum[:, 4, 32:48]))
                V.tensor_tensor(gd, gl, gcc, ALU.subtract)
                settle(V.tensor_tensor(units(1), pair(6), gcc.rearrange("p (u a) -> p u a", a=1).broadcast_to([P, U, P]), ALU.subtract))
                settle(V.tensor_scalar(work[:, 2, :], work[:, 1, :], 0.0, None, ALU.max))
                V.tensor_scalar(work[:, 1, :], work[:, 1, :], 0.0, None, ALU.min).then_inc(l_args, 1)
                dve.wait_ge(exp_small, 2 * l + 2)
                settle(V.scalar_tensor_tensor(nbeg, beta[:, 0:U], -1.0, egc, ALU.mult, ALU.mult))
                dve.wait_ge(glu_done, CT * (l + 1))
                for tap in range(DW):
                    for j in range(CT):
                        w = par("dw_w", (l * CT + j) * DW + tap)
                        if tap == 0:
                            ins = V.tensor_scalar(c[:, j, 0:TP], u_pad[:, j, 0:TP], w, par("dw_b", l * CT + j), ALU.mult, ALU.add)
                        else:
                            ins = V.scalar_tensor_tensor(c[:, j, 0:TP], u_pad[:, j, tap:tap + TP], w, c[:, j, 0:TP], ALU.mult, ALU.add)
                    settle(ins)
                prod = work[:, 8, 0:CT * NB * DW].rearrange("p (c b n) -> p c b n", c=CT, b=NB)
                for j in range(CT):
                    ins = V.tensor_tensor(prod[:, j], u_win[:, j], par("dw_w", (l * CT + j) * DW, DW).rearrange("p (a n) -> p a n", a=1).broadcast_to([P, NB, DW]), ALU.mult)
                settle(ins)
                for j in range(CT):
                    ins = V.tensor_reduce(c[:, j, TP:T], prod[:, j], AX_X, ALU.add)
                settle(ins)
                for j in range(CT):
                    V.tensor_scalar(c[:, j, TP:T], c[:, j, TP:T], par("dw_b", l * CT + j), None, ALU.add).then_inc(conv_out, 1)
                for t0 in range(0, QT, 4):
                    for tap in range(QW):
                        for t in range(t0, t0 + 4):
                            if tap == 0:
                                dve.wait_ge(act_evac, 32 * l + t + 1)
                            w = par("qk_w", (l * QT + t) * QW + tap)
                            if tap == 0:
                                ins = V.tensor_scalar(qkv[:, t, 0:TP], q_pad[:, t, 0:TP], w, None, ALU.mult)
                            else:
                                ins = V.scalar_tensor_tensor(qkv[:, t, 0:TP], q_pad[:, t, tap:tap + TP], w, qkv[:, t, 0:TP], ALU.mult, ALU.add)
                        settle(ins)
                    for t in range(t0, t0 + 4):
                        qprod = work[:, 8, 32 * t:32 * (t + 1)].rearrange("p (b n) -> p b n", b=NB)
                        ins = V.tensor_tensor(qprod, q_win[:, t], par("qk_w", (l * QT + t) * QW, QW).rearrange("p (a n) -> p a n", a=1).broadcast_to([P, NB, QW]), ALU.mult)
                    settle(ins)
                    for t in range(t0, t0 + 4):
                        qprod = work[:, 8, 32 * t:32 * (t + 1)].rearrange("p (b n) -> p b n", b=NB)
                        V.tensor_reduce(qkv[:, t, TP:T], qprod, AX_X, ALU.add).then_inc(qconv_done, 1)
                for i in range(2):
                    dve.wait_ge(qk_rms, 2 * l + i + 1)
                    settle(V.reciprocal(norm4(7), norm4(7)))
                    group = qkv[:, i * H:(i + 1) * H, :]
                    V.scalar_tensor_tensor(group, group, float(P) ** -0.5 if i == 0 else 1.0, norm4(7), ALU.mult, ALU.mult).then_inc(qk_normed, 1)
                dve.wait_ge(qk_normed, 2 * l + 2)
                dve.wait_ge(pool_l, l + 1)
                dve.wait_ge(gram_done, 2 * l + 1)
                V.tensor_tensor(units(7), pair(4), units(2), ALU.mult).then_inc(gram_taken, 1)
                dve.wait_ge(gram_done, 2 * l + 2)
                V.tensor_tensor(units(1), pair(6), units(1), ALU.mult).then_inc(gram_taken, 1)
                q4 = qkv[:, 0:H, 0:TP].rearrange("p h (c i) -> p c h i", c=NC)
                w04 = work[:, 0, :].rearrange("p (c h i) -> p c h i", c=NC, h=H)
                for cc in range(NC):
                    settle(V.tensor_tensor(w04[:, cc], w04[:, cc], q4[:, cc], ALU.mult))
                ib = ident.rearrange("p (a i) -> p a i", a=1).broadcast_to([P, U, P])
                dve.wait_ge(level_masked, LEVELS * l + 1)
                V.tensor_tensor(units(3), ib, units(5), ALU.subtract)
                dve.wait_ge(first_tr, l + 1)
                V.tensor_tensor(units(4), ib, pair(4), ALU.subtract).then_inc(tu_done, 1)
                for v in range(1, LEVELS):
                    n_pq = (2 * (LEVELS - 1) - 1) * l + 2 * (v - 1)
                    dve.wait_ge(pq_mm, n_pq + 1)
                    u_ins = V.tensor_tensor(units(4), units(4), pair(6), ALU.subtract)
                    if v < LEVELS - 1:
                        dve.wait_ge(pq_mm, n_pq + 2)
                        u_ins = V.tensor_tensor(units(3), units(3), pair(4), ALU.subtract)
                    u_ins.then_inc(tu_done, 1)
                bc = lambda col: col.rearrange("p (u a) -> p u a", a=1).broadcast_to([P, U, P])
                dve.wait_ge(kv_tr, l + 1)
                V.tensor_tensor(units(5), pair(4), bc(nbeg), ALU.mult)
                V.tensor_tensor(units(7), pair(4), bc(kdsc), ALU.mult)
                V.tensor_tensor(units(6), pair(6), bc(beta[:, 0:U]), ALU.mult).then_inc(kv_taken, 1)
                q_s = qkv[:, 0:H, TP:T].rearrange("p h b -> p b h")
                kk = qkv[:, H:2 * H, TP:T].rearrange("p h b -> p b h")
                vv = qkv[:, 2 * H:3 * H, TP:T].rearrange("p h b -> p b h")

                def bh(t):
                    return t.rearrange("p (b h) -> p b h", h=H)

                V.tensor_copy(bh(k_s), kk)
                V.tensor_tensor(bh(s_prod), q_s, kk, ALU.mult).then_inc(samp_vn, 1)
                for cc in range(NC):
                    dve.wait_ge(vn_mm, NC * l + cc + 1)
                    V.tensor_copy(work[:, 2, cc * 512:cc * 512 + 512], psum[:, 6, :]).then_inc(vn_taken, 1)
                    dve.wait_ge(os_mm, 2 * NC * l + 2 * cc + 1)
                    V.tensor_copy(qkv[:, 8:12, cc * P:(cc + 1) * P], psum[:, 4, :].rearrange("p (h i) -> p h i", h=H))
                    dve.wait_ge(os_mm, 2 * NC * l + 2 * cc + 2)
                    if cc == 0:
                        V.tensor_copy(work[:, 3, 0:512], psum[:, 5, :]).then_inc(os_taken, 1)
                    else:
                        for h in range(H):
                            ins = V.scalar_tensor_tensor(units(3)[:, h, :], units(3)[:, h, :], egl[:, cc * H + h:cc * H + h + 1],
                                                         psum[:, 5, h * P:(h + 1) * P], ALU.mult, ALU.add)
                        ins.then_inc(os_taken, 1)
                dve.wait_ge(samp_mm, l + 1)
                sk = psum[:, 7, 0:64].rearrange("p (u n) -> p u n", n=2)
                settle(V.tensor_tensor(vn_s, sk[:, :, 1], egs, ALU.mult))
                settle(V.tensor_tensor(bh(vn_s), vv, bh(vn_s), ALU.subtract))
                settle(V.tensor_tensor(vn_s, vn_s, betas, ALU.mult))
                V.tensor_tensor(o_t, sk[:, :, 0], egs, ALU.mult)
                settle(V.tensor_tensor(qk_s, psum[:, 7, 64:96], vn_s, ALU.mult))
                V.tensor_tensor(vv, bh(o_t), bh(qk_s), ALU.add).then_inc(samp_vn, 1)
                dve.wait_ge(samp_tr, l + 1)
                settle(V.tensor_copy(rows32[0:32, 0, :], psum[0:32, 7, 128:256]))
                V.tensor_copy(rows32[0:32, 1, :], psum[0:32, 7, 256:384]).then_inc(samp_rows, 1)
                dve.wait_ge(state_out, 16 * (6 * l + 5))
                V.tensor_tensor(vmask[0:32], rows32[0:32, 0, :].rearrange("p (a d) -> p a d", a=1).broadcast_to([32, 32, P]),
                                ident[0:32, 0:32].rearrange("p (u a) -> p u a", a=1).broadcast_to([32, 32, P]), ALU.mult).then_inc(samp_vm, 1)
                dve.wait_ge(s0_scaled, l + 1)
                for g in range(8):
                    dve.wait_ge(outer_mm, 8 * l + g + 1)
                    blk = s0[:, 4 * g:4 * g + 4, :].rearrange("p u d -> p (u d)")
                    V.tensor_tensor(blk, blk, psum[:, 4 + g % 2, :], ALU.add).then_inc(outer_taken, 1)
                dve.wait_ge(o_rms, l + 1)
                settle(V.reciprocal(norm4(0), norm4(0)))
                o_all = qkv[:, 2 * H:3 * H, :]
                settle(V.scalar_tensor_tensor(o_all, o_all, par("o_g", l), norm4(0), ALU.mult, ALU.mult))
                V.tensor_tensor(o_all, o_all, zs[:, :, :], ALU.mult).then_inc(o_done, 1)
                dve.wait_ge(ln_sum, l + 1)
                for j in range(CT):
                    V.scalar_tensor_tensor(c[:, j, :], psum[:, 0, 0:T], -1.0 / (CT * P), c[:, j, :], ALU.mult, ALU.add).then_inc(ln_cen, 1)
                dve.wait_ge(ln_rms, l + 1)
                settle(V.reciprocal(rstd[:, :], rstd[:, :]))
                for j in range(CT):
                    V.tensor_tensor(c[:, j, :], c[:, j, :], rstd[:, :], ALU.mult).then_inc(ln_norm, 1)
                for t in range(KD):
                    dve.wait_ge(units_used, base_ord[f"mix{l}"] + N_PROJ + t + 1)
                    settle(V.tensor_tensor(gs[:, t, :], gs[:, t, :], psum[:, 2 * (t % 2), 0:T], ALU.mult))
                    settle(V.tensor_tensor(gs[:, KD + t, :], gs[:, KD + t, :], psum[:, 2 * (t % 2) + 1, 0:T], ALU.mult))
                    V.tensor_tensor(hT[:, t, :], gs[:, t, :], gs[:, KD + t, :], ALU.add).then_inc(merged_done, 1)
                for t in range(KD):
                    dve.wait_ge(units_used, base_ord[f"mix{l}"] + N_PROJ + N_MIX + t + 1)
                    V.tensor_tensor(xT[:, t, :], xT[:, t, :], psum[:, t % 4, 0:T], ALU.add).then_inc(x_done, 1)
                dve.wait_ge(x_done, KD * (l + 1))
                model_norm(2 * l + 1, "norm2", l * KD, hT, h_done)
                if l == 0:
                    with dve.Fori(0, 2) as half:
                        for j in range(FT // 2):
                            f = half * (FT // 2) + j
                            dve.wait_ge(silu_done, f + 1)
                            dve.wait_ge(units_used, f * 2 + (base_ord["ffn"] + 2))
                            V.tensor_tensor(act_all[:, bass.ds(f, 1), :].rearrange("p a t -> p (a t)"), silu_g[:, j % 3, :],
                                            psum[:, 2 * (j % 3) + 1, 0:T], ALU.mult).then_inc(act_done, 1)
                    for t in range(KD):
                        if t % 4 == 3:
                            dve.wait_ge(units_used, base_ord["ffn"] + 2 * FT + (t + 1) * FT // KD)
                        else:
                            dve.wait_ge(down_done, t + 1 - t // 4)
                        if t >= 1:
                            dve.wait_ge(down_taken, t)
                        V.tensor_tensor(xT[:, t, :], xT[:, t, :], psum[:, 6 + t % 2, 0:T], ALU.add).then_inc(down_taken, 1)
                    dve.wait_ge(down_taken, KD)
                else:
                    dve.wait_ge(router_mm, 1)
                    lg = psum[:, 4, 0:24]
                    r3 = lambda t: t.rearrange("p (t e) -> p t e", e=NE)
                    c3 = lambda t: t.rearrange("p (t a) -> p t a", a=1).broadcast_to([P, 3, NE])
                    iota = par("iota", 0, 24)
                    logit, oh1, oh2, tmp, sent, rank = rl, rt[:, 5, :], rt[:, 6, :], rt[:, 7, :], rt[:, 8, :], rt[:, 9, :]
                    settle(V.tensor_copy(logit, lg))
                    settle(V.tensor_reduce(rt[:, 0, 0:3], r3(logit), AX_X, ALU.max))

                    def first_of(value, onehot):
                        settle(V.tensor_tensor(r3(tmp), r3(logit), c3(value), ALU.is_lt))
                        settle(V.scalar_tensor_tensor(tmp, tmp, 64.0, iota, ALU.mult, ALU.add))
                        settle(V.tensor_reduce(rt[:, 4, 0:3], r3(tmp), AX_X, ALU.min))
                        settle(V.tensor_tensor(r3(onehot), r3(iota), c3(rt[:, 4, 0:3]), ALU.is_equal))

                    first_of(rt[:, 0, 0:3], oh1)
                    settle(V.scalar_tensor_tensor(logit, oh1, -3.0e38, logit, ALU.mult, ALU.add))
                    settle(V.tensor_reduce(rt[:, 1, 0:3], r3(logit), AX_X, ALU.max))
                    first_of(rt[:, 1, 0:3], oh2)
                    V.tensor_tensor(rt[:, 2, 0:3], rt[:, 1, 0:3], rt[:, 0, 0:3], ALU.subtract).then_inc(gates_exp_in, 1)
                    settle(V.tensor_tensor(sent, oh1, oh2, ALU.add))
                    V.tensor_tensor(sent, sent, par("keep", 0, 24), ALU.mult).then_inc(chosen, 1)
                    slots, gates = rt[:, 10, 0:6], rt[:, 10, 6:12]
                    dve.wait_ge(gates_exp, 1)
                    settle(V.tensor_scalar(rt[:, 0, 0:3], rt[:, 3, 0:3], 1.0, None, ALU.add))
                    settle(V.reciprocal(gates[:, 0:3], rt[:, 0, 0:3]))
                    V.tensor_tensor(gates[:, 3:6], rt[:, 3, 0:3], gates[:, 0:3], ALU.mult)
                    settle(V.memset(scan[:, :, :], 0.0))
                    dve.wait_ge(ranks_mm, 1)
                    count = rt[:, 0, 8:16]
                    n_of, s1, s2, s3 = (scan[:, i, NE:2 * NE] for i in range(4))
                    V.tensor_copy(rank, psum[:, 5, 0:24])
                    settle(V.tensor_copy(count, psum[:, 5, 24:32]))
                    settle(V.tensor_scalar(n_of, count, 0.0, None, ALU.is_gt))
                    settle(V.memset(scan[:, 0, NE:NE + 1], 1.0))
                    for full in range(1, -(-T // CAP)):
                        settle(V.scalar_tensor_tensor(n_of, count, float(full * CAP), n_of, ALU.is_gt, ALU.add))
                    for i, step in enumerate((1, 2, 4)):
                        settle(V.tensor_tensor(scan[:, i + 1, NE:2 * NE], scan[:, i, NE:2 * NE], scan[:, i, NE - step:2 * NE - step], ALU.add))
                    ends = rt[:, 0:5, :].rearrange("p a b -> p (a b)")[:, 0:MAX_JOBS * NE].rearrange("p (j e) -> p j e", e=NE)
                    settle(V.tensor_tensor(s1, s3, n_of, ALU.subtract))
                    settle(V.scalar_tensor_tensor(r3(rank), s1.rearrange("p (a e) -> p a e", a=1).broadcast_to([P, 3, NE]), float(CAP), r3(rank), ALU.mult, ALU.add))
                    for i, oh in enumerate((oh1, oh2)):
                        settle(V.tensor_tensor(tmp, oh, rank, ALU.mult))
                        settle(V.tensor_reduce(slots[:, 3 * i:3 * i + 3], r3(tmp), AX_X, ALU.add))
                    settle(V.tensor_tensor(slots, slots, par("drop", 0, 6), ALU.add))

                    for m in range(3):
                        ins = V.tensor_scalar(take[:, m, :], par("slot_row", 0, CAP), slots[:, m:m + 1], None, ALU.is_equal)
                    settle(ins)
                    for m in range(3):
                        ins = V.scalar_tensor_tensor(take[:, m, :], par("slot_row", 0, CAP), slots[:, 3 + m:4 + m], take[:, m, :],
                                                     ALU.is_equal, ALU.add)
                    ins.then_inc(take_done, 1)
                    settle(V.tensor_tensor(ends, s3.rearrange("p (a e) -> p a e", a=1).broadcast_to([P, MAX_JOBS, NE]),
                                           par("job_no", 0, MAX_JOBS * NE).rearrange("p (j e) -> p j e", e=NE), ALU.is_le))
                    settle(V.tensor_reduce(scan[:, 0:2, :].rearrange("p a b -> p (a b)")[:, 0:MAX_JOBS], ends, AX_X, ALU.add))
                    V.tensor_copy(jobs[:, MAX_JOBS:MAX_JOBS + 1], scan[:, 3, 2 * NE - 1:2 * NE])
                    V.tensor_copy(jobs[:, 0:MAX_JOBS], scan[:, 0:2, :].rearrange("p a b -> p (a b)")[:, 0:MAX_JOBS]).then_inc(jobs_done, 1)
                    rows_in = work[:, 0:2, :].rearrange("p a b -> p (a b)")[:, 0:12 * P].rearrange("p (v i) -> p v i", i=P)
                    V.tensor_tensor(rows_in, ident.rearrange("p (a i) -> p a i", a=1).broadcast_to([P, 12, P]),
                                    rt[:, 10, 0:12].rearrange("p (v a) -> p v a", a=1).broadcast_to([P, 12, P]), ALU.mult).then_inc(rows_rhs, 1)
                    V.tensor_copy(slot_no[:, :], par("slot_col", 0))
                    dve.wait_ge(rows_mm, 1)
                    for v in range(4):
                        row = psum[:, 2:5, :].rearrange("p b n -> p (b n)")[:, v * 3 * P:(v + 1) * 3 * P]
                        V.tensor_copy(rows4[:, v, 0:TP], row[:, 0:TP])
                        ins = V.tensor_copy(rows4[:, v, TP:T], row[:, 2 * P + SAMPLE_ROW:3 * P])
                    ins.then_inc(rows_done, 1)
                    dve.wait_ge(rows_done, 1)
                    dve.wait_ge(jobs_done, 1)
                    n_jobs = dve.value_load(jobs[0:1, MAX_JOBS:MAX_JOBS + 1], min_val=2, max_val=MAX_JOBS)
                    with dve.Fori(0, n_jobs) as job:
                        with dve.Fori(0, 2) as half:
                            for j in range(FT // 2):
                                f = half * (FT // 2) + j
                                dve.wait_ge(silu_done, job * FT + f + (FT + 1))
                                dve.wait_ge(units_used, job * N_FFN + half * FT + (base_ord["experts"] + 2 * j + 2))
                                V.tensor_tensor(act_job[:, bass.ds(f, 1), :].rearrange("p a t -> p (a t)"), silu_job[:, j % 3, :],
                                                psum[:, 2 * (j % 3) + 1, 0:CAP], ALU.mult).then_inc(act_done, 1)
                        slot_c = slot_no[0:CAP, :]
                        V.scalar_tensor_tensor(put, rows4[0:CAP, 0, :], slot_c, rows4[0:CAP, 2, :], ALU.is_equal, ALU.mult)
                        V.scalar_tensor_tensor(put_2, rows4[0:CAP, 1, :], slot_c, rows4[0:CAP, 3, :], ALU.is_equal, ALU.mult).then_inc(put_step, 1)
                        dve.wait_ge(put_step, job * 4 + 1)
                        V.tensor_tensor(put, put, put_2, ALU.add).then_inc(put_done, 1)
                        V.tensor_scalar(slot_no[:, :], slot_no[:, :], float(CAP), None, ALU.add).then_inc(put_step, 1)
                        dve.wait_ge(put_step, job * 4 + 2)
                        V.tensor_scalar(slots, slots, float(-CAP), None, ALU.add).then_inc(put_step, 1)
                        dve.wait_ge(put_step, job * 4 + 3)
                        for m in range(3):
                            ins = V.tensor_scalar(take[:, m, :], par("slot_row", 0, CAP), slots[:, m:m + 1], None, ALU.is_equal)
                        ins.then_inc(put_step, 1)
                        dve.wait_ge(put_step, job * 4 + 4)
                        for m in range(3):
                            ins = V.scalar_tensor_tensor(take[:, m, :], par("slot_row", 0, CAP), slots[:, 3 + m:4 + m], take[:, m, :],
                                                         ALU.is_equal, ALU.add)
                        ins.then_inc(take_done, 1)
                        for t in range(KD):
                            dve.wait_ge(scatter_mm, job * KD + (t + 1))
                            V.tensor_tensor(xT[:, t, :], xT[:, t, :], psum[:, 4 + t % 2, 0:T], ALU.add).then_inc(down_taken, 1)
                    dve.wait_ge(down_taken, n_jobs * KD + KD)
            model_norm(2 * DEPTH, "final", 0, hT, y_done)

        @block.tensor
        def _(pe):
            M = nc.tensor.matmul

            def arrived(section, i):
                p = first_position(section) + i
                pe.wait_ge(slot_loaded[p % RING], 16 * (uses_before(p) + 1))
                return ring[:, p % RING, :, :]

            def model_sums(l2):
                for k in range(KD):
                    pe.wait_ge(squares_done, KD * l2 + k + 1)
                    last = M(psum[:, 7, 0:T], ones, sq[:, k, :], start=(k == 0), stop=(k == KD - 1))
                last.then_inc(sums_done, 1)

            pe.wait_ge(consts_loaded, 48)
            for l in range(DEPTH):
                section = f"mix{l}"
                if l:
                    pe.wait_ge(down_taken, KD)
                model_sums(2 * l)

                def project(t):
                    w = arrived(section, t)
                    if t == 0:
                        pe.wait_ge(h_done, 2 * KD * l + KD)
                    elif 4 <= t < 12:
                        pe.wait_ge(glu_done, CT * l + (t - 4) // 2 + 1)
                    elif t >= 12:
                        pe.wait_ge(act_evac, 32 * l + t - 4 - 8 + 1)
                    for k in range(KD):
                        last = M(psum[:, t % 4, 0:T], w[:, k, :], hT[:, k, :], start=(k == 0), stop=(k == KD - 1))
                    last.then_inc(units_used, 1)

                for t in range(8):
                    project(t)
                for m, t0 in enumerate((0, P, T - P)):
                    for k in range(KD):
                        last = M(psum[:, 4, m * 8:m * 8 + 8], hT[:, k, t0:t0 + P], par_block("w_ab", l, KD * 8)[:, k * 8:(k + 1) * 8],
                                 start=(k == 0), stop=(k == KD - 1))
                last.then_inc(ab_done, 1)
                project(8)
                project(9)
                pe.wait_ge(g_done, l + 1)
                for b in range(2):
                    M(psum[:, 6 + b, :], ones, work[:, 0, b * 512:b * 512 + 512], start=True, stop=True)
                M(psum[:, 4, 32:40], triu, g_tok[:, 0:U], start=True, stop=True)
                M(psum[:, 4, 40:48], ones, g_tok[:, 0:U], start=True, stop=True)
                M(psum[:, 4, 64:128], ones, samp_rhs, start=True, stop=True).then_inc(g_rows, 1)
                for t in range(10, 24):
                    project(t)
                for t in range(2 * H):
                    if t == 0:
                        pe.wait_ge(exp_small, 2 * l + 2)
                        pe.wait_ge(l_args, l + 1)
                        pe.wait_ge(exp_big, 3 * l + 1)
                    if t == H:
                        project(24)
                        pe.wait_ge(qk_rms, 2 * l + 1)
                    pe.wait_ge(qk_squares, 2 * H * l + t + 1)
                    M(psum[:, 4 + t % 4, 0:T], ones, sq_qk[:, t, :], start=True, stop=True).then_inc(qk_sums, 1)
                project(25)
                pe.wait_ge(qk_normed, 2 * (l + 1))

                def kq(first, h, cc):
                    return qkv[:, first + h, cc * P:(cc + 1) * P]

                for cc in range(NC):
                    for h in range(H):
                        last = M(psum[:, 4 + cc, h * P:(h + 1) * P], kq(H, h, cc), kq(H, h, cc), start=True, stop=True)
                last.then_inc(gram_done, 1)
                for cc in range(NC):
                    for h in range(H):
                        last = M(psum[:, 6 + cc, h * P:(h + 1) * P], kq(H, h, cc), kq(0, h, cc), start=True, stop=True)
                last.then_inc(gram_done, 1)
                project(26)
                project(27)
                pe.wait_ge(level_masked, LEVELS * l + 1)
                pe.wait_ge(gram_taken, 2 * l + 1)
                for u in range(U):
                    last = nc.tensor.transpose(pair(4)[:, u, :], units(5)[:, u, :], ident)
                last.then_inc(first_tr, 1)
                for v in range(1, LEVELS):
                    pe.wait_ge(tu_done, LEVELS * l + v)
                    pe.wait_ge(level_masked, LEVELS * l + v + 1)
                    for u in range(U):
                        last = M(pair(4)[:, u, :], units(5 + v % 2)[:, u, :], units(4)[:, u, :], start=True, stop=True)
                    last.then_inc(b_mm, 1)
                    project(26 + 2 * v)
                    pe.wait_ge(b_taken, (LEVELS - 1) * l + v)
                    if v == 1:
                        pe.wait_ge(gram_taken, 2 * l + 2)
                    for u in range(U):
                        last = M(pair(6)[:, u, :], units(3)[:, u, :], units(8)[:, u, :], start=True, stop=True)
                    last.then_inc(pq_mm, 1)
                    if v < LEVELS - 1:
                        for u in range(U):
                            last = M(pair(4)[:, u, :], units(8)[:, u, :], units(3)[:, u, :], start=True, stop=True)
                        last.then_inc(pq_mm, 1)
                    project(27 + 2 * v)
                pe.wait_ge(tu_done, LEVELS * (l + 1))
                for cc in range(NC):
                    for h in range(H):
                        nc.tensor.transpose(psum[:, 4 + cc, h * P:(h + 1) * P], kq(H, h, cc), ident)
                        last = nc.tensor.transpose(psum[:, 6 + cc, h * P:(h + 1) * P], kq(2 * H, h, cc), ident)
                last.then_inc(kv_tr, 1)
                pe.wait_ge(kv_taken, l + 1)
                for u in range(U):
                    last = M(pair(4)[:, u, :], units(5)[:, u, :], units(4)[:, u, :], start=True, stop=True)
                last.then_inc(w_mm, 1)
                pe.wait_ge(samp_vn, 2 * l + 1)
                pe.wait_ge(s0_loaded, 16 * (l + 1))
                for b in range(NB):
                    for h in range(H):
                        u = b * H + h
                        M(psum[:, 7, 2 * u:2 * u + 2], s0[:, u, :], qkv[:, h:2 * H:H, TP + b], start=True, stop=True)
                M(psum[:, 7, 64:96], ones, s_prod, start=True, stop=True).then_inc(samp_mm, 1)
                for cc in range(NC):
                    if cc:
                        pe.wait_ge(os_taken, 2 * l + cc)
                    else:
                        pe.wait_ge(w_taken, l + 1)
                    for h in range(H):
                        u = cc * H + h
                        last = M(psum[:, 6, h * P:(h + 1) * P], units(4)[:, u, :], units(6)[:, u, :], start=True, stop=(cc == 0))
                        if cc:
                            last = M(psum[:, 6, h * P:(h + 1) * P], units(8)[:, u, :], units(3)[:, h, :], start=False, stop=True)
                    last.then_inc(vn_mm, 1)
                    pe.wait_ge(vn_taken, NC * l + cc + 1)
                    for h in range(H):
                        u = cc * H + h
                        last = M(psum[:, 4, h * P:(h + 1) * P], units(2)[:, u, :], units(1)[:, u, :], start=True, stop=(cc == 0))
                        if cc:
                            last = M(psum[:, 4, h * P:(h + 1) * P], units(3)[:, h, :], units(0)[:, u, :], start=False, stop=True)
                    last.then_inc(os_mm, 1)
                    for h in range(H):
                        u = cc * H + h
                        last = M(psum[:, 5, h * P:(h + 1) * P], units(7)[:, u, :], units(2)[:, u, :], start=True, stop=True)
                    last.then_inc(os_mm, 1)
                pe.wait_ge(samp_vn, 2 * l + 2)
                nc.tensor.transpose(psum[0:32, 7, 128:256], vn_s, ident)
                nc.tensor.transpose(psum[0:32, 7, 256:384], k_s, ident).then_inc(samp_tr, 1)
                pe.wait_ge(samp_rows, l + 1)
                pe.wait_ge(samp_vm, l + 1)
                pe.wait_ge(os_taken, 2 * l + 2)
                for g in range(8):
                    if g >= 2:
                        pe.wait_ge(outer_taken, 8 * l + g - 1)
                    M(psum[:, 4 + g % 2, :], rows32[0:32, 1, :], vmask[0:32, 4 * g:4 * g + 4, :].rearrange("p u d -> p (u d)"),
                      start=True, stop=True).then_inc(outer_mm, 1)
                pe.wait_ge(outer_taken, 8 * (l + 1))
                for h in range(H):
                    pe.wait_ge(o_squares, H * l + h + 1)
                    M(psum[:, 4 + h, 0:T], ones, work[:, 4 + h, 0:T], start=True, stop=True).then_inc(o_sums, 1)
                pe.wait_ge(conv_out, CT * (l + 1))
                pe.wait_ge(act_evac, 32 * (l + 1))
                for j in range(CT):
                    last = M(psum[:, 0, 0:T], ones, c[:, j, :], start=(j == 0), stop=(j == CT - 1))
                last.then_inc(ln_sum, 1)
                for j in range(CT):
                    pe.wait_ge(ln_sq, CT * l + j + 1)
                    last = M(psum[:, 1, 0:T], ones, work[:, 4 + j, 512:512 + T], start=(j == 0), stop=(j == CT - 1))
                last.then_inc(ln_var, 1)
                pe.wait_ge(o_done, l + 1)
                pe.wait_ge(c_done, CT * (l + 1))
                for t in range(KD):
                    w = arrived(section, N_PROJ + t)
                    if t >= 2:
                        pe.wait_ge(merged_done, KD * l + t - 1)
                    for j in range(CT):
                        M(psum[:, 2 * (t % 2), 0:T], w[:, j, :], c[:, j, :], start=(j == 0), stop=(j == CT - 1))
                    for h in range(H):
                        last = M(psum[:, 2 * (t % 2) + 1, 0:T], w[:, CT + h, :], qkv[:, 8 + h, :], start=(h == 0), stop=(h == H - 1))
                    last.then_inc(units_used, 1)
                pe.wait_ge(merged_done, KD * (l + 1))
                for t in range(KD):
                    w = arrived(section, N_PROJ + N_MIX + t)
                    if t >= 4:
                        pe.wait_ge(x_done, KD * l + t - 3)
                    for k in range(KD):
                        last = M(psum[:, t % 4, 0:T], w[:, k, :], hT[:, k, :], start=(k == 0), stop=(k == KD - 1))
                    last.then_inc(units_used, 1)
                model_sums(2 * l + 1)

                if l == 0:
                    n0 = [uses_before(first_position("ffn") + s) for s in range(RING)]
                    pe.wait_ge(h_done, 2 * KD)
                    for half in range(2):
                        for j in range(FT // 2):
                            n_act = half * (FT // 2) + j
                            if n_act >= 3:
                                pe.wait_ge(act_done, n_act - (1 if j < 2 else 2))
                            for i in range(2):
                                pe.wait_ge(slot_loaded[2 * j + i], 16 * (n0[2 * j + i] + half + 1))
                                for k in range(KD):
                                    last = M(psum[:, 2 * (j % 3) + i, 0:T], ring[:, 2 * j + i, k, :], hT[:, k, :], start=(k == 0), stop=(k == KD - 1))
                                last.then_inc(units_used, 1)
                    for i in range(KD * FT):
                        t, f = divmod(i, FT)
                        s = i // KD
                        if i % KD == 0:
                            pe.wait_ge(slot_loaded[s], 16 * (n0[s] + 3))
                        if i == 0:
                            pe.wait_ge(act_done, FT)
                        if f == 0 and t >= 2:
                            pe.wait_ge(down_taken, t - 1)
                        last = M(psum[:, 6 + t % 2, 0:T], ring[:, s, i % KD, :], act_all[:, f, :], start=(f == 0), stop=(f == FT - 1))
                        if i % KD == KD - 1:
                            last.then_inc(units_used, 1)
                        elif f == FT - 1:
                            last.then_inc(down_done, 1)
                else:
                    n0 = [uses_before(first_position("experts") + s) for s in range(RING)]
                    pe.wait_ge(h_done, 4 * KD)
                    for m, t0 in enumerate((0, P, T - P)):
                        for k in range(KD):
                            last = M(psum[:, 4, m * 8:m * 8 + 8], hT[:, k, t0:t0 + P], par("router", k * 8, 8),
                                     start=(k == 0), stop=(k == KD - 1))
                    last.then_inc(router_mm, 1)
                    for m, t0 in enumerate((0, P, T - P)):
                        for k in range(KD):
                            b = (0, 2, 6)[m] + k // 4
                            last = nc.tensor.transpose(psum[:, b, k % 4 * P:(k % 4 + 1) * P], hT[:, k, t0:t0 + P], ident)
                        last.then_inc(h_tr, 1)
                    pe.wait_ge(chosen, 1)
                    sent = rt[:, 8, :]
                    for m in range(3):
                        for before in range(m):
                            M(psum[:, 5, m * NE:(m + 1) * NE], ones, sent[:, before * NE:(before + 1) * NE], start=(before == 0), stop=False)
                        M(psum[:, 5, m * NE:(m + 1) * NE], triu_strict, sent[:, m * NE:(m + 1) * NE], start=(m == 0), stop=True)
                    for m in range(3):
                        last = M(psum[:, 5, 24:32], ones, sent[:, m * NE:(m + 1) * NE], start=(m == 0), stop=(m == 2))
                    last.then_inc(ranks_mm, 1)

                    def gather(job):
                        pe.wait_ge(take_done, job + 1)
                        for k in range(KD):
                            for m in range(3):
                                last = M(psum[:, k // 4, k % 4 * CAP:(k % 4 + 1) * CAP], h_tok[:, m, k * P:(k + 1) * P], take[:, m, :],
                                         start=(m == 0), stop=(m == 2))
                        last.then_inc(gather_mm, 1)

                    pe.wait_ge(h_tok_done, 3)
                    gather(0)
                    pe.wait_ge(rows_rhs, 1)
                    for b in range(3):
                        last = M(psum[:, 2 + b, :], ones, work[:, 0:2, :].rearrange("p a b -> p (a b)")[:, b * 512:(b + 1) * 512], start=True, stop=True)
                    last.then_inc(rows_mm, 1)
                    pe.wait_ge(rows_done, 1)
                    pe.wait_ge(jobs_done, 1)
                    n_jobs = pe.value_load(jobs[0:1, MAX_JOBS:MAX_JOBS + 1], min_val=2, max_val=MAX_JOBS)
                    with pe.Fori(0, n_jobs) as job:
                        with pe.Fori(0, 2) as half:
                            for j in range(FT // 2):
                                if j == 0:
                                    pe.wait_ge(h_job_done, job + 1)
                                elif j == 2:
                                    pe.wait_ge(down_taken, job * KD + KD)
                                pe.wait_ge(act_done, job * FT + half * (FT // 2) + (FT + j - (1 if j < 2 else 2)))
                                for i in range(2):
                                    pe.wait_ge(slot_loaded[2 * j + i], job * 48 + half * 16 + 16 * (n0[2 * j + i] + 1))
                                    for k in range(KD):
                                        last = M(psum[:, 2 * (j % 3) + i, 0:CAP], ring[:, 2 * j + i, k, :], h_job[:, k, :],
                                                 start=(k == 0), stop=(k == KD - 1))
                                    last.then_inc(units_used, 1)
                        pe.wait_ge(act_done, job * FT + 2 * FT)
                        for i in range(KD * FT):
                            t, f = divmod(i, FT)
                            s = i // KD
                            if i % KD == 0:
                                pe.wait_ge(slot_loaded[s], job * 48 + 16 * (n0[s] + 3))
                            if f == 0 and t >= 2:
                                pe.wait_ge(y_taken, job * KD + (t - 1))
                            last = M(psum[:, 6 + t % 2, 0:CAP], ring[:, s, i % KD, :], act_job[:, f, :], start=(f == 0), stop=(f == FT - 1))
                            if i % KD == KD - 1:
                                last.then_inc(units_used, 1)
                            elif f == FT - 1:
                                last.then_inc(down_done, 1)
                        gather(job + 1)
                        pe.wait_ge(y_taken, job * KD + KD)
                        for t in range(KD):
                            last = nc.tensor.transpose(psum[0:CAP, 2 + t // 4, t % 4 * P:(t % 4 + 1) * P], y_job[:, t, :], ident)
                        last.then_inc(y_tr, 1)
                        pe.wait_ge(y_tok_done, job + 1)
                        pe.wait_ge(put_done, job + 1)
                        for t in range(KD):
                            if t >= 2:
                                pe.wait_ge(down_taken, job * KD + (KD + t - 1))
                            M(psum[:, 4 + t % 2, 0:T], y_tok[:, t * P:(t + 1) * P], put, start=True, stop=True).then_inc(scatter_mm, 1)
                    pe.wait_ge(down_taken, n_jobs * KD + KD)
            model_sums(2 * DEPTH)


PARAMS = [("norm1", DEPTH * KD), ("norm2", DEPTH * KD), ("final", KD), ("o_g", DEPTH), ("dw_b", DEPTH * CT),
          ("ln_g", DEPTH * CT), ("ln_b", DEPTH * CT), ("dw_w", DEPTH * CT * DW), ("qk_w", DEPTH * QT * QW),
          ("a_log", DEPTH * H), ("dt_bias", DEPTH * H), ("w_ab", DEPTH * KD * 8), ("router", KD * NE),
          ("samp_mask", NB), ("iota", 24), ("eps", 1),
          ("keep", 3 * NE), ("drop", 6), ("slot_row", CAP), ("slot_col", 1), ("job_no", MAX_JOBS * NE)]


def kernel(x_prompt, x_sample, state_delta, state_qkv_conv, state_dwconv, norm1_g, w_in, qkv_conv_w,
           a_log, dt_bias, o_norm_g, w_delta_out, dw_w, dw_b, ln_g, ln_b, w_conv_out, w_o, norm2_g,
           ffn_w_gate, ffn_w_up, ffn_w_down, router_w, exp_w_gate, exp_w_up, exp_w_down, final_norm_g):
    import concourse.bacc as bacc
    from concourse.bass_utils import run_bass_kernel_spmd

    n = lambda x: np.ascontiguousarray(np.asarray(x))
    L, F = DEPTH, np.float32

    def feat(x):
        x = n(x)
        lead = tuple(range(x.ndim - 1))
        y = x.reshape(x.shape[:-1] + (x.shape[-1] // P, P))
        return y.transpose((y.ndim - 1, y.ndim - 2) + lead)

    def by_layer(x):
        return n(x).reshape(L, -1, P).transpose(2, 0, 1).reshape(P, -1)

    def out_tiles(w):
        w = n(w)
        return w.reshape(w.shape[0] // P, P, w.shape[1] // P, P).transpose(2, 1, 0, 3).reshape(w.shape[1] // P, P, -1)

    def ffn_units(wg, wu, wd):
        gu = np.stack([out_tiles(wg), out_tiles(wu)], 1).reshape(2 * FT, P, KD * P)
        blocks = n(wd).reshape(FT, P, KD, P).transpose(2, 0, 1, 3).reshape(FT, KD, P, P)
        return np.concatenate([gu, blocks.transpose(0, 2, 1, 3).reshape(FT, P, KD * P)])

    w_in = n(w_in)
    w_mixer = np.empty((L, N_LAYER, P, KD * P), F)
    for l in range(L):
        t = out_tiles(w_in[l, :, 0:3072])
        w_mixer[l, 0:8:2], w_mixer[l, 1:8:2], w_mixer[l, 8:24] = t[0:4], t[4:8], t[8:24]
        w_mixer[l, 24:40] = out_tiles(w_in[l, :, 3080:])
        w_mixer[l, 40:48] = np.concatenate([out_tiles(w_conv_out[l]), out_tiles(w_delta_out[l])], 2)
        w_mixer[l, 48:56] = out_tiles(w_o[l])
    w_exp = np.concatenate([ffn_units(exp_w_gate[0][e], exp_w_up[0][e], exp_w_down[0][e]) for e in range(NE)])

    everywhere = lambda x: np.broadcast_to(n(x).reshape(1, -1), (P, n(x).size))
    real = (np.arange(P)[:, None] >= SAMPLE_ROW) | (np.arange(3)[None] < 2)
    packed = {
        "norm1": by_layer(norm1_g), "norm2": by_layer(norm2_g), "final": n(final_norm_g).reshape(KD, P).T,
        "o_g": n(o_norm_g).T, "dw_b": by_layer(dw_b), "ln_g": by_layer(ln_g), "ln_b": by_layer(ln_b),
        "dw_w": n(dw_w).reshape(L, DW, CT, P).transpose(3, 0, 2, 1).reshape(P, -1),
        "qk_w": n(qkv_conv_w).reshape(L, QW, QT, P).transpose(3, 0, 2, 1).reshape(P, -1),
        "a_log": everywhere(a_log), "dt_bias": everywhere(dt_bias),
        "w_ab": w_in[:, :, 3072:3080].reshape(L, KD, P, 8).transpose(2, 0, 1, 3).reshape(P, -1),
        "router": n(router_w)[0].reshape(KD, P, NE).transpose(1, 0, 2).reshape(P, -1),
        "samp_mask": (np.arange(P)[:, None] == SAMPLE_ROW + np.arange(NB)[None]).astype(F),
        "keep": np.repeat(real, NE, 1).astype(F), "drop": np.tile(np.where(real, 0.0, -1e6), (1, 2)).astype(F),
        "slot_row": np.broadcast_to(np.arange(CAP).astype(F)[None], (P, CAP)), "slot_col": np.arange(P).astype(F)[:, None],
        "job_no": np.broadcast_to(np.repeat(np.arange(MAX_JOBS), NE).astype(F)[None], (P, MAX_JOBS * NE)),
        "eps": np.full((P, 1), EPS, F),
        "iota": np.broadcast_to(np.tile(np.arange(NE), 3).astype(F)[None], (P, 3 * NE)),
    }
    i, j = np.arange(P)[:, None], np.arange(P)[None]
    masks = [i == j, i >= 0 * j, j >= i, j > i]
    level_masks = []
    for v in range(LEVELS):
        b = 1 << v
        level_masks.append((i // (2 * b) == j // (2 * b)) & (i // b % 2 == 1) & (j // b % 2 == 0))
    x_all = np.concatenate([n(x_prompt)[0], n(x_sample)[:, 0]], 0)

    def window(state, taps):
        s = n(state)
        w = np.zeros((L, P, s.shape[-1] // P, NB, taps), F)
        w[..., :-1] = s.reshape(L, NB, taps - 1, -1, P).transpose(0, 4, 3, 1, 2)
        return w.reshape(L, P, -1)

    arrays = {
        "xT": feat(x_all).reshape(P, -1), "params": np.concatenate([packed[k] for k, _ in PARAMS], 1),
        "consts": np.stack(masks, 1).astype(F).reshape(P, -1), "w_mixer": w_mixer,
        "level_masks": np.stack(level_masks, 1).astype(mybir.dt.np(mybir.dt.bfloat16)).reshape(P, -1), "w_ffn": ffn_units(ffn_w_gate[0], ffn_w_up[0], ffn_w_down[0]), "w_exp": w_exp,
        "s0": n(state_delta).transpose(0, 3, 1, 2, 4).reshape(L, P, -1),
        "dw_win": window(state_dwconv, DW), "qkv_win": window(state_qkv_conv, QW),
    }
    outs = {"yT": (P, KD * T), "sp": (L, P, H * P), "ss": (L, P, NB * H * P), "dwp": (L, P, CT, DW - 1),
            "dws": (L, P, CT * NB * DW), "qkp": (L, P, QT, QW - 1), "qks": (L, P, QT * NB * QW)}

    nc = bacc.Bacc("TRN2", target_bir_lowering=False, num_devices=1)
    ins = {}
    for name, value in arrays.items():
        arrays[name] = np.ascontiguousarray(value)
        ins[name] = nc.dram_tensor("in_" + name, value.shape, mybir.dt.from_np(arrays[name].dtype), kind="ExternalInput").ap()
    o = {name: nc.dram_tensor("out_" + name, shape, F32, kind="ExternalOutput").ap() for name, shape in outs.items()}
    build(nc, ins, o)
    r = run_bass_kernel_spmd(nc, [{"in_" + k: v for k, v in arrays.items()}], core_ids=[0]).results[0]
    g = {name: np.asarray(r["out_" + name]) for name in outs}

    y = g["yT"].reshape(P, KD, T).transpose(2, 1, 0).reshape(T, D)

    def rows(x, lead):
        x = x.reshape((L, P) + lead)
        return n(np.moveaxis(x, (2, 1), (-2, -1)).reshape((L,) + lead[1:] + (-1,)))

    return (
        n(y[None, :TP]), n(y[TP:, None]),
        n(g["sp"].reshape(L, P, H, P).transpose(0, 2, 1, 3)[:, None]),
        rows(g["qkp"], (QT, QW - 1))[:, None], rows(g["dwp"], (CT, DW - 1))[:, None],
        n(g["ss"].reshape(L, P, NB, H, P).transpose(0, 2, 3, 1, 4)),
        n(rows(g["qks"], (QT, NB, QW))[:, :, 1:]), n(rows(g["dws"], (CT, NB, DW))[:, :, 1:]),
    )
```

```python
from contextlib import ExitStack

import numpy as np

import concourse.bass as bass
from concourse import mybir

ALU = mybir.AluOpType
ACT = mybir.ActivationFunctionType
F32 = mybir.dt.float32
F32R = mybir.dt.float32r
AX_X = mybir.AxisListType.X

P = 128
D = 1024
KD = D // P
TP = 256
NB = 8
T = TP + NB
NC = TP // P
H = 4
U = NC * H
DEPTH = 2
DW = 31
QW = 4
CT = 4
QT = 12
FT = 22
NE = 8
EPS = 1e-6
N_PROJ = 40
GLU0, QKV0, Z0, GATE0 = 0, 8, 20, 24
N_MIX = 8
N_WO = 8
N_FFN = 66
N_LAYER = N_PROJ + N_MIX + N_WO
RING = 11
N_PROJ_SPLIT = 34
SPLIT = 3
CHUNK = 256
NCH = FT * P // CHUNK
LEVELS = 7
CAP = 96
MAX_JOBS = (2 * T + NE * (CAP - 1)) // CAP + 1
SAMPLE_ROW = P - NB


def first_position(section):
    return {"mix0": 0, "ffn": N_FFN, "mix1": 2 * N_FFN, "experts": 3 * N_FFN}[section]


def build(nc, a, o):
    ctx = ExitStack()
    with ctx:
        def sb(name, shape, dt=F32):
            return ctx.enter_context(nc.sbuf_tensor(name, [P] + list(shape), dt))

        def sem(name):
            return ctx.enter_context(nc.semaphore(name))

        ring = sb("ring", [RING, KD, P])
        xT = sb("xT", [KD, T])
        hT = sb("hT", [KD, T])
        early = sb("early", [NB * H * P])
        n_pad = CT * (DW - 1 + TP)
        u_pad = early[:, 0:n_pad].rearrange("p (c n) -> p c n", c=CT)
        u_win = early[:, n_pad:n_pad + CT * NB * DW].rearrange("p (c b n) -> p c b n", c=CT, b=NB)
        s0 = early[:, :].rearrange("p (u n) -> p u n", n=P)
        c = sb("c", [CT, T])
        qkv = sb("qkv", [QT, T])
        zs = sb("zs", [H, T])
        gs = sb("gs", [2 * KD, T])
        work = sb("work", [9, U * P])
        w_hi, w_lo = sb("w_hi", [SPLIT, KD * P], F32R), sb("w_lo", [SPLIT, KD * P], F32R)
        h_hi, h_lo = sb("h_hi", [KD * CAP], F32R), sb("h_lo", [KD * CAP], F32R)
        hid_hi, hid_lo = (sb(name, [max(FT * CAP, KD * T)], F32R) for name in ("hid_hi", "hid_lo"))
        x_hi, x_lo = (x[:, 0:KD * T].rearrange("p (k t) -> p k t", t=T) for x in (hid_hi, hid_lo))
        act_hi, act_lo = (x[:, 0:FT * CAP].rearrange("p (f s) -> p f s", s=CAP) for x in (hid_hi, hid_lo))
        consts = sb("consts", [4, P])
        level_masks = sb("level_masks", [LEVELS, P], mybir.dt.bfloat16)
        small = sb("small", [576])
        prm = sb("prm", [a["params"].shape[1]])

        ident, ones, triu, triu_strict = (consts[:, i, :] for i in range(4))
        psum = ctx.enter_context(nc.psum_tensor("psum", [P, 8, 512], F32))

        def pair(b):
            return psum[:, b:b + 2, :].rearrange("p b (u i) -> p (b u) i", i=P)

        def units(w):
            return work[:, w, :].rearrange("p (u i) -> p u i", i=P)

        pads = work[:, 3:7, :].rearrange("p a b -> p (a b)")
        q_pad = pads[:, 0:QT * (QW - 1 + TP)].rearrange("p (t n) -> p t n", t=QT)
        q_win = pads[:, QT * (QW - 1 + TP):QT * (QW - 1 + TP + NB * QW)].rearrange(
            "p (t b n) -> p t b n", t=QT, b=NB)
        sq_qk = gs[:, 0:2 * H, :]
        act_all = work[:, 0:6, :].rearrange("p a b -> p (a b)")[:, 0:FT * T].rearrange("p (f t) -> p f t", t=T)
        silu_g = work[:, 6, 0:3 * T].rearrange("p (r t) -> p r t", t=T)
        h_tok = gs[:, :, :].rearrange("p k t -> p (k t)")[:, 0:3 * D].rearrange("p (m d) -> p m d", m=3)
        silu_job = work[0:CAP, 0, :].rearrange("p (r s) -> p r s", r=4)
        prod_job = work[0:CAP, 1, :].rearrange("p (r s) -> p r s", r=4)
        y_tok = work[0:CAP, 5, :]
        put = work[0:CAP, 7, 0:T]
        put_2 = work[0:CAP, 7, T:2 * T]
        take = work[:, 8, 0:3 * CAP].rearrange("p (m s) -> p m s", m=3)
        rows4 = c[:, :, :]
        sq = gs[:, 0:KD, :]

        def glu_gate(j):
            return work[:, 8, (j % 2) * T:(j % 2 + 1) * T]

        vmask = work[:, 0:4, :].rearrange("p a (u d) -> p (a u) d", d=P)

        at = {}
        pos = 0
        for name, n in PARAMS:
            at[name] = pos
            pos += n

        def par(name, i, n=1):
            return prm[:, at[name] + i:at[name] + i + n]

        def par_block(name, l, k):
            return prm[:, at[name] + l * k:at[name] + (l + 1) * k]

        smalls = {}
        spos = [0]

        def sm(name, n):
            smalls[name] = (spos[0], n)
            spos[0] += n
            return small[:, spos[0] - n:spos[0]]

        t_a = sm("t_a", 12)
        t_abs = sm("t_abs", 12)
        t_exp = sm("t_exp", 12)
        t_ln = sm("t_ln", 12)
        g_tok = sm("g_tok", 12)
        b_exp = sm("b_exp", 12)
        beta = sm("beta", 12)
        nea = sm("nea", 4)
        ab_tok = sm("ab_tok", 24)
        tables = sm("tables", 96)
        gcc = tables[:, 0:8]
        gl = tables[:, 8:16]
        betas = tables[:, 64:96]
        gd = sm("gd", 8)
        egc = sm("egc", 8)
        egl = sm("egl", 8)
        kdsc = sm("kdsc", 8)
        nbeg = sm("nbeg", 8)
        samp_rhs = sm("samp_rhs", 64)
        egs = sm("egs", 32)
        vn_s = sm("vn_s", 32)
        k_s = sm("k_s", 32)
        qk_s = sm("qk_s", 32)
        o_t = sm("o_t", 32)
        s_prod = sm("s_prod", 32)
        rl = sm("rl", 24)
        warm_cells = sm("warm_cells", 16)
        assert spos[0] <= 576
        rstd = sb("rstd", [T])
        o_rstd = work[:, 8, 512:512 + T]
        rows32 = sb("rows32", [2, P])
        after_z = zs[:, :, :].rearrange("p h t -> p (h t)")
        rt = after_z[:, 0:12 * 24].rearrange("p (a b) -> p a b", a=12)
        scan = after_z[:, 12 * 24:12 * 24 + 8 * NE].rearrange("p (a b) -> p a b", a=4)
        slot_no = sb("slot_no", [1])
        jobs = ctx.enter_context(nc.sbuf_tensor("jobs", [P, MAX_JOBS + 1], mybir.dt.int32))

        slot_loaded = [sem(f"slot_loaded{i}") for i in range(RING)]
        units_used = sem("units_used")
        x_loaded = sem("x_loaded")
        consts_loaded = sem("consts_loaded")
        masks_loaded = sem("masks_loaded")
        states_loaded = sem("states_loaded")
        dw_loaded = sem("dw_loaded")
        zeros_set = sem("zeros_set")
        squares_done = sem("squares_done")
        sums_done = sem("sums_done")
        h_done = sem("h_done")
        glu_sig = sem("glu_sig")
        glu_done = sem("glu_done")
        conv_out = sem("conv_out")
        act_evac = sem("act_evac")
        ab_done = sem("ab_done")
        soft_in = sem("soft_in")
        soft_exp = sem("soft_exp")
        g_done = sem("g_done")
        g_rows = sem("g_rows")
        l_args = sem("l_args")
        exp_small = sem("exp_small")
        exp_big = sem("exp_big")
        pool_l = sem("pool_l")
        qconv_done = sem("qconv_done")
        qkv_silu = sem("qkv_silu")
        qk_squares = sem("qk_squares")
        rms_done = sem("rms_done")
        ln_rms = sem("ln_rms")
        qk_normed = sem("qk_normed")
        gram_done = sem("gram_done")
        gram_taken = sem("gram_taken")
        level_masked = sem("level_masked")
        first_tr = sem("first_tr")
        tu_done = sem("tu_done")
        b_mm = sem("b_mm")
        b_taken = sem("b_taken")
        pq_mm = sem("pq_mm")
        kv_tr = sem("kv_tr")
        kv_taken = sem("kv_taken")
        w_mm = sem("w_mm")
        w_taken = sem("w_taken")
        vn_mm = sem("vn_mm")
        vn_taken = sem("vn_taken")
        os_mm = sem("os_mm")
        os_taken = sem("os_taken")
        samp_mm = sem("samp_mm")
        samp_vn = sem("samp_vn")
        samp_tr = sem("samp_tr")
        samp_rows = sem("samp_rows")
        samp_vm = sem("samp_vm")
        s0_scaled = sem("s0_scaled")
        outer_mm = sem("outer_mm")
        outer_taken = sem("outer_taken")
        o_squares = sem("o_squares")
        o_done = sem("o_done")
        ln_sum = sem("ln_sum")
        ln_cen = sem("ln_cen")
        ln_sq = sem("ln_sq")
        ln_var = sem("ln_var")
        ln_norm = sem("ln_norm")
        c_done = sem("c_done")
        merged_done = sem("merged_done")
        x_done = sem("x_done")
        silu_done = sem("silu_done")
        act_done = sem("act_done")
        down_done = sem("down_done")
        down_taken = sem("down_taken")
        router_mm = sem("router_mm")
        gates_exp_in = sem("gates_exp_in")
        gates_exp = sem("gates_exp")
        h_tr = sem("h_tr")
        h_tok_done = sem("h_tok_done")
        chosen = sem("chosen")
        ranks_mm = sem("ranks_mm")
        jobs_done = sem("jobs_done")
        take_done = sem("take_done")
        rows_rhs = sem("rows_rhs")
        rows_mm = sem("rows_mm")
        rows_done = sem("rows_done")
        gather_mm = sem("gather_mm")
        hi_done = sem("hi_done")
        lo_done = sem("lo_done")
        pool_lo_done = sem("pool_lo_done")
        x_hi_done = sem("x_hi_done")
        x_lo_done = sem("x_lo_done")
        h_hi_done = sem("h_hi_done")
        h_job_done = sem("h_job_done")
        chunk_silu = sem("chunk_silu")
        chunk_done = sem("chunk_done")
        act_tr = sem("act_tr")
        act_hi_done = sem("act_hi_done")
        act_lo_done = sem("act_lo_done")
        y_tok_done = sem("y_tok_done")
        put_done = sem("put_done")
        scatter_mm = sem("scatter_mm")
        put_step = sem("put_step")
        s0_loaded = sem("s0_loaded")
        y_done = sem("y_done")
        state_out = sem("state_out")
        final_out = sem("final_out")
        dve_step = sem("dve_step")
        rows_sum = sem("rows_sum")
        rows_rms = sem("rows_rms")
        rows_recip = sem("rows_recip")
        rows_spread = sem("rows_spread")

        ordinal = {}
        n = 0
        for section, count in (("mix0", N_LAYER), ("ffn", N_FFN), ("mix1", N_LAYER)):
            for i in range(count):
                ordinal[first_position(section) + i] = n
                n += 1
        base_ord = {"mix0": 0, "ffn": N_LAYER, "mix1": N_LAYER + N_FFN, "experts": 2 * N_LAYER + N_FFN}

        split_ord, low_ord, by_pool = {}, {}, set()
        for section, i0, i1 in (("mix0", 0, N_PROJ_SPLIT), ("mix0", N_PROJ + N_MIX, N_LAYER), ("ffn", 0, 2 * FT),
                                ("mix1", 0, N_PROJ_SPLIT), ("mix1", N_PROJ + N_MIX, N_LAYER)):
            for i in range(i0, i1):
                p = first_position(section) + i
                pool_does = section != "ffn" and i < N_PROJ_SPLIT
                low_ord[p] = sum(1 for q in split_ord if (q in by_pool) == pool_does)
                split_ord[p] = len(split_ord)
                if pool_does:
                    by_pool.add(p)
        split_at = {v: k for k, v in split_ord.items()}
        n_split = len(split_ord)
        n_low = n_split - len(by_pool)

        def low_count(p):
            return (pool_lo_done if p in by_pool else lo_done), low_ord[p] + 1

        assert N_FFN % SPLIT == 0

        def uses_before(position):
            return sum(1 for p in ordinal if p < position and p % RING == position % RING)

        n0 = [uses_before(first_position("experts") + s) for s in range(RING)]

        block = ctx.enter_context(nc.Block())

        @block.sync
        def _(sp):
            def load_static(section, i, src):
                p = first_position(section) + i
                before = [q for q in ordinal if q < p and q % RING == p % RING]
                if before and max(before) in split_ord:
                    sp.wait_ge(*low_count(max(before)))
                elif before:
                    sp.wait_ge(units_used, ordinal[max(before)] + 1)
                sp.dma_start(ring[:, p % RING, :, :].rearrange("p k n -> p (k n)"), src).then_inc(slot_loaded[p % RING], 16)

            sp.dma_start(xT[:, :, :].rearrange("p k t -> p (k t)"), a["xT"]).then_inc(x_loaded, 16)
            sp.dma_start(consts[:, :, :].rearrange("p k t -> p (k t)"), a["consts"]).then_inc(consts_loaded, 16)
            sp.dma_start(prm[:, :], a["params"]).then_inc(consts_loaded, 16)
            for i in range(N_LAYER):
                load_static("mix0", i, a["w_mixer"][0, i])
            for i in range(RING):
                load_static("ffn", i, a["w_ffn"][i])
            with sp.Fori(1, 2 * FT // RING + 1) as r:
                for s in range(RING):
                    sp.wait_ge(lo_done, r * RING + (low_ord[first_position("ffn")] + s + 1 - RING))
                    sp.dma_start(ring[:, s, :, :].rearrange("p k n -> p (k n)"),
                                 a["w_ffn"][bass.ds(r * RING + s, 1), :, :].rearrange("a p n -> p (a n)")
                                 ).then_inc(slot_loaded[s], 16)
            for i in range(2 * FT + RING, N_FFN):
                load_static("ffn", i, a["w_ffn"][i])
            for i in range(N_LAYER):
                load_static("mix1", i, a["w_mixer"][1, i])
            for i in range(RING):
                load_static("experts", i, a["w_exp"][i])

            def load_expert(expert, job, first_revolution):
                with sp.Fori(first_revolution, N_FFN // RING) as r:
                    for s in range(RING):
                        sp.wait_ge(lo_done, job * N_FFN + r * RING + (n_low + s + 1 - RING))
                        sp.dma_start(ring[:, s, :, :].rearrange("p k n -> p (k n)"),
                                     a["w_exp"][bass.ds(expert * N_FFN + r * RING + s, 1), :, :].rearrange("a p n -> p (a n)")
                                     ).then_inc(slot_loaded[s], 16)

            load_expert(0, 0, 1)
            sp.wait_ge(jobs_done, 1)
            n_jobs = sp.value_load(jobs[0:1, MAX_JOBS:MAX_JOBS + 1], min_val=2, max_val=MAX_JOBS)
            with sp.Fori(1, n_jobs) as job:
                expert = sp.value_load(jobs[0:1, bass.ds(job, 1)], min_val=0, max_val=NE - 1)
                load_expert(expert, job, 0)

        @block.gpsimd
        def _(pool):
            def mask_level(v):
                nc.gpsimd.tensor_tensor(units(5 + v % 2), units(7),
                                        level_masks[:, v, :].rearrange("p (a i) -> p a i", a=1).broadcast_to([P, U, P]),
                                        ALU.mult).then_inc(level_masked, 1)

            def low_part(l, t):
                p = first_position(f"mix{l}") + t
                n = split_ord[p]
                pool.wait_ge(hi_done, n + 1)
                nc.gpsimd.tensor_tensor(w_lo[:, n % SPLIT, :], ring[:, p % RING, :, :].rearrange("p k n -> p (k n)"),
                                        w_hi[:, n % SPLIT, :], ALU.subtract).then_inc(pool_lo_done, 1)

            for l in range(DEPTH):
                for t in range(SPLIT):
                    low_part(l, t)
                if l:
                    pool.wait_ge(merged_done, KD * l)
                    pool.wait_ge(state_out, 16 * 6 * l)
                    pool.wait_ge(down_taken, KD * l)
                nc.gpsimd.memset(u_pad[:, :, 0:DW - 1], 0.0).then_inc(zeros_set, 1)
                nc.gpsimd.memset(q_pad[:, :, 0:QW - 1], 0.0).then_inc(zeros_set, 1)
                pool.dma_start(early[:, n_pad:n_pad + CT * NB * DW], a["dw_win"][l]).then_inc(dw_loaded, 16)
                pool.dma_start(q_win.rearrange("p t b n -> p (t b n)"), a["qkv_win"][l]).then_inc(states_loaded, 16)
                if l == 0:
                    pool.dma_start(level_masks[:, :, :].rearrange("p k t -> p (k t)"), a["level_masks"]).then_inc(masks_loaded, 16)
                for k in range(KD):
                    pool.wait_ge(x_hi_done, 3 * KD * l + k + 1)
                    nc.gpsimd.tensor_tensor(x_lo[:, k, :], hT[:, k, :], x_hi[:, k, :], ALU.subtract).then_inc(x_lo_done, 1)
                for t in range(SPLIT, 16):
                    low_part(l, t)
                pool.wait_ge(glu_done, CT * (l + 1))
                pool.dma_start(o["dwp"][l], u_pad[:, :, TP:TP + DW - 1]).then_inc(state_out, 16)
                low_part(l, 16)
                pool.dma_start(o["dws"][l], early[:, n_pad:n_pad + CT * NB * DW]).then_inc(state_out, 16)
                for t in range(17, QKV0 + QT + SPLIT):
                    low_part(l, t)
                pool.wait_ge(exp_big, 3 * l + 2)
                nc.gpsimd.tensor_tensor(units(1), units(1), triu.rearrange("p (a i) -> p a i", a=1).broadcast_to([P, U, P]), ALU.mult)
                pool.wait_ge(exp_big, 3 * l + 3)
                pool.wait_ge(g_done, l + 1)
                nc.gpsimd.tensor_tensor(units(2), units(2), beta[:, 0:U].rearrange("p (u a) -> p u a", a=1).broadcast_to([P, U, P]),
                                        ALU.mult).then_inc(pool_l, 1)
                pool.wait_ge(act_evac, 32 * l + QT)
                pool.dma_start(o["qkp"][l], q_pad[:, :, TP:TP + QW - 1]).then_inc(state_out, 16)
                pool.dma_start(o["qks"][l], q_win.rearrange("p t b n -> p (t b n)")).then_inc(state_out, 16)
                for t in range(QKV0 + QT + SPLIT, GATE0 + 2):
                    low_part(l, t)
                pool.wait_ge(masks_loaded, 16)
                pool.wait_ge(gram_taken, 2 * l + 2)
                pool.wait_ge(state_out, 16 * (6 * l + 4))
                mask_level(0)
                mask_level(1)
                t = GATE0 + 2
                for v in range(2, LEVELS):
                    for _ in range(2 if v in (2, 3, 5) else 1):
                        low_part(l, t)
                        t += 1
                    if v == 2:
                        pool.wait_ge(tu_done, LEVELS * l + 1)
                    else:
                        pool.wait_ge(b_mm, (LEVELS - 1) * l + v - 2)
                    mask_level(v)
                pool.wait_ge(conv_out, CT * (l + 1))
                pool.wait_ge(state_out, 16 * (6 * l + 4))
                pool.dma_start(early[:, :], a["s0"][l]).then_inc(s0_loaded, 16)
                pool.wait_ge(samp_mm, l + 1)
                pool.wait_ge(exp_small, 2 * l + 2)
                nc.gpsimd.tensor_tensor(s0[:, :, :], s0[:, :, :], egs.rearrange("p (u a) -> p u a", a=1).broadcast_to([P, NB * H, P]),
                                        ALU.mult).then_inc(s0_scaled, 1)
                pool.wait_ge(os_taken, 2 * l + 2)
                pool.dma_start(o["sp"][l], units(3)[:, 0:H, :].rearrange("p h d -> p (h d)")).then_inc(state_out, 16)
                pool.wait_ge(outer_taken, 8 * (l + 1))
                pool.dma_start(o["ss"][l], early[:, :]).then_inc(state_out, 16)
            pool.wait_ge(y_done, KD)
            pool.dma_start(o["yT"], hT[:, :, :].rearrange("p k t -> p (k t)")).then_inc(final_out, 16)
            pool.wait_ge(state_out, 16 * 6 * DEPTH)
            pool.wait_ge(final_out, 16)

        @block.scalar
        def _(act):
            A = nc.scalar.activation

            def model_squares(l2):
                for k in range(KD):
                    if k == 0:
                        act.wait_ge(x_loaded, 16)
                    if l2 % 2:
                        act.wait_ge(x_done, KD * (l2 // 2) + k + 1)
                    elif l2 == 2:
                        act.wait_ge(down_taken, k + 1)
                    A(sq[:, k, :], xT[:, k, :], ACT.Square).then_inc(squares_done, 1)

            def model_rms(l2):
                warm(ACT.Sqrt)
                act.wait_ge(sums_done, l2 + 1)
                A(rstd[:, :], psum[:, 5, 0:T], ACT.Sqrt, scale=1.0 / D, bias=par("eps", 0)).then_inc(rms_done, 1)

            def high_part(section, i):
                p = first_position(section) + i
                act.wait_ge(slot_loaded[p % RING], 16 * (uses_before(p) + 1))
                n = split_ord[p]
                if n >= SPLIT:
                    act.wait_ge(units_used, ordinal[split_at[n - SPLIT]] + 1)
                A(w_hi[:, n % SPLIT, :], ring[:, p % RING, :, :].rearrange("p k n -> p (k n)"), ACT.Copy).then_inc(hi_done, 1)

            warmed = []

            def warm(func):
                A(warm_cells[:, len(warmed):len(warmed) + 1], par("eps", 0), func)
                warmed.append(func)

            for l in range(DEPTH):
                model_squares(2 * l)
                if l == 0:
                    act.wait_ge(consts_loaded, 32)
                for t in range(SPLIT):
                    high_part(f"mix{l}", t)
                model_rms(2 * l)
                for k in range(KD):
                    act.wait_ge(h_done, 2 * KD * l + k + 1)
                    A(x_hi[:, k, :], hT[:, k, :], ACT.Copy).then_inc(x_hi_done, 1)
                act.wait_ge(soft_in, l + 1)
                A(t_exp, t_abs, ACT.Exp, scale=-1.0).then_inc(soft_exp, 1)
                act.wait_ge(soft_exp, 4 * l + 1)
                A(b_exp.rearrange("p (t n) -> p t n", t=3), ab_tok.rearrange("p (t n) -> p t n", t=3)[:, :, H:2 * H], ACT.Exp, scale=-1.0).then_inc(soft_exp, 1)
                A(nea, par_block("a_log", l, H), ACT.Exp).then_inc(soft_exp, 1)
                A(t_ln, t_exp, ACT.Ln, bias=1.0).then_inc(soft_exp, 1)

                def glu_sigmoid(j):
                    high_part(f"mix{l}", GLU0 + 2 * j + SPLIT)
                    act.wait_ge(units_used, base_ord[f"mix{l}"] + GLU0 + 2 * j + 2)
                    if j >= 2:
                        act.wait_ge(glu_done, CT * l + j - 1)
                    A(glu_gate(j), psum[:, (GLU0 + 2 * j + 1) % 4, 0:T], ACT.Sigmoid).then_inc(glu_sig, 1)
                    high_part(f"mix{l}", GLU0 + 2 * j + SPLIT + 1)

                glu_sigmoid(0)
                glu_sigmoid(1)
                act.wait_ge(l_args, l + 1)
                A(units(0), pair(6), ACT.Exp).then_inc(exp_big, 1)
                A(egc, gcc, ACT.Exp)
                A(egl, gl, ACT.Exp)
                A(egs, tables[:, 32:64], ACT.Exp).then_inc(exp_small, 1)
                A(kdsc, gd, ACT.Exp).then_inc(exp_small, 1)
                A(units(1), units(1), ACT.Exp).then_inc(exp_big, 1)
                A(units(2), units(2), ACT.Exp, scale=-1.0).then_inc(exp_big, 1)

                glu_sigmoid(2)
                glu_sigmoid(3)

                def evac_qkv(t):
                    act.wait_ge(units_used, base_ord[f"mix{l}"] + QKV0 + t + 1)
                    if t == 0:
                        act.wait_ge(states_loaded, 16 * (l + 1))
                        act.wait_ge(zeros_set, 2 * l + 2)
                    A(q_pad[:, t, QW - 1:QW - 1 + TP], psum[:, t % 4, 0:TP], ACT.Copy)
                    A(q_win[:, t, :, QW - 1], psum[:, t % 4, TP:T], ACT.Copy).then_inc(act_evac, 1)
                    high_part(f"mix{l}", QKV0 + t + SPLIT)

                def silu_qkv(first):
                    for t in range(first, first + 4):
                        act.wait_ge(qconv_done, QT * l + t + 1)
                        A(qkv[:, t, :], qkv[:, t, :], ACT.Silu).then_inc(qkv_silu, 1)

                def squares_qk(first):
                    act.wait_ge(qkv_silu, QT * l + first + 4)
                    for t in range(first, first + 4):
                        A(sq_qk[:, t, :], qkv[:, t, :], ACT.Square).then_inc(qk_squares, 1)

                for t in range(7):
                    evac_qkv(t)
                silu_qkv(0)
                evac_qkv(7)
                squares_qk(0)
                for t in range(8, 11):
                    evac_qkv(t)
                silu_qkv(H)
                evac_qkv(11)
                squares_qk(H)
                warm(ACT.Sqrt)
                act.wait_ge(rows_sum, 2 * l + 1)
                A(rstd[0:2 * H, :], psum[0:2 * H, 4, 0:T], ACT.Sqrt, bias=par("eps", 0)[0:2 * H, :]).then_inc(rows_rms, 1)
                for t in range(H):
                    act.wait_ge(units_used, base_ord[f"mix{l}"] + Z0 + t + 1)
                    A(zs[:, t, :], psum[:, t % 4, 0:T], ACT.Silu).then_inc(act_evac, 1)
                    high_part(f"mix{l}", Z0 + t + SPLIT)
                silu_qkv(2 * H)

                def gates(n0, n1):
                    for t in range(n0, n1):
                        act.wait_ge(units_used, base_ord[f"mix{l}"] + GATE0 + t + 1)
                        A(gs[:, t, :], psum[:, (GATE0 + t) % 4, 0:T], ACT.Sigmoid).then_inc(act_evac, 1)
                        if GATE0 + t + SPLIT < N_PROJ_SPLIT:
                            high_part(f"mix{l}", GATE0 + t + SPLIT)

                gates(0, 1)
                n = 1
                for v in range(1, LEVELS):
                    act.wait_ge(b_mm, (LEVELS - 1) * l + v)
                    A(units(8), pair(4), ACT.Copy).then_inc(b_taken, 1)
                    gates(n, n + 1 + v % 2)
                    n += 1 + v % 2
                gates(10, 11)
                act.wait_ge(w_mm, l + 1)
                A(units(8), pair(4), ACT.Copy).then_inc(w_taken, 1)
                gates(11, 13)
                for j in range(CT):
                    act.wait_ge(ln_cen, CT * l + j + 1)
                    A(work[:, 4 + j, 512:512 + T], c[:, j, :], ACT.Square).then_inc(ln_sq, 1)
                act.wait_ge(os_taken, 2 * l + 2)
                act.wait_ge(samp_vn, 2 * l + 2)
                for h in range(H):
                    A(work[:, 4 + h, 0:T], qkv[:, 8 + h, :], ACT.Square).then_inc(o_squares, 1)
                gates(13, 14)
                warm(ACT.Sqrt)
                act.wait_ge(ln_var, l + 1)
                A(rstd[:, :], psum[:, 7, 0:T], ACT.Sqrt, scale=1.0 / (CT * P), bias=par("eps", 0)).then_inc(ln_rms, 1)
                act.wait_ge(rows_sum, 2 * l + 2)
                A(o_rstd[0:H, :], psum[0:H, 6, 0:T], ACT.Sqrt, scale=1.0 / P, bias=par("eps", 0)[0:H, :]).then_inc(rows_rms, 1)
                warm(ACT.Silu)
                for j in range(CT):
                    act.wait_ge(ln_norm, CT * l + j + 1)
                    A(c[:, j, :], c[:, j, :], ACT.Silu, scale=par("ln_g", l * CT + j), bias=par("ln_b", l * CT + j)).then_inc(c_done, 1)
                gates(14, 16)
                for k in range(KD):
                    act.wait_ge(merged_done, KD * l + k + 1)
                    A(x_hi[:, k, :], hT[:, k, :], ACT.Copy).then_inc(x_hi_done, 1)
                    if k < SPLIT:
                        high_part(f"mix{l}", N_PROJ + N_MIX + k)
                for t in range(SPLIT, N_WO):
                    high_part(f"mix{l}", N_PROJ + N_MIX + t)
                model_squares(2 * l + 1)
                model_rms(2 * l + 1)
                if l == 0:
                    high_part("ffn", 0)
                    for k in range(KD):
                        act.wait_ge(h_done, KD + k + 1)
                        A(x_hi[:, k, :], hT[:, k, :], ACT.Copy).then_inc(x_hi_done, 1)
                    for u in range(1, 2 * FT + 2):
                        if u < 2 * FT:
                            high_part("ffn", u)
                        if u % 2 == 0 and u >= 4 or u == 2 * FT + 1:
                            f = (u - 4) // 2 if u < 2 * FT + 1 else FT - 1
                            act.wait_ge(units_used, base_ord["ffn"] + 2 * f + 1)
                            if f >= 3:
                                act.wait_ge(act_done, f - 2)
                            A(silu_g[:, f % 3, :], psum[:, 2 * (f % 3), 0:T], ACT.Silu).then_inc(silu_done, 1)
                else:
                    for m in range(3):
                        act.wait_ge(h_tr, m + 1)
                        A(h_tok[:, m, :], psum[:, (0, 2, 6)[m]:(0, 2, 6)[m] + 2, :].rearrange("p b n -> p (b n)"), ACT.Copy).then_inc(h_tok_done, 1)
                    act.wait_ge(gates_exp_in, 1)
                    A(rt[:, 3, 0:3], rt[:, 2, 0:3], ACT.Exp).then_inc(gates_exp, 1)

                    def gathered(job, part):
                        act.wait_ge(gather_mm, job * 2 + (part + 1))
                        A(h_hi[:, part * 4 * CAP:(part + 1) * 4 * CAP], psum[:, part, 0:4 * CAP], ACT.Copy).then_inc(h_hi_done, 1)

                    gathered(0, 0)
                    act.wait_ge(jobs_done, 1)
                    n_jobs = act.value_load(jobs[0:1, MAX_JOBS:MAX_JOBS + 1], min_val=2, max_val=MAX_JOBS)
                    with act.Fori(0, n_jobs) as job:
                        for u in range(N_FFN):
                            act.wait_ge(slot_loaded[u % RING], job * (16 * N_FFN // RING) + 16 * (n0[u % RING] + u // RING + 1))
                            act.wait_ge(units_used, job * N_FFN + (base_ord["experts"] + u + 1 - SPLIT))
                            A(w_hi[:, (n_split + u) % SPLIT, :], ring[:, u % RING, :, :].rearrange("p k n -> p (k n)"), ACT.Copy).then_inc(hi_done, 1)
                            if u == 1:
                                gathered(job, 1)
                            ch = (u - 4) // 4
                            if u % 4 == 0 and 0 <= ch < NCH:
                                act.wait_ge(units_used, job * N_FFN + (base_ord["experts"] + 4 * ch + 2))
                                if ch >= 2:
                                    act.wait_ge(chunk_done, job * NCH + (ch - 1))
                                A(silu_job[:, ch % 2, :], psum[0:CAP, ch % 2, 0:CHUNK], ACT.Silu).then_inc(chunk_silu, 1)
                            ch = (u - 10) // 4
                            if u % 4 == 2 and 0 <= ch < NCH:
                                act.wait_ge(act_tr, job * NCH + (ch + 1))
                                A(act_hi[:, 2 * ch:2 * ch + 2, :].rearrange("p f s -> p (f s)"), psum[:, 4 + ch % 2, 0:2 * CAP], ACT.Copy).then_inc(act_hi_done, 1)
                        act.wait_ge(units_used, job * N_FFN + (base_ord["experts"] + N_FFN))
                        A(y_tok, psum[0:CAP, 6:8, :].rearrange("p b n -> p (b n)"), ACT.Copy).then_inc(y_tok_done, 1)
                        gathered(job + 1, 0)
                    act.wait_ge(down_taken, n_jobs * KD + KD)
            model_squares(2 * DEPTH)
            model_rms(2 * DEPTH)

        @block.vector
        def _(dve):
            V = nc.vector

            def q_prod(t):
                return rows32[:, t % 4 // 2, 32 * (t % 2):32 * (t % 2) + 32].rearrange("p (b n) -> p b n", b=NB)
            dve_n = [0]

            def settle(ins):
                dve_n[0] += 1
                ins.then_inc(dve_step, 1)
                dve.wait_ge(dve_step, dve_n[0])

            def low_part(section, i):
                p = first_position(section) + i
                n = split_ord[p]
                dve.wait_ge(hi_done, n + 1)
                V.tensor_tensor(w_lo[:, n % SPLIT, :], ring[:, p % RING, :, :].rearrange("p k n -> p (k n)"),
                                w_hi[:, n % SPLIT, :], ALU.subtract).then_inc(lo_done, 1)

            def x_low(stage, k):
                dve.wait_ge(x_hi_done, KD * stage + k + 1)
                V.tensor_tensor(x_lo[:, k, :], hT[:, k, :], x_hi[:, k, :], ALU.subtract).then_inc(x_lo_done, 1)

            def model_norm(l2, g_name, g_at, out, done, split_stage=None):
                dve.wait_ge(rms_done, l2 + 1)
                settle(V.reciprocal(rstd[:, :], rstd[:, :]))
                for k in range(KD):
                    V.scalar_tensor_tensor(out[:, k, :], xT[:, k, :], par(g_name, g_at + k), rstd[:, :], ALU.mult, ALU.mult).then_inc(done, 1)
                    if split_stage is not None and k:
                        x_low(split_stage, k - 1)
                if split_stage is not None:
                    x_low(split_stage, KD - 1)

            dve.wait_ge(consts_loaded, 32)
            dve.wait_ge(x_loaded, 16)
            for l in range(DEPTH):
                model_norm(2 * l, "norm1", l * KD, hT, h_done)
                dve.wait_ge(ab_done, l + 1)
                settle(V.tensor_copy(ab_tok, psum[:, 4, 0:24]))
                ab = ab_tok.rearrange("p (t n) -> p t n", t=3)
                settle(V.tensor_tensor(t_a.rearrange("p (t n) -> p t n", t=3), ab[:, :, 0:H],
                                       par_block("dt_bias", l, H).rearrange("p (a n) -> p a n", a=1).broadcast_to([P, 3, H]), ALU.add))
                V.scalar_tensor_tensor(t_abs, t_a, -1.0, t_a, ALU.mult, ALU.max).then_inc(soft_in, 1)
                dve.wait_ge(soft_exp, 4 * (l + 1))
                settle(V.scalar_tensor_tensor(g_tok, t_a, 0.0, t_ln, ALU.max, ALU.add))
                settle(V.scalar_tensor_tensor(g_tok.rearrange("p (t n) -> p t n", t=3), g_tok.rearrange("p (t n) -> p t n", t=3), -1.0,
                                              nea.rearrange("p (a n) -> p a n", a=1).broadcast_to([P, 3, H]), ALU.mult, ALU.mult))
                settle(V.tensor_scalar(b_exp, b_exp, 1.0, None, ALU.add))
                settle(V.reciprocal(beta, b_exp))
                smask = par("samp_mask", 0, NB)
                for i, col in enumerate((g_tok, beta)):
                    V.tensor_tensor(samp_rhs[:, i * 32:(i + 1) * 32].rearrange("p (b h) -> p b h", h=H),
                                    smask.rearrange("p (b a) -> p b a", a=1).broadcast_to([P, NB, H]),
                                    col[:, 8:12].rearrange("p (a h) -> p a h", a=1).broadcast_to([P, NB, H]), ALU.mult)
                V.tensor_tensor(units(0), triu.rearrange("p (a i) -> p a i", a=1).broadcast_to([P, U, P]),
                                g_tok[:, 0:U].rearrange("p (u a) -> p u a", a=1).broadcast_to([P, U, P]), ALU.mult).then_inc(g_done, 1)
                def glu(j):
                    dve.wait_ge(glu_sig, CT * l + j + 1)
                    if j == 0:
                        dve.wait_ge(dw_loaded, 16 * (l + 1))
                        dve.wait_ge(zeros_set, 2 * l + 1)
                    b = (GLU0 + 2 * j) % 4
                    V.tensor_tensor(u_pad[:, j, DW - 1:], psum[:, b, 0:TP], glu_gate(j)[:, 0:TP], ALU.mult)
                    V.tensor_tensor(u_win[:, j, :, DW - 1], psum[:, b, TP:T], glu_gate(j)[:, TP:T], ALU.mult).then_inc(glu_done, 1)

                def conv_taps(first, last):
                    for tap in range(first, last):
                        for j in range(CT):
                            w = par("dw_w", (l * CT + j) * DW + tap)
                            if tap == 0:
                                ins = V.tensor_scalar(c[:, j, 0:TP], u_pad[:, j, 0:TP], w, par("dw_b", l * CT + j), ALU.mult, ALU.add)
                            else:
                                ins = V.scalar_tensor_tensor(c[:, j, 0:TP], u_pad[:, j, tap:tap + TP], w, c[:, j, 0:TP], ALU.mult, ALU.add)
                        settle(ins)

                glu(0)
                dve.wait_ge(g_rows, l + 1)
                V.tensor_copy(tables[:, 32:96], psum[:, 4, 64:128])
                settle(V.tensor_copy(tables[:, 0:16], psum[:, 4, 32:48]))
                V.tensor_tensor(gd, gl, gcc, ALU.subtract)
                settle(V.tensor_tensor(units(1), pair(6), gcc.rearrange("p (u a) -> p u a", a=1).broadcast_to([P, U, P]), ALU.subtract))
                settle(V.tensor_scalar(work[:, 2, :], work[:, 1, :], 0.0, None, ALU.max))
                V.tensor_scalar(work[:, 1, :], work[:, 1, :], 0.0, None, ALU.min).then_inc(l_args, 1)
                for j in range(1, CT):
                    glu(j)
                dve.wait_ge(exp_small, 2 * l + 2)
                settle(V.scalar_tensor_tensor(nbeg, beta[:, 0:U], -1.0, egc, ALU.mult, ALU.mult))
                def conv_qkv(t0):
                    for tap in range(QW):
                        for t in range(t0, t0 + 4):
                            if tap == 0:
                                dve.wait_ge(act_evac, 32 * l + t + 1)
                            w = par("qk_w", (l * QT + t) * QW + tap)
                            if tap == 0:
                                ins = V.tensor_scalar(qkv[:, t, 0:TP], q_pad[:, t, 0:TP], w, None, ALU.mult)
                            else:
                                ins = V.scalar_tensor_tensor(qkv[:, t, 0:TP], q_pad[:, t, tap:tap + TP], w, qkv[:, t, 0:TP], ALU.mult, ALU.add)
                        settle(ins)
                    for t in range(t0, t0 + 4):
                        qprod = q_prod(t)
                        ins = V.tensor_tensor(qprod, q_win[:, t], par("qk_w", (l * QT + t) * QW, QW).rearrange("p (a n) -> p a n", a=1).broadcast_to([P, NB, QW]), ALU.mult)
                    settle(ins)
                    for t in range(t0, t0 + 4):
                        qprod = q_prod(t)
                        V.tensor_reduce(qkv[:, t, TP:T], qprod, AX_X, ALU.add).then_inc(qconv_done, 1)

                dve.wait_ge(glu_done, CT * (l + 1))
                conv_taps(0, 7)
                conv_qkv(0)
                conv_taps(7, 10)
                conv_qkv(H)
                conv_qkv(2 * H)
                dve.wait_ge(rows_rms, 2 * l + 1)
                V.reciprocal(rstd[0:2 * H, :], rstd[0:2 * H, :]).then_inc(rows_recip, 1)
                for i in range(2):
                    dve.wait_ge(rows_spread, 3 * l + i + 1)
                    group = qkv[:, i * H:(i + 1) * H, :]
                    V.scalar_tensor_tensor(group, group, float(P) ** -0.5 if i == 0 else 1.0, psum[:, 4:8, 0:T], ALU.mult, ALU.mult).then_inc(qk_normed, 1)
                conv_taps(10, 13)
                dve.wait_ge(qk_normed, 2 * l + 2)
                dve.wait_ge(pool_l, l + 1)
                dve.wait_ge(gram_done, 2 * l + 1)
                V.tensor_tensor(units(7), pair(4), units(2), ALU.mult).then_inc(gram_taken, 1)
                dve.wait_ge(gram_done, 2 * l + 2)
                V.tensor_tensor(units(1), pair(6), units(1), ALU.mult).then_inc(gram_taken, 1)
                q4 = qkv[:, 0:H, 0:TP].rearrange("p h (c i) -> p c h i", c=NC)
                w04 = work[:, 0, :].rearrange("p (c h i) -> p c h i", c=NC, h=H)
                for cc in range(NC):
                    ins = V.tensor_tensor(w04[:, cc], w04[:, cc], q4[:, cc], ALU.mult)
                settle(ins)
                ib = ident.rearrange("p (a i) -> p a i", a=1).broadcast_to([P, U, P])
                dve.wait_ge(level_masked, LEVELS * l + 1)
                V.tensor_tensor(units(3), ib, units(5), ALU.subtract)
                dve.wait_ge(first_tr, l + 1)
                V.tensor_tensor(units(4), ib, pair(4), ALU.subtract).then_inc(tu_done, 1)
                for v in range(1, LEVELS):
                    conv_taps(10 + 3 * v, 13 + 3 * v)
                    n_pq = (2 * (LEVELS - 1) - 1) * l + 2 * (v - 1)
                    dve.wait_ge(pq_mm, n_pq + 1)
                    ins = V.tensor_tensor(units(4), units(4), pair(6), ALU.subtract)
                    if v < LEVELS - 1:
                        dve.wait_ge(pq_mm, n_pq + 2)
                        ins = V.tensor_tensor(units(3), units(3), pair(4), ALU.subtract)
                    ins.then_inc(tu_done, 1)
                prod = work[:, 2, 0:CT * NB * DW].rearrange("p (c b n) -> p c b n", c=CT, b=NB)
                for j in range(CT):
                    ins = V.tensor_tensor(prod[:, j], u_win[:, j], par("dw_w", (l * CT + j) * DW, DW).rearrange("p (a n) -> p a n", a=1).broadcast_to([P, NB, DW]), ALU.mult)
                settle(ins)
                for j in range(CT):
                    ins = V.tensor_reduce(c[:, j, TP:T], prod[:, j], AX_X, ALU.add)
                settle(ins)
                for j in range(CT):
                    V.tensor_scalar(c[:, j, TP:T], c[:, j, TP:T], par("dw_b", l * CT + j), None, ALU.add).then_inc(conv_out, 1)
                bc = lambda col: col.rearrange("p (u a) -> p u a", a=1).broadcast_to([P, U, P])
                dve.wait_ge(kv_tr, l + 1)
                V.tensor_tensor(units(5), pair(4), bc(nbeg), ALU.mult)
                V.tensor_tensor(units(7), pair(4), bc(kdsc), ALU.mult)
                V.tensor_tensor(units(6), pair(6), bc(beta[:, 0:U]), ALU.mult).then_inc(kv_taken, 1)
                q_s = qkv[:, 0:H, TP:T].rearrange("p h b -> p b h")
                kk = qkv[:, H:2 * H, TP:T].rearrange("p h b -> p b h")
                vv = qkv[:, 2 * H:3 * H, TP:T].rearrange("p h b -> p b h")

                def bh(t):
                    return t.rearrange("p (b h) -> p b h", h=H)

                V.tensor_copy(bh(k_s), kk)
                V.tensor_tensor(bh(s_prod), q_s, kk, ALU.mult).then_inc(samp_vn, 1)
                for cc in range(NC):
                    dve.wait_ge(vn_mm, NC * l + cc + 1)
                    V.tensor_copy(work[:, 2, cc * 512:cc * 512 + 512], psum[:, 6, :]).then_inc(vn_taken, 1)
                    dve.wait_ge(os_mm, 2 * NC * l + 2 * cc + 1)
                    V.tensor_copy(qkv[:, 8:12, cc * P:(cc + 1) * P], psum[:, 4, :].rearrange("p (h i) -> p h i", h=H))
                    dve.wait_ge(os_mm, 2 * NC * l + 2 * cc + 2)
                    if cc == 0:
                        V.tensor_copy(work[:, 3, 0:512], psum[:, 5, :]).then_inc(os_taken, 1)
                    else:
                        for h in range(H):
                            ins = V.scalar_tensor_tensor(units(3)[:, h, :], units(3)[:, h, :], egl[:, cc * H + h:cc * H + h + 1],
                                                         psum[:, 5, h * P:(h + 1) * P], ALU.mult, ALU.add)
                        ins.then_inc(os_taken, 1)
                dve.wait_ge(samp_mm, l + 1)
                sk = psum[:, 7, 0:64].rearrange("p (u n) -> p u n", n=2)
                settle(V.tensor_tensor(vn_s, sk[:, :, 1], egs, ALU.mult))
                settle(V.tensor_tensor(bh(vn_s), vv, bh(vn_s), ALU.subtract))
                settle(V.tensor_tensor(vn_s, vn_s, betas, ALU.mult))
                V.tensor_tensor(o_t, sk[:, :, 0], egs, ALU.mult)
                settle(V.tensor_tensor(qk_s, psum[:, 7, 64:96], vn_s, ALU.mult))
                V.tensor_tensor(vv, bh(o_t), bh(qk_s), ALU.add).then_inc(samp_vn, 1)
                dve.wait_ge(samp_tr, l + 1)
                settle(V.tensor_copy(rows32[0:32, 0, :], psum[0:32, 7, 128:256]))
                V.tensor_copy(rows32[0:32, 1, :], psum[0:32, 7, 256:384]).then_inc(samp_rows, 1)
                dve.wait_ge(ln_sum, l + 1)
                for j in range(CT):
                    V.scalar_tensor_tensor(c[:, j, :], psum[:, 6, 0:T], -1.0 / (CT * P), c[:, j, :], ALU.mult, ALU.add).then_inc(ln_cen, 1)
                dve.wait_ge(state_out, 16 * (6 * l + 5))
                V.tensor_tensor(vmask[0:32], rows32[0:32, 0, :].rearrange("p (a d) -> p a d", a=1).broadcast_to([32, 32, P]),
                                ident[0:32, 0:32].rearrange("p (u a) -> p u a", a=1).broadcast_to([32, 32, P]), ALU.mult).then_inc(samp_vm, 1)
                dve.wait_ge(s0_scaled, l + 1)
                for g in range(8):
                    dve.wait_ge(outer_mm, 8 * l + g + 1)
                    blk = s0[:, 4 * g:4 * g + 4, :].rearrange("p u d -> p (u d)")
                    V.tensor_tensor(blk, blk, psum[:, 4 + g % 2, :], ALU.add).then_inc(outer_taken, 1)
                dve.wait_ge(ln_rms, l + 1)
                settle(V.reciprocal(rstd[:, :], rstd[:, :]))
                for j in range(CT):
                    V.tensor_tensor(c[:, j, :], c[:, j, :], rstd[:, :], ALU.mult).then_inc(ln_norm, 1)
                dve.wait_ge(rows_rms, 2 * l + 2)
                V.reciprocal(o_rstd[0:H, :], o_rstd[0:H, :]).then_inc(rows_recip, 1)
                dve.wait_ge(rows_spread, 3 * l + 3)
                o_all = qkv[:, 2 * H:3 * H, :]
                settle(V.scalar_tensor_tensor(o_all, o_all, par("o_g", l), psum[:, 4:8, 0:T], ALU.mult, ALU.mult))
                V.tensor_tensor(o_all, o_all, zs[:, :, :], ALU.mult).then_inc(o_done, 1)
                for t in range(KD):
                    dve.wait_ge(units_used, base_ord[f"mix{l}"] + N_PROJ + t + 1)
                    settle(V.tensor_tensor(gs[:, t, :], gs[:, t, :], psum[:, 2 * (t % 2), 0:T], ALU.mult))
                    settle(V.tensor_tensor(gs[:, KD + t, :], gs[:, KD + t, :], psum[:, 2 * (t % 2) + 1, 0:T], ALU.mult))
                    V.tensor_tensor(hT[:, t, :], gs[:, t, :], gs[:, KD + t, :], ALU.add).then_inc(merged_done, 1)
                    if t:
                        x_low(3 * l + 1, t - 1)
                        if t <= SPLIT:
                            low_part(f"mix{l}", N_PROJ + N_MIX + t - 1)
                x_low(3 * l + 1, KD - 1)
                for t in range(KD):
                    dve.wait_ge(units_used, base_ord[f"mix{l}"] + N_PROJ + N_MIX + t + 1)
                    V.tensor_tensor(xT[:, t, :], xT[:, t, :], psum[:, t % 4, 0:T], ALU.add).then_inc(x_done, 1)
                    if SPLIT + t < N_WO:
                        low_part(f"mix{l}", N_PROJ + N_MIX + SPLIT + t)
                dve.wait_ge(x_done, KD * (l + 1))
                if l == 0:
                    low_part("ffn", 0)
                model_norm(2 * l + 1, "norm2", l * KD, hT, h_done, 2 if l == 0 else None)
                if l == 0:
                    for u in range(1, 2 * FT + 2):
                        if u < 2 * FT:
                            low_part("ffn", u)
                        if u % 2 == 0 and u >= 4 or u == 2 * FT + 1:
                            f = (u - 4) // 2 if u < 2 * FT + 1 else FT - 1
                            dve.wait_ge(silu_done, f + 1)
                            dve.wait_ge(units_used, base_ord["ffn"] + 2 * f + 2)
                            V.tensor_tensor(act_all[:, f, :], silu_g[:, f % 3, :], psum[:, 2 * (f % 3) + 1, 0:T], ALU.mult).then_inc(act_done, 1)
                    for t in range(KD):
                        if t % 4 == 3:
                            dve.wait_ge(units_used, base_ord["ffn"] + 2 * FT + (t + 1) * FT // KD)
                        else:
                            dve.wait_ge(down_done, t + 1 - t // 4)
                        if t >= 1:
                            dve.wait_ge(down_taken, t)
                        V.tensor_tensor(xT[:, t, :], xT[:, t, :], psum[:, 6 + t % 2, 0:T], ALU.add).then_inc(down_taken, 1)
                    dve.wait_ge(down_taken, KD)
                else:
                    dve.wait_ge(router_mm, 1)
                    lg = psum[:, 4, 0:24]
                    r3 = lambda t: t.rearrange("p (t e) -> p t e", e=NE)
                    c3 = lambda t: t.rearrange("p (t a) -> p t a", a=1).broadcast_to([P, 3, NE])
                    iota = par("iota", 0, 24)
                    logit, oh1, oh2, tmp, sent, rank = rl, rt[:, 5, :], rt[:, 6, :], rt[:, 7, :], rt[:, 8, :], rt[:, 9, :]
                    settle(V.tensor_copy(logit, lg))
                    settle(V.tensor_reduce(rt[:, 0, 0:3], r3(logit), AX_X, ALU.max))

                    def first_of(value, onehot):
                        settle(V.tensor_tensor(r3(tmp), r3(logit), c3(value), ALU.is_lt))
                        settle(V.scalar_tensor_tensor(tmp, tmp, 64.0, iota, ALU.mult, ALU.add))
                        settle(V.tensor_reduce(rt[:, 4, 0:3], r3(tmp), AX_X, ALU.min))
                        settle(V.tensor_tensor(r3(onehot), r3(iota), c3(rt[:, 4, 0:3]), ALU.is_equal))

                    first_of(rt[:, 0, 0:3], oh1)
                    settle(V.scalar_tensor_tensor(logit, oh1, -3.0e38, logit, ALU.mult, ALU.add))
                    settle(V.tensor_reduce(rt[:, 1, 0:3], r3(logit), AX_X, ALU.max))
                    first_of(rt[:, 1, 0:3], oh2)
                    V.tensor_tensor(rt[:, 2, 0:3], rt[:, 1, 0:3], rt[:, 0, 0:3], ALU.subtract).then_inc(gates_exp_in, 1)
                    settle(V.tensor_tensor(sent, oh1, oh2, ALU.add))
                    V.tensor_tensor(sent, sent, par("keep", 0, 24), ALU.mult).then_inc(chosen, 1)
                    slots, gates = rt[:, 10, 0:6], rt[:, 10, 6:12]
                    settle(V.memset(scan[:, :, :], 0.0))
                    dve.wait_ge(ranks_mm, 1)
                    count = rt[:, 0, 8:16]
                    n_of, s1, s2, s3 = (scan[:, i, NE:2 * NE] for i in range(4))
                    V.tensor_copy(rank, psum[:, 5, 0:24])
                    settle(V.tensor_copy(count, psum[:, 5, 24:32]))
                    settle(V.tensor_scalar(n_of, count, 0.0, None, ALU.is_gt))
                    settle(V.memset(scan[:, 0, NE:NE + 1], 1.0))
                    for full in range(1, -(-T // CAP)):
                        settle(V.scalar_tensor_tensor(n_of, count, float(full * CAP), n_of, ALU.is_gt, ALU.add))
                    for i, step in enumerate((1, 2, 4)):
                        settle(V.tensor_tensor(scan[:, i + 1, NE:2 * NE], scan[:, i, NE:2 * NE], scan[:, i, NE - step:2 * NE - step], ALU.add))
                    ends = rt[:, 0:5, :].rearrange("p a b -> p (a b)")[:, 0:MAX_JOBS * NE].rearrange("p (j e) -> p j e", e=NE)
                    settle(V.tensor_tensor(s1, s3, n_of, ALU.subtract))
                    settle(V.scalar_tensor_tensor(r3(rank), s1.rearrange("p (a e) -> p a e", a=1).broadcast_to([P, 3, NE]), float(CAP), r3(rank), ALU.mult, ALU.add))
                    for i, oh in enumerate((oh1, oh2)):
                        settle(V.tensor_tensor(tmp, oh, rank, ALU.mult))
                        settle(V.tensor_reduce(slots[:, 3 * i:3 * i + 3], r3(tmp), AX_X, ALU.add))
                    settle(V.tensor_tensor(slots, slots, par("drop", 0, 6), ALU.add))

                    for m in range(3):
                        ins = V.tensor_scalar(take[:, m, :], par("slot_row", 0, CAP), slots[:, m:m + 1], None, ALU.is_equal)
                    settle(ins)
                    for m in range(3):
                        ins = V.scalar_tensor_tensor(take[:, m, :], par("slot_row", 0, CAP), slots[:, 3 + m:4 + m], take[:, m, :],
                                                     ALU.is_equal, ALU.add)
                    ins.then_inc(take_done, 1)
                    dve.wait_ge(gates_exp, 1)
                    settle(V.tensor_scalar(rt[:, 0, 0:3], rt[:, 3, 0:3], 1.0, None, ALU.add))
                    settle(V.reciprocal(gates[:, 0:3], rt[:, 0, 0:3]))
                    settle(V.tensor_tensor(gates[:, 3:6], rt[:, 3, 0:3], gates[:, 0:3], ALU.mult))
                    settle(V.tensor_tensor(ends, s3.rearrange("p (a e) -> p a e", a=1).broadcast_to([P, MAX_JOBS, NE]),
                                           par("job_no", 0, MAX_JOBS * NE).rearrange("p (j e) -> p j e", e=NE), ALU.is_le))
                    settle(V.tensor_reduce(scan[:, 0:2, :].rearrange("p a b -> p (a b)")[:, 0:MAX_JOBS], ends, AX_X, ALU.add))
                    V.tensor_copy(jobs[:, MAX_JOBS:MAX_JOBS + 1], scan[:, 3, 2 * NE - 1:2 * NE])
                    V.tensor_copy(jobs[:, 0:MAX_JOBS], scan[:, 0:2, :].rearrange("p a b -> p (a b)")[:, 0:MAX_JOBS]).then_inc(jobs_done, 1)
                    rows_in = work[:, 0:2, :].rearrange("p a b -> p (a b)")[:, 0:12 * P].rearrange("p (v i) -> p v i", i=P)
                    V.tensor_tensor(rows_in, ident.rearrange("p (a i) -> p a i", a=1).broadcast_to([P, 12, P]),
                                    rt[:, 10, 0:12].rearrange("p (v a) -> p v a", a=1).broadcast_to([P, 12, P]), ALU.mult).then_inc(rows_rhs, 1)
                    V.tensor_copy(slot_no[:, :], par("slot_col", 0))
                    dve.wait_ge(rows_mm, 1)
                    for v in range(4):
                        row = psum[:, 2:5, :].rearrange("p b n -> p (b n)")[:, v * 3 * P:(v + 1) * 3 * P]
                        V.tensor_copy(rows4[:, v, 0:TP], row[:, 0:TP])
                        ins = V.tensor_copy(rows4[:, v, TP:T], row[:, 2 * P + SAMPLE_ROW:3 * P])
                    ins.then_inc(rows_done, 1)
                    dve.wait_ge(rows_done, 1)
                    dve.wait_ge(jobs_done, 1)
                    n_jobs = dve.value_load(jobs[0:1, MAX_JOBS:MAX_JOBS + 1], min_val=2, max_val=MAX_JOBS)
                    def h_low(job, part):
                        dve.wait_ge(h_hi_done, job * 2 + (part + 1))
                        cols = slice(part * 4 * CAP, (part + 1) * 4 * CAP)
                        V.tensor_tensor(h_lo[:, cols], psum[:, part, 0:4 * CAP], h_hi[:, cols], ALU.subtract).then_inc(h_job_done, 1)

                    h_low(0, 0)
                    with dve.Fori(0, n_jobs) as job:
                        for u in range(N_FFN):
                            dve.wait_ge(hi_done, job * N_FFN + (n_split + u + 1))
                            V.tensor_tensor(w_lo[:, (n_split + u) % SPLIT, :], ring[:, u % RING, :, :].rearrange("p k n -> p (k n)"),
                                            w_hi[:, (n_split + u) % SPLIT, :], ALU.subtract).then_inc(lo_done, 1)
                            if u == 1:
                                h_low(job, 1)
                            ch = (u - 6) // 4
                            if u % 4 == 2 and 0 <= ch < NCH:
                                dve.wait_ge(chunk_silu, job * NCH + (ch + 1))
                                dve.wait_ge(units_used, job * N_FFN + (base_ord["experts"] + 4 * ch + 4))
                                if ch >= 2:
                                    dve.wait_ge(act_tr, job * NCH + (ch - 1))
                                V.tensor_tensor(prod_job[:, ch % 2, :], silu_job[:, ch % 2, :], psum[0:CAP, 2 + ch % 2, 0:CHUNK], ALU.mult).then_inc(chunk_done, 1)
                            ch = (u - 11) // 4
                            if u % 4 == 3 and 0 <= ch < NCH:
                                dve.wait_ge(act_hi_done, job * NCH + (ch + 1))
                                V.tensor_tensor(act_lo[:, 2 * ch:2 * ch + 2, :].rearrange("p f s -> p (f s)"), psum[:, 4 + ch % 2, 0:2 * CAP],
                                                act_hi[:, 2 * ch:2 * ch + 2, :].rearrange("p f s -> p (f s)"), ALU.subtract).then_inc(act_lo_done, 1)
                        V.tensor_scalar(slots, slots, float(-CAP), None, ALU.add).then_inc(put_step, 1)
                        dve.wait_ge(put_step, job * 4 + 1)
                        for m in range(3):
                            ins = V.tensor_scalar(take[:, m, :], par("slot_row", 0, CAP), slots[:, m:m + 1], None, ALU.is_equal)
                        ins.then_inc(put_step, 1)
                        dve.wait_ge(put_step, job * 4 + 2)
                        for m in range(3):
                            ins = V.scalar_tensor_tensor(take[:, m, :], par("slot_row", 0, CAP), slots[:, 3 + m:4 + m], take[:, m, :],
                                                         ALU.is_equal, ALU.add)
                        ins.then_inc(take_done, 1)
                        slot_c = slot_no[0:CAP, :]
                        V.scalar_tensor_tensor(put, rows4[0:CAP, 0, :], slot_c, rows4[0:CAP, 2, :], ALU.is_equal, ALU.mult)
                        V.scalar_tensor_tensor(put_2, rows4[0:CAP, 1, :], slot_c, rows4[0:CAP, 3, :], ALU.is_equal, ALU.mult).then_inc(put_step, 1)
                        dve.wait_ge(put_step, job * 4 + 3)
                        V.tensor_tensor(put, put, put_2, ALU.add).then_inc(put_done, 1)
                        V.tensor_scalar(slot_no[:, :], slot_no[:, :], float(CAP), None, ALU.add).then_inc(put_step, 1)
                        dve.wait_ge(put_step, job * 4 + 4)
                        h_low(job + 1, 0)
                        for t in range(KD):
                            dve.wait_ge(scatter_mm, job * KD + (t + 1))
                            V.tensor_tensor(xT[:, t, :], xT[:, t, :], psum[:, 2 + t % 4, 0:T], ALU.add).then_inc(down_taken, 1)
                    dve.wait_ge(down_taken, n_jobs * KD + KD)
            model_norm(2 * DEPTH, "final", 0, hT, y_done)

        @block.tensor
        def _(pe):
            M = nc.tensor.matmul

            def arrived(section, i):
                p = first_position(section) + i
                pe.wait_ge(slot_loaded[p % RING], 16 * (uses_before(p) + 1))
                return ring[:, p % RING, :, :]

            def parts(section, i):
                p = first_position(section) + i
                n = split_ord[p]
                pe.wait_ge(*low_count(p))
                return [w[:, n % SPLIT, :].rearrange("p (k n) -> p k n", n=P) for w in (w_hi, w_lo)]

            def split_products(out, lhs, rhs, start, stop):
                for n, (x, w) in enumerate(((0, 0), (0, 1), (1, 0))):
                    last = M(out, lhs[x], rhs[w], start=(start and n == 0), stop=(stop and n == 2))
                return last

            def split_tile(out, w, stage):
                for k in range(KD):
                    pe.wait_ge(x_lo_done, KD * stage + k + 1)
                    last = split_products(out, [h[:, k, :] for h in w], [h[:, k, :] for h in (x_hi, x_lo)], k == 0, k == KD - 1)
                return last

            def model_sums(l2):
                for k in range(KD):
                    pe.wait_ge(squares_done, KD * l2 + k + 1)
                    last = M(psum[:, 5, 0:T], ones, sq[:, k, :], start=(k == 0), stop=(k == KD - 1))
                last.then_inc(sums_done, 1)

            pe.wait_ge(consts_loaded, 32)
            for l in range(DEPTH):
                section = f"mix{l}"
                model_sums(2 * l)

                def project(*tiles):
                    for t in tiles:
                        w = parts(section, t) if t < N_PROJ_SPLIT else arrived(section, t)
                        if 4 <= t < 4 + QKV0:
                            pe.wait_ge(glu_done, CT * l + (t - 4 - GLU0) // 2 + 1)
                        elif t >= 4 + QKV0:
                            pe.wait_ge(act_evac, 32 * l + t - 4 - QKV0 + 1)
                        if t < N_PROJ_SPLIT:
                            last = split_tile(psum[:, t % 4, 0:T], w, 3 * l)
                        else:
                            for k in range(KD):
                                last = M(psum[:, t % 4, 0:T], w[:, k, :], hT[:, k, :], start=(k == 0), stop=(k == KD - 1))
                        last.then_inc(units_used, 1)

                for m, t0 in enumerate((0, P, T - P)):
                    for k in range(KD):
                        if m == 0:
                            pe.wait_ge(h_done, 2 * KD * l + k + 1)
                        last = M(psum[:, 4, m * 8:m * 8 + 8], hT[:, k, t0:t0 + P], par_block("w_ab", l, KD * 8)[:, k * 8:(k + 1) * 8],
                                 start=(k == 0), stop=(k == KD - 1))
                last.then_inc(ab_done, 1)
                project(0, 1, 2)
                pe.wait_ge(g_done, l + 1)
                for b in range(2):
                    M(psum[:, 6 + b, :], ones, work[:, 0, b * 512:b * 512 + 512], start=True, stop=True)
                M(psum[:, 4, 32:40], triu, g_tok[:, 0:U], start=True, stop=True)
                M(psum[:, 4, 40:48], ones, g_tok[:, 0:U], start=True, stop=True)
                M(psum[:, 4, 64:128], ones, samp_rhs, start=True, stop=True).then_inc(g_rows, 1)
                project(*range(3, Z0))
                pick = par("pick", 0, 15)
                pe.wait_ge(l_args, l + 1)
                for t in range(2 * H):
                    pe.wait_ge(qk_squares, 2 * H * l + t + 1)
                    last = M(psum[0:2 * H, 4, 0:T], pick[:, 7 - t:15 - t], sq_qk[:, t, :], start=(t == 0), stop=(t == 2 * H - 1))
                last.then_inc(rows_sum, 1)
                project(20)

                def spread(rows, n, first):
                    for h in range(H):
                        last = M(psum[:, 4 + h, 0:T], ident[0:n, first + h:first + h + 1].broadcast_to([n, P]), rows[0:n, :], start=True, stop=True)
                    last.then_inc(rows_spread, 1)

                pe.wait_ge(rows_recip, 2 * l + 1)
                pe.wait_ge(exp_big, 3 * l + 1)
                spread(rstd, 2 * H, 0)
                project(21)
                pe.wait_ge(qk_normed, 2 * l + 1)
                spread(rstd, 2 * H, H)
                project(22)
                pe.wait_ge(qk_normed, 2 * (l + 1))

                def kq(first, h, cc):
                    return qkv[:, first + h, cc * P:(cc + 1) * P]

                for cc in range(NC):
                    for h in range(H):
                        last = M(psum[:, 4 + cc, h * P:(h + 1) * P], kq(H, h, cc), kq(H, h, cc), start=True, stop=True)
                last.then_inc(gram_done, 1)
                for cc in range(NC):
                    for h in range(H):
                        last = M(psum[:, 6 + cc, h * P:(h + 1) * P], kq(H, h, cc), kq(0, h, cc), start=True, stop=True)
                last.then_inc(gram_done, 1)
                project(23)
                pe.wait_ge(level_masked, LEVELS * l + 1)
                pe.wait_ge(gram_taken, 2 * l + 1)
                for u in range(U):
                    last = nc.tensor.transpose(pair(4)[:, u, :], units(5)[:, u, :], ident)
                last.then_inc(first_tr, 1)
                project(GATE0)
                t = GATE0 + 1
                for v in range(1, LEVELS):
                    pe.wait_ge(tu_done, LEVELS * l + v)
                    pe.wait_ge(level_masked, LEVELS * l + v + 1)
                    for u in range(U):
                        last = M(pair(4)[:, u, :], units(5 + v % 2)[:, u, :], units(4)[:, u, :], start=True, stop=True)
                    last.then_inc(b_mm, 1)
                    project(t)
                    pe.wait_ge(b_taken, (LEVELS - 1) * l + v)
                    if v == 1:
                        pe.wait_ge(gram_taken, 2 * l + 2)
                    for u in range(U):
                        last = M(pair(6)[:, u, :], units(3)[:, u, :], units(8)[:, u, :], start=True, stop=True)
                    last.then_inc(pq_mm, 1)
                    if v < LEVELS - 1:
                        for u in range(U):
                            last = M(pair(4)[:, u, :], units(8)[:, u, :], units(3)[:, u, :], start=True, stop=True)
                        last.then_inc(pq_mm, 1)
                    t += 1
                    if v % 2:
                        project(t)
                        t += 1
                pe.wait_ge(tu_done, LEVELS * (l + 1))
                for cc in range(NC):
                    for h in range(H):
                        nc.tensor.transpose(psum[:, 4 + cc, h * P:(h + 1) * P], kq(H, h, cc), ident)
                        last = nc.tensor.transpose(psum[:, 6 + cc, h * P:(h + 1) * P], kq(2 * H, h, cc), ident)
                last.then_inc(kv_tr, 1)
                project(34)
                pe.wait_ge(kv_taken, l + 1)
                for u in range(U):
                    last = M(pair(4)[:, u, :], units(5)[:, u, :], units(4)[:, u, :], start=True, stop=True)
                last.then_inc(w_mm, 1)

                def v_new(cc):
                    if cc:
                        pe.wait_ge(os_taken, 2 * l + cc)
                    for h in range(H):
                        u = cc * H + h
                        last = M(psum[:, 6, h * P:(h + 1) * P], units(4)[:, u, :], units(6)[:, u, :], start=True, stop=(cc == 0))
                        if cc:
                            last = M(psum[:, 6, h * P:(h + 1) * P], units(8)[:, u, :], units(3)[:, h, :], start=False, stop=True)
                    last.then_inc(vn_mm, 1)

                def out_and_state(cc):
                    pe.wait_ge(vn_taken, NC * l + cc + 1)
                    pe.wait_ge(w_taken, l + 1)
                    for h in range(H):
                        u = cc * H + h
                        last = M(psum[:, 4, h * P:(h + 1) * P], units(2)[:, u, :], units(1)[:, u, :], start=True, stop=(cc == 0))
                        if cc:
                            last = M(psum[:, 4, h * P:(h + 1) * P], units(3)[:, h, :], units(0)[:, u, :], start=False, stop=True)
                    last.then_inc(os_mm, 1)
                    for h in range(H):
                        u = cc * H + h
                        last = M(psum[:, 5, h * P:(h + 1) * P], units(7)[:, u, :], units(2)[:, u, :], start=True, stop=True)
                    last.then_inc(os_mm, 1)

                v_new(0)
                project(35)
                out_and_state(0)
                pe.wait_ge(samp_vn, 2 * l + 1)
                pe.wait_ge(s0_loaded, 16 * (l + 1))
                for b in range(NB):
                    for h in range(H):
                        u = b * H + h
                        M(psum[:, 7, 2 * u:2 * u + 2], s0[:, u, :], qkv[:, h:2 * H:H, TP + b], start=True, stop=True)
                M(psum[:, 7, 64:96], ones, s_prod, start=True, stop=True).then_inc(samp_mm, 1)
                v_new(1)
                out_and_state(1)
                pe.wait_ge(conv_out, CT * (l + 1))
                for j in range(CT):
                    last = M(psum[:, 6, 0:T], ones, c[:, j, :], start=(j == 0), stop=(j == CT - 1))
                last.then_inc(ln_sum, 1)
                pe.wait_ge(samp_vn, 2 * l + 2)
                nc.tensor.transpose(psum[0:32, 7, 128:256], vn_s, ident)
                nc.tensor.transpose(psum[0:32, 7, 256:384], k_s, ident).then_inc(samp_tr, 1)
                project(36)
                pe.wait_ge(samp_rows, l + 1)
                for j in range(CT):
                    pe.wait_ge(ln_sq, CT * l + j + 1)
                    last = M(psum[:, 7, 0:T], ones, work[:, 4 + j, 512:512 + T], start=(j == 0), stop=(j == CT - 1))
                last.then_inc(ln_var, 1)
                for h in range(H):
                    pe.wait_ge(o_squares, H * l + h + 1)
                    last = M(psum[0:2 * H, 6, 0:T], pick[:, 7 - h:15 - h], work[:, 4 + h, 0:T], start=(h == 0), stop=(h == H - 1))
                last.then_inc(rows_sum, 1)
                project(37)
                pe.wait_ge(samp_vm, l + 1)
                pe.wait_ge(os_taken, 2 * l + 2)
                for g in range(8):
                    if g >= 2:
                        pe.wait_ge(outer_taken, 8 * l + g - 1)
                    M(psum[:, 4 + g % 2, :], rows32[0:32, 1, :], vmask[0:32, 4 * g:4 * g + 4, :].rearrange("p u d -> p (u d)"),
                      start=True, stop=True).then_inc(outer_mm, 1)
                project(38)
                pe.wait_ge(outer_taken, 8 * (l + 1))
                pe.wait_ge(rows_recip, 2 * l + 2)
                pe.wait_ge(ln_rms, l + 1)
                spread(o_rstd, H, 0)
                project(39)
                pe.wait_ge(act_evac, 32 * (l + 1))
                pe.wait_ge(o_done, l + 1)
                pe.wait_ge(c_done, CT * (l + 1))
                for t in range(KD):
                    w = arrived(section, N_PROJ + t)
                    if t >= 2:
                        pe.wait_ge(merged_done, KD * l + t - 1)
                    for j in range(CT):
                        M(psum[:, 2 * (t % 2), 0:T], w[:, j, :], c[:, j, :], start=(j == 0), stop=(j == CT - 1))
                    for h in range(H):
                        last = M(psum[:, 2 * (t % 2) + 1, 0:T], w[:, CT + h, :], qkv[:, 8 + h, :], start=(h == 0), stop=(h == H - 1))
                    last.then_inc(units_used, 1)
                pe.wait_ge(merged_done, KD * (l + 1))
                for t in range(KD):
                    w = parts(section, N_PROJ + N_MIX + t)
                    if t >= 4:
                        pe.wait_ge(x_done, KD * l + t - 3)
                    split_tile(psum[:, t % 4, 0:T], w, 3 * l + 1).then_inc(units_used, 1)
                model_sums(2 * l + 1)

                if l == 0:
                    for f in range(FT):
                        if f >= 3:
                            pe.wait_ge(act_done, f - 2)
                        for i in range(2):
                            w = parts("ffn", 2 * f + i)
                            split_tile(psum[:, 2 * (f % 3) + i, 0:T], w, 2).then_inc(units_used, 1)
                    for i in range(KD * FT):
                        t, f = divmod(i, FT)
                        if i % KD == 0:
                            w = arrived("ffn", 2 * FT + i // KD)
                        if i == 0:
                            pe.wait_ge(act_done, FT)
                        if f == 0 and t >= 2:
                            pe.wait_ge(down_taken, t - 1)
                        last = M(psum[:, 6 + t % 2, 0:T], w[:, i % KD, :], act_all[:, f, :], start=(f == 0), stop=(f == FT - 1))
                        if i % KD == KD - 1:
                            last.then_inc(units_used, 1)
                        elif f == FT - 1:
                            last.then_inc(down_done, 1)
                else:
                    pe.wait_ge(h_done, 4 * KD)
                    for m, t0 in enumerate((0, P, T - P)):
                        for k in range(KD):
                            last = M(psum[:, 4, m * 8:m * 8 + 8], hT[:, k, t0:t0 + P], par("router", k * 8, 8),
                                     start=(k == 0), stop=(k == KD - 1))
                    last.then_inc(router_mm, 1)
                    for m, t0 in enumerate((0, P, T - P)):
                        for k in range(KD):
                            b = (0, 2, 6)[m] + k // 4
                            last = nc.tensor.transpose(psum[:, b, k % 4 * P:(k % 4 + 1) * P], hT[:, k, t0:t0 + P], ident)
                        last.then_inc(h_tr, 1)
                    pe.wait_ge(chosen, 1)
                    sent = rt[:, 8, :]
                    for m in range(3):
                        for before in range(m):
                            M(psum[:, 5, m * NE:(m + 1) * NE], ones, sent[:, before * NE:(before + 1) * NE], start=(before == 0), stop=False)
                        M(psum[:, 5, m * NE:(m + 1) * NE], triu_strict, sent[:, m * NE:(m + 1) * NE], start=(m == 0), stop=True)
                    for m in range(3):
                        last = M(psum[:, 5, 24:32], ones, sent[:, m * NE:(m + 1) * NE], start=(m == 0), stop=(m == 2))
                    last.then_inc(ranks_mm, 1)

                    def gather(job, part):
                        pe.wait_ge(take_done, job + 1)
                        for k in range(4 * part, 4 * part + 4):
                            for m in range(3):
                                last = M(psum[:, part, k % 4 * CAP:(k % 4 + 1) * CAP], h_tok[:, m, k * P:(k + 1) * P], take[:, m, :],
                                         start=(m == 0), stop=(m == 2))
                        last.then_inc(gather_mm, 1)

                    pe.wait_ge(h_tok_done, 3)
                    gather(0, 0)
                    pe.wait_ge(rows_rhs, 1)
                    for b in range(3):
                        last = M(psum[:, 2 + b, :], ones, work[:, 0:2, :].rearrange("p a b -> p (a b)")[:, b * 512:(b + 1) * 512], start=True, stop=True)
                    last.then_inc(rows_mm, 1)
                    pe.wait_ge(rows_done, 1)
                    pe.wait_ge(jobs_done, 1)
                    n_jobs = pe.value_load(jobs[0:1, MAX_JOBS:MAX_JOBS + 1], min_val=2, max_val=MAX_JOBS)
                    with pe.Fori(0, n_jobs) as job:
                        gather(job, 1)
                        for u in range(N_FFN):
                            if u < 2:
                                pe.wait_ge(h_job_done, job * 2 + (u + 1))
                            s = (n_split + u) % SPLIT
                            pe.wait_ge(lo_done, job * N_FFN + (n_low + u + 1))
                            if u < 4 * NCH:
                                ch, up, part = u // 4, u // 2 % 2, u % 2
                                if part == 0 and u < 8:
                                    pe.wait_ge(down_taken, job * KD + KD)
                                elif part == 0:
                                    pe.wait_ge(chunk_done if up else chunk_silu, job * NCH + (ch - 1))
                                for kk in range(4):
                                    k = 4 * part + kk
                                    last = split_products(psum[0:CAP, 2 * up + ch % 2, 0:CHUNK],
                                                          [x[:, k * CAP:(k + 1) * CAP] for x in (h_hi, h_lo)],
                                                          [w[:, s, kk * CHUNK:(kk + 1) * CHUNK] for w in (w_hi, w_lo)], k == 0, k == KD - 1)
                            else:
                                f = u - 4 * NCH
                                pe.wait_ge(act_lo_done, job * NCH + (f // 2 + 1))
                                for i in range(2):
                                    last = split_products(psum[0:CAP, 6 + i, :], [x[:, f, :] for x in (act_hi, act_lo)],
                                                          [w[:, s, i * 512:(i + 1) * 512] for w in (w_hi, w_lo)], f == 0, f == FT - 1)
                            last.then_inc(units_used, 1)
                            ch = (u - 7) // 4
                            if u % 4 == 3 and 0 <= ch < NCH:
                                pe.wait_ge(chunk_done, job * NCH + (ch + 1))
                                if ch >= 2:
                                    pe.wait_ge(act_lo_done, job * NCH + (ch - 1))
                                for i in range(2):
                                    last = nc.tensor.transpose(psum[:, 4 + ch % 2, i * CAP:(i + 1) * CAP], prod_job[:, ch % 2, i * P:(i + 1) * P], ident[0:CAP, 0:CAP])
                                last.then_inc(act_tr, 1)
                        gather(job + 1, 0)
                        pe.wait_ge(y_tok_done, job + 1)
                        pe.wait_ge(put_done, job + 1)
                        for t in range(KD):
                            if t >= 4:
                                pe.wait_ge(down_taken, job * KD + (KD + t - 3))
                            M(psum[:, 2 + t % 4, 0:T], y_tok[:, t * P:(t + 1) * P], put, start=True, stop=True).then_inc(scatter_mm, 1)
                    pe.wait_ge(down_taken, n_jobs * KD + KD)
            model_sums(2 * DEPTH)


PARAMS = [("norm1", DEPTH * KD), ("norm2", DEPTH * KD), ("final", KD), ("o_g", DEPTH), ("dw_b", DEPTH * CT),
          ("ln_g", DEPTH * CT), ("ln_b", DEPTH * CT), ("dw_w", DEPTH * CT * DW), ("qk_w", DEPTH * QT * QW),
          ("a_log", DEPTH * H), ("dt_bias", DEPTH * H), ("w_ab", DEPTH * KD * 8), ("router", KD * NE),
          ("samp_mask", NB), ("iota", 24), ("eps", 1), ("pick", 15),
          ("keep", 3 * NE), ("drop", 6), ("slot_row", CAP), ("slot_col", 1), ("job_no", MAX_JOBS * NE)]


def kernel(x_prompt, x_sample, state_delta, state_qkv_conv, state_dwconv, norm1_g, w_in, qkv_conv_w,
           a_log, dt_bias, o_norm_g, w_delta_out, dw_w, dw_b, ln_g, ln_b, w_conv_out, w_o, norm2_g,
           ffn_w_gate, ffn_w_up, ffn_w_down, router_w, exp_w_gate, exp_w_up, exp_w_down, final_norm_g):
    import concourse.bacc as bacc
    from concourse.bass_utils import run_bass_kernel_spmd

    n = lambda x: np.ascontiguousarray(np.asarray(x))
    L, F = DEPTH, np.float32

    def feat(x):
        x = n(x)
        lead = tuple(range(x.ndim - 1))
        y = x.reshape(x.shape[:-1] + (x.shape[-1] // P, P))
        return y.transpose((y.ndim - 1, y.ndim - 2) + lead)

    def by_layer(x):
        return n(x).reshape(L, -1, P).transpose(2, 0, 1).reshape(P, -1)

    def out_tiles(w):
        w = n(w)
        return w.reshape(w.shape[0] // P, P, w.shape[1] // P, P).transpose(2, 1, 0, 3).reshape(w.shape[1] // P, P, -1)

    def ffn_units(wg, wu, wd):
        gu = np.stack([out_tiles(wg), out_tiles(wu)], 1).reshape(2 * FT, P, KD * P)
        blocks = n(wd).reshape(FT, P, KD, P).transpose(2, 0, 1, 3).reshape(FT, KD, P, P)
        return np.concatenate([gu, blocks.transpose(0, 2, 1, 3).reshape(FT, P, KD * P)])

    def expert_units(wg, wu, wd):
        gu = np.stack([n(wg), n(wu)]).reshape(2, 2, 4, P, NCH, CHUNK)
        return np.concatenate([gu.transpose(4, 0, 1, 3, 2, 5).reshape(4 * NCH, P, 4 * CHUNK), n(wd).reshape(FT, P, D)])

    w_in = n(w_in)
    w_mixer = np.empty((L, N_LAYER, P, KD * P), F)
    for l in range(L):
        t = out_tiles(w_in[l, :, 0:3072])
        w_mixer[l, QKV0:GATE0], w_mixer[l, GLU0:QKV0:2], w_mixer[l, GLU0 + 1:QKV0:2] = t[8:24], t[0:4], t[4:8]
        w_mixer[l, GATE0:N_PROJ] = out_tiles(w_in[l, :, 3080:])
        w_mixer[l, 40:48] = np.concatenate([out_tiles(w_conv_out[l]), out_tiles(w_delta_out[l])], 2)
        w_mixer[l, 48:56] = out_tiles(w_o[l])
    w_exp = np.concatenate([expert_units(exp_w_gate[0][e], exp_w_up[0][e], exp_w_down[0][e]) for e in range(NE)])

    everywhere = lambda x: np.broadcast_to(n(x).reshape(1, -1), (P, n(x).size))
    real = (np.arange(P)[:, None] >= SAMPLE_ROW) | (np.arange(3)[None] < 2)
    packed = {
        "norm1": by_layer(norm1_g), "norm2": by_layer(norm2_g), "final": n(final_norm_g).reshape(KD, P).T,
        "o_g": n(o_norm_g).T, "dw_b": by_layer(dw_b), "ln_g": by_layer(ln_g), "ln_b": by_layer(ln_b),
        "dw_w": n(dw_w).reshape(L, DW, CT, P).transpose(3, 0, 2, 1).reshape(P, -1),
        "qk_w": n(qkv_conv_w).reshape(L, QW, QT, P).transpose(3, 0, 2, 1).reshape(P, -1),
        "a_log": everywhere(a_log), "dt_bias": everywhere(dt_bias),
        "w_ab": w_in[:, :, 3072:3080].reshape(L, KD, P, 8).transpose(2, 0, 1, 3).reshape(P, -1),
        "router": n(router_w)[0].reshape(KD, P, NE).transpose(1, 0, 2).reshape(P, -1),
        "samp_mask": (np.arange(P)[:, None] == SAMPLE_ROW + np.arange(NB)[None]).astype(F),
        "keep": np.repeat(real, NE, 1).astype(F), "drop": np.tile(np.where(real, 0.0, -1e6), (1, 2)).astype(F),
        "slot_row": np.broadcast_to(np.arange(CAP).astype(F)[None], (P, CAP)), "slot_col": np.arange(P).astype(F)[:, None],
        "job_no": np.broadcast_to(np.repeat(np.arange(MAX_JOBS), NE).astype(F)[None], (P, MAX_JOBS * NE)),
        "pick": np.broadcast_to((np.arange(15) == 7).astype(F)[None], (P, 15)),
        "eps": np.full((P, 1), EPS, F),
        "iota": np.broadcast_to(np.tile(np.arange(NE), 3).astype(F)[None], (P, 3 * NE)),
    }
    i, j = np.arange(P)[:, None], np.arange(P)[None]
    masks = [i == j, i >= 0 * j, j >= i, j > i]
    level_masks = []
    for v in range(LEVELS):
        b = 1 << v
        level_masks.append((i // (2 * b) == j // (2 * b)) & (i // b % 2 == 1) & (j // b % 2 == 0))
    x_all = np.concatenate([n(x_prompt)[0], n(x_sample)[:, 0]], 0)

    def window(state, taps):
        s = n(state)
        w = np.zeros((L, P, s.shape[-1] // P, NB, taps), F)
        w[..., :-1] = s.reshape(L, NB, taps - 1, -1, P).transpose(0, 4, 3, 1, 2)
        return w.reshape(L, P, -1)

    arrays = {
        "xT": feat(x_all).reshape(P, -1), "params": np.concatenate([packed[k] for k, _ in PARAMS], 1),
        "consts": np.stack(masks, 1).astype(F).reshape(P, -1), "w_mixer": w_mixer,
        "level_masks": np.stack(level_masks, 1).astype(mybir.dt.np(mybir.dt.bfloat16)).reshape(P, -1),
        "w_ffn": ffn_units(ffn_w_gate[0], ffn_w_up[0], ffn_w_down[0]), "w_exp": w_exp,
        "s0": n(state_delta).transpose(0, 3, 1, 2, 4).reshape(L, P, -1),
        "dw_win": window(state_dwconv, DW), "qkv_win": window(state_qkv_conv, QW),
    }
    outs = {"yT": (P, KD * T), "sp": (L, P, H * P), "ss": (L, P, NB * H * P), "dwp": (L, P, CT, DW - 1),
            "dws": (L, P, CT * NB * DW), "qkp": (L, P, QT, QW - 1), "qks": (L, P, QT * NB * QW)}

    nc = bacc.Bacc("TRN2", target_bir_lowering=False, num_devices=1)
    ins = {}
    for name, value in arrays.items():
        arrays[name] = np.ascontiguousarray(value)
        ins[name] = nc.dram_tensor("in_" + name, value.shape, mybir.dt.from_np(arrays[name].dtype), kind="ExternalInput").ap()
    o = {name: nc.dram_tensor("out_" + name, shape, F32, kind="ExternalOutput").ap() for name, shape in outs.items()}
    build(nc, ins, o)
    r = run_bass_kernel_spmd(nc, [{"in_" + k: v for k, v in arrays.items()}], core_ids=[0]).results[0]
    g = {name: np.asarray(r["out_" + name]) for name in outs}

    y = g["yT"].reshape(P, KD, T).transpose(2, 1, 0).reshape(T, D)

    def rows(x, lead):
        x = x.reshape((L, P) + lead)
        return n(np.moveaxis(x, (2, 1), (-2, -1)).reshape((L,) + lead[1:] + (-1,)))

    return (
        n(y[None, :TP]), n(y[TP:, None]),
        n(g["sp"].reshape(L, P, H, P).transpose(0, 2, 1, 3)[:, None]),
        rows(g["qkp"], (QT, QW - 1))[:, None], rows(g["dwp"], (CT, DW - 1))[:, None],
        n(g["ss"].reshape(L, P, NB, H, P).transpose(0, 2, 3, 1, 4)),
        n(rows(g["qks"], (QT, NB, QW))[:, :, 1:]), n(rows(g["dws"], (CT, NB, DW))[:, :, 1:]),
    )
```
